# Optimizing a Trainium2 kernel written in Bass

```python
import jax, jax.numpy as jnp
from jax import lax
import numpy as np

D_MODEL = 1024
BATCH = 1
SEQ = 512
DEPTH = 1

MEM_LEN = 256
EPS = 1e-6
RET_HEADS = 4
RET_HEAD_DIM = D_MODEL // RET_HEADS
RET_WIDTH = RET_HEADS * RET_HEAD_DIM
RET_CHUNK = 128
ROPE_BASE = 10000.0
FOX_HEADS = 16
FOX_HEAD_DIM = D_MODEL // FOX_HEADS
FOX_WIDTH = FOX_HEADS * FOX_HEAD_DIM
Q_BLOCK = 128
MEM_HEADS = 4
MEM_HEAD_DIM = D_MODEL // MEM_HEADS
MEM_WIDTH = MEM_HEADS * MEM_HEAD_DIM
N_BRANCHES = 3
SPLIT_SIZES = (RET_WIDTH, RET_WIDTH, RET_WIDTH, RET_WIDTH,
               FOX_WIDTH, FOX_WIDTH, FOX_WIDTH, FOX_HEADS,
               MEM_WIDTH,
               D_MODEL, D_MODEL, D_MODEL)
IN_COLS = sum(SPLIT_SIZES)
N_EXPERTS = 16
N_GROUPS = 4
EXPERTS_PER_GROUP = N_EXPERTS // N_GROUPS
TOP_K = 2
D_FF_EXPERT = D_MODEL // 2

kernel_name = "hybrid_retention_fox_memory_grouped_moe"

def rms_norm(x, gain):
    xf = x.astype(jnp.float32)
    y = xf * lax.rsqrt(jnp.mean(xf * xf, axis=-1, keepdims=True) + EPS)
    return (y * gain.astype(jnp.float32)).astype(x.dtype)

def head_rms(x):
    xf = x.astype(jnp.float32)
    return (xf * lax.rsqrt(jnp.mean(xf * xf, axis=-1, keepdims=True) + EPS)).astype(x.dtype)

def rotary(x):
    s, d = x.shape[1], x.shape[-1]
    inv_freq = ROPE_BASE ** (-jnp.arange(0, d, 2, dtype=jnp.float32) / d)
    ang = jnp.arange(s, dtype=jnp.float32)[:, None] * inv_freq[None, :]
    cos = jnp.cos(ang)[None, :, None, :]
    sin = jnp.sin(ang)[None, :, None, :]
    xf = x.astype(jnp.float32)
    x1, x2 = xf[..., : d // 2], xf[..., d // 2:]
    return jnp.concatenate([x1 * cos - x2 * sin, x2 * cos + x1 * sin], axis=-1).astype(x.dtype)

def retention(q, k, v):
    b, s, h, dk = q.shape
    dv = v.shape[-1]
    c = RET_CHUNK
    n = s // c
    log_gamma = jnp.log1p(-(2.0 ** (-5.0 - jnp.arange(h, dtype=jnp.float32))))
    idx = jnp.arange(c, dtype=jnp.float32)
    diff = idx[:, None] - idx[None, :]
    intra = jnp.where(diff >= 0, jnp.exp(log_gamma[:, None, None] * jnp.maximum(diff, 0.0)), 0.0)
    q_decay = jnp.exp(log_gamma[:, None] * (idx + 1.0))[None, :, :, None]
    k_decay = jnp.exp(log_gamma[:, None] * (c - 1.0 - idx))[None, :, :, None]
    chunk_decay = jnp.exp(log_gamma * c)[None, :, None, None]

    def to_chunks(t):
        return t.reshape(b, n, c, h, t.shape[-1]).transpose(1, 0, 3, 2, 4)

    qc, kc, vc = to_chunks(q), to_chunks(k * (dk ** -0.5)), to_chunks(v)

    def step(state, inp):
        qi, ki, vi = inp
        scores = jnp.einsum('bhid,bhjd->bhij', qi, ki) * intra
        o = (jnp.einsum('bhij,bhje->bhie', scores, vi)
             + jnp.einsum('bhid,bhde->bhie', qi * q_decay, state))
        state = state * chunk_decay + jnp.einsum('bhjd,bhje->bhde', ki * k_decay, vi)
        return state, o

    state0 = jnp.zeros((b, h, dk, dv), jnp.float32)
    _, o = lax.scan(step, state0, (qc, kc, vc))
    return o.transpose(1, 0, 3, 2, 4).reshape(b, s, h, dv).astype(v.dtype)

def forgetting_attention(q, k, v, log_f):
    b, s, h, d = q.shape
    nb = s // Q_BLOCK
    scale = d ** -0.5
    cum = jnp.cumsum(log_f, axis=1).transpose(0, 2, 1)
    kh = k.transpose(0, 2, 1, 3)
    vh = v.transpose(0, 2, 1, 3)
    qb = q.reshape(b, nb, Q_BLOCK, h, d).transpose(1, 0, 3, 2, 4)
    cb = cum.reshape(b, h, nb, Q_BLOCK).transpose(2, 0, 1, 3)
    key_pos = jnp.arange(s)

    def block(args):
        qi, ci, i = args
        q_pos = i * Q_BLOCK + jnp.arange(Q_BLOCK)
        logits = (jnp.einsum('bhqd,bhkd->bhqk', qi, kh).astype(jnp.float32) * scale
                  + ci[..., None] - cum[:, :, None, :])
        logits = jnp.where(key_pos[None, :] <= q_pos[:, None], logits, -jnp.inf)
        p = jax.nn.softmax(logits, axis=-1).astype(v.dtype)
        return jnp.einsum('bhqk,bhkd->bhqd', p, vh)

    o = lax.map(block, (qb, cb, jnp.arange(nb)))
    return o.transpose(1, 0, 3, 2, 4).reshape(b, s, h, d)

def memory_attention(q, k, v):
    logits = jnp.einsum('bshd,bmhd->bhsm', q, k).astype(jnp.float32) * (q.shape[-1] ** -0.5)
    p = jax.nn.softmax(logits, axis=-1).astype(v.dtype)
    return jnp.einsum('bhsm,bmhd->bshd', p, v)

def grouped_moe(h, router_w, router_bias, w_gate, w_up, w_down):
    t = h.reshape(-1, h.shape[-1])
    logits = t.astype(jnp.float32) @ router_w.astype(jnp.float32)
    scores = jax.nn.sigmoid(logits)
    biased = scores + router_bias.astype(jnp.float32)
    group_score = lax.top_k(biased.reshape(-1, N_GROUPS, EXPERTS_PER_GROUP), TOP_K)[0].sum(-1)
    top_group = jnp.argmax(group_score, axis=-1)
    expert_group = jnp.arange(N_EXPERTS) // EXPERTS_PER_GROUP
    masked = jnp.where(top_group[:, None] == expert_group[None, :], biased, -jnp.inf)
    _, idx = lax.top_k(masked, TOP_K)
    sel = jnp.take_along_axis(scores, idx, axis=-1)
    w = sel / jnp.sum(sel, axis=-1, keepdims=True)
    gates = jnp.einsum('tk,tke->te', w, jax.nn.one_hot(idx, N_EXPERTS, dtype=jnp.float32)).astype(t.dtype)
    out = jnp.zeros_like(t)
    for e in range(N_EXPERTS):
        a = jax.nn.silu(t @ w_gate[e]) * (t @ w_up[e])
        out = out + gates[:, e:e + 1] * (a @ w_down[e])
    return out.reshape(h.shape)

def setup_inputs(seed: int = 0) -> dict:
    key = jax.random.key(seed)
    ks = jax.random.split(key, 21)

    def nrm(k, shape, scale):
        return scale * jax.random.normal(k, shape, jnp.float32)

    resid = (2.0 * DEPTH) ** -0.5
    return {
        "x": nrm(ks[0], (BATCH, SEQ, D_MODEL), 1.0),
        "mem": nrm(ks[1], (BATCH, MEM_LEN, D_MODEL), 1.0),
        "norm_mix": 1.0 + nrm(ks[2], (DEPTH, D_MODEL), 0.02),
        "norm_mem": 1.0 + nrm(ks[3], (DEPTH, D_MODEL), 0.02),
        "w_in": nrm(ks[4], (DEPTH, D_MODEL, IN_COLS), D_MODEL ** -0.5),
        "b_forget": 2.0 + nrm(ks[5], (DEPTH, FOX_HEADS), 0.1),
        "fox_q_norm": 1.0 + nrm(ks[6], (DEPTH, FOX_HEAD_DIM), 0.02),
        "fox_k_norm": 1.0 + nrm(ks[7], (DEPTH, FOX_HEAD_DIM), 0.02),
        "mem_q_norm": 1.0 + nrm(ks[8], (DEPTH, MEM_HEAD_DIM), 0.02),
        "mem_k_norm": 1.0 + nrm(ks[9], (DEPTH, MEM_HEAD_DIM), 0.02),
        "w_mem_kv": nrm(ks[10], (DEPTH, D_MODEL, 2 * MEM_WIDTH), D_MODEL ** -0.5),
        "w_o_ret": nrm(ks[11], (DEPTH, RET_WIDTH, D_MODEL), RET_WIDTH ** -0.5),
        "w_o_fox": nrm(ks[12], (DEPTH, FOX_WIDTH, D_MODEL), FOX_WIDTH ** -0.5),
        "w_o_mem": nrm(ks[13], (DEPTH, MEM_WIDTH, D_MODEL), MEM_WIDTH ** -0.5),
        "w_out": nrm(ks[14], (DEPTH, D_MODEL, D_MODEL), D_MODEL ** -0.5 * resid),
        "norm_ffn": 1.0 + nrm(ks[15], (DEPTH, D_MODEL), 0.02),
        "router_w": nrm(ks[16], (D_MODEL, N_EXPERTS), D_MODEL ** -0.5),
        "router_bias": nrm(ks[17], (N_EXPERTS,), 0.01),
        "w_gate": nrm(ks[18], (DEPTH, N_EXPERTS, D_MODEL, D_FF_EXPERT), D_MODEL ** -0.5),
        "w_up": nrm(ks[19], (DEPTH, N_EXPERTS, D_MODEL, D_FF_EXPERT), D_MODEL ** -0.5),
        "w_down": nrm(ks[20], (DEPTH, N_EXPERTS, D_FF_EXPERT, D_MODEL), D_FF_EXPERT ** -0.5 * resid),
    }

def reference(x, mem, norm_mix, norm_mem, w_in, b_forget, fox_q_norm, fox_k_norm,
              mem_q_norm, mem_k_norm, w_mem_kv, w_o_ret, w_o_fox, w_o_mem, w_out,
              norm_ffn, router_w, router_bias, w_gate, w_up, w_down):
    b, s, _ = x.shape
    m = mem.shape[1]
    split_points = [int(p) for p in np.cumsum(SPLIT_SIZES)[:-1]]

    def heads(t, n_heads):
        return t.reshape(t.shape[0], t.shape[1], n_heads, -1)

    for l in range(DEPTH):
        h = rms_norm(x, norm_mix[l])
        proj = h @ w_in[l]
        (rq, rk, rv, rg, fq, fk, fv, ff, mq,
         g_ret, g_fox, g_mem) = jnp.split(proj, split_points, axis=-1)

        ro = retention(rotary(heads(rq, RET_HEADS)), rotary(heads(rk, RET_HEADS)), heads(rv, RET_HEADS))
        ro = head_rms(ro).reshape(b, s, RET_WIDTH) * jax.nn.silu(rg)
        y_ret = ro @ w_o_ret[l]

        log_f = jax.nn.log_sigmoid((ff + b_forget[l]).astype(jnp.float32))
        fo = forgetting_attention(rms_norm(heads(fq, FOX_HEADS), fox_q_norm[l]),
                                  rms_norm(heads(fk, FOX_HEADS), fox_k_norm[l]),
                                  heads(fv, FOX_HEADS), log_f)
        y_fox = fo.reshape(b, s, FOX_WIDTH) @ w_o_fox[l]

        mk, mv = jnp.split(rms_norm(mem, norm_mem[l]) @ w_mem_kv[l], 2, axis=-1)
        mo = memory_attention(rms_norm(heads(mq, MEM_HEADS), mem_q_norm[l]),
                              rms_norm(mk.reshape(b, m, MEM_HEADS, MEM_HEAD_DIM), mem_k_norm[l]),
                              mv.reshape(b, m, MEM_HEADS, MEM_HEAD_DIM))
        y_mem = mo.reshape(b, s, MEM_WIDTH) @ w_o_mem[l]

        merged = (jax.nn.sigmoid(g_ret) * y_ret + jax.nn.sigmoid(g_fox) * y_fox
                  + jax.nn.sigmoid(g_mem) * y_mem)
        x = x + merged @ w_out[l]

        x = x + grouped_moe(rms_norm(x, norm_ffn[l]), router_w, router_bias,
                            w_gate[l], w_up[l], w_down[l])
    return x


_drawn_inputs = setup_inputs


def setup_inputs(seed=0):
    import zlib

    import numpy as np

    out = dict(_drawn_inputs(seed))
    spreads = {}
    factors = {'norm_mem': 8.0,
     'fox_q_norm': 15.269,
     'fox_k_norm': 27.969,
     'mem_q_norm': 8.0,
     'mem_k_norm': 8.0,
     'b_forget': 42.92,
     'norm_ffn': 3.843}
    for name, (base, spread) in spreads.items():
        noise = np.random.default_rng([zlib.crc32(name.encode()), seed]).standard_normal(out[name].shape)
        drawn = base * np.exp(spread * noise) if base else spread * noise
        out[name] = __import__('jax').numpy.asarray(drawn.astype(out[name].dtype))
    for name, factor in factors.items():
        out[name] = (out[name] * factor).astype(out[name].dtype)
    return out
```

```python
from contextlib import ExitStack

import numpy as np

import concourse.bass as bass
from concourse import mybir

F32 = mybir.dt.float32
F32R = mybir.dt.float32r
I32 = mybir.dt.int32
U32 = mybir.dt.uint32
ALU = mybir.AluOpType
ACT = mybir.ActivationFunctionType
AX = mybir.AxisListType

P = 128
D = 1024
S = 512
M = 256
KT = D // P
TT = S // P
MT = M // P
EPS = 1e-6
RET_HEADS, FOX_HEADS, MEM_HEADS = 4, 16, 4
PAIRS = FOX_HEADS // 2
FOX_DIM = D // FOX_HEADS
HEAD_TILES = 2
N_EXPERTS, N_GROUPS, PER_GROUP, FF = 16, 4, 4, 512
TOP_K = 2
MAX_BLOCKS = N_EXPERTS + TOP_K * S // P - 1
BLOCK_CHUNKS = KT + FF // P
NEG = -1.0e30

RAW, SPLIT = 6, 3
E_SPLIT = 4
FT = FF // P
IDX_COLS = MAX_BLOCKS + 1
AHEAD = 2


def chunk_list():
    out = [("fv", i) for i in range(8)] + [("ff", 0)]
    for p in range(PAIRS):
        out += [("fq", p), ("fk", p)]
    out += [("g_fox", n) for n in range(KT)] + [("o_fox", n) for n in range(KT)]
    out += [("rv", i) for i in range(8)]
    for h in range(RET_HEADS):
        out += [(k, HEAD_TILES * h + t) for k in ("rk", "rq", "rg") for t in range(HEAD_TILES)]
    out += [("g_ret", n) for n in range(KT)] + [("o_ret", n) for n in range(KT)]
    out += [("mk", n) for n in range(KT)] + [("mv", i) for i in range(8)]
    out += [("mq", n) for n in range(KT)]
    out += [("g_mem", n) for n in range(KT)] + [("o_mem", n) for n in range(KT)]
    out += [("out", i) for i in range(8)]
    return out


CHUNKS = chunk_list()
NATURAL = ("fv", "rv", "mv", "out")
FIRST = {}
for _c, (_kind, _i) in enumerate(CHUNKS):
    FIRST.setdefault(_kind, _c)


def schedule():
    steps = {}

    def put(slot, *step):
        steps.setdefault(slot, []).append(step)

    base = 4 * FIRST["fq"]
    for p in range(PAIRS):
        put(base + 8 * p + 5, "norm", 2 * p)
        put(base + 8 * p + 9, "norm", 2 * p + 1)
        for half in range(2):
            put(base + 8 * p + 12 + 4 * half, "forget", 2 * p + half)
            put(base + 8 * p + 20 + 4 * half, "fox_pv", 2 * p + half)
        for j in range(8):
            put(base + 8 * p + 14 + j, "fox_score", 8 * p + j)
            put(base + 8 * p + 15 + j, "fox_scale", 8 * p + j)
            put(base + 8 * p + 16 + j, "fox_turn", 8 * p + j)
    base = 4 * FIRST["rk"]
    for h in range(RET_HEADS):
        b = base + 24 * h
        put(b + 9, "rotary", 2 * h)
        put(b + 17, "rotary", 2 * h + 1)
        for j in range(TT):
            put(b + 22 + 2 * j, "ret_score", TT * h + j)
        for e in range(HEAD_TILES):
            put(b + 30 + 2 * e, "ret_pv", HEAD_TILES * h + e)
        put(b + 34, "norm", 16 + h)
        put(b + 39, "ret_out", h)
    base = 4 * FIRST["o_ret"]
    put(base + 2, "mem_load", 0)
    put(base + 12, "mem_norm", 0)
    put(4 * FIRST["mk"] - 1, "mem_split", 0)
    base = 4 * FIRST["mk"]
    for h in range(MEM_HEADS):
        put(base + 8 * h + 9, "norm", 20 + h)
    base = 4 * FIRST["mq"]
    for h in range(MEM_HEADS):
        b = base + 8 * h
        put(b + 9, "norm", 24 + h)
        for j in range(TT):
            put(b + 14 + j, "mem_score", TT * h + j)
            put(b + 15 + j, "mem_scale", TT * h + j)
            put(b + 16 + j, "mem_turn", TT * h + j)
        for e in range(HEAD_TILES):
            put(b + 20 + e, "mem_pv", HEAD_TILES * h + e)
    order = ("rotary", "norm", "forget", "fox_score", "mem_score", "ret_score", "fox_scale", "mem_scale",
             "fox_turn", "mem_turn", "fox_pv", "mem_pv", "ret_pv")
    for slot in steps:
        steps[slot].sort(key=lambda s: order.index(s[0]) if s[0] in order else 99)
    return steps


STEPS = schedule()
RET_AT = [sum(S - m * P for m in range(k)) for k in range(TT)]
FOX_NORMS, RET_NORMS, MK_NORMS, MQ_NORMS = range(0, 16), range(16, 20), range(20, 24), range(24, 28)


def norm_tiles(n):
    return 1 if n in FOX_NORMS else HEAD_TILES


def count_before(kinds, chunk):
    return sum(CHUNKS[c][0] in kinds for c in range(chunk))


def mixing_and_experts(nc, dram):
    assert D == 1024 and S == 512 and M == 256
    ctx = ExitStack()
    with ctx:
        def sb(name, shape, dt=F32):
            return ctx.enter_context(nc.sbuf_tensor(name, shape, dt))

        def sem(name):
            return ctx.enter_context(nc.semaphore(name))

        ps = ctx.enter_context(nc.psum_tensor("ps", [P, 8, 512], F32))
        STAT, SCORE, TURN, PV = 2, 3, 5, 7

        h_split = sb("h_split", [P, 2, KT, S], F32R)
        w_split = sb("w_split", [P, 2, SPLIT, 1024], F32R)
        o_split = sb("o_split", [P, 2, KT, S], F32R)
        id_r = sb("id_r", [P, P], F32R)
        mask_r = sb("mask_r", [P, P], F32R)
        mem_split = o_split[:].rearrange("p a k s -> p (a k s)")[:, 0:2 * KT * M].rearrange(
            "p (a k s) -> p a k s", a=2, k=KT)
        big = sb("big", [P, RAW * 1024 + 3 * 4096])
        raw = big[:, 0:RAW * 1024].rearrange("p (r n) -> p r n", r=RAW)
        fvm = big[:, RAW * 1024:RAW * 1024 + 4096]
        gat = big[:, RAW * 1024 + 4096:RAW * 1024 + 8192]
        vreg = big[:, RAW * 1024 + 8192:RAW * 1024 + 12288]
        fv = fvm.rearrange("p (t n) -> p t n", t=TT)
        merged = fvm.rearrange("p (k s) -> p k s", k=KT)
        gate = gat.rearrange("p (k s) -> p k s", k=KT)
        xT = gate
        x_nat = gat.rearrange("p (t n) -> p t n", t=TT)
        fox_pt = vreg.rearrange("p (b j i) -> p b j i", b=2, j=TT)
        x1 = vreg.rearrange("p (t n) -> p t n", t=TT)
        rv = vreg.rearrange("p (t n) -> p t n", t=TT)
        mkT = vreg[:, 0:KT * M].rearrange("p (k m) -> p k m", k=KT)
        memT = vreg[:, KT * M:2 * KT * M].rearrange("p (k m) -> p k m", k=KT)
        mv = vreg[:, KT * M:2 * KT * M].rearrange("p (t n) -> p t n", t=MT)
        work = sb("work", [P, 9984])
        used = [0]

        def carve(words):
            used[0] += words
            return work[:, used[0] - words:used[0]]

        sq = carve(1024).rearrange("p (b s) -> p b s", b=2)
        var, rstd, newton = carve(512), carve(512), carve(512)
        common = used[0]
        fox_raw = carve(1024).rearrange("p (b s) -> p b s", b=2)
        fox_q = carve(1024).rearrange("p (b s) -> p b s", b=2)
        fox_k = carve(1024).rearrange("p (b s) -> p b s", b=2)
        logits = carve(1024).rearrange("p (b s) -> p b s", b=2)
        prob = carve(1024).rearrange("p (b s) -> p b s", b=2)
        forget = carve(1024).rearrange("p (b s) -> p b s", b=2)
        used[0] = common
        ret_raw = carve(1024).rearrange("p (b s) -> p b s", b=2)
        ret_k = carve(1024).rearrange("p (b s) -> p b s", b=2)
        ret_q = carve(1024).rearrange("p (b s) -> p b s", b=2)
        ret_o = carve(1024).rearrange("p (b s) -> p b s", b=2)
        ret_p = carve(1280)
        rot = carve(512)
        cos = carve(512)
        sin = carve(512)
        decay = carve(512)
        used[0] = common
        mem_raw = carve(1024).rearrange("p (b s) -> p b s", b=2)
        mem_q = carve(1024).rearrange("p (b s) -> p b s", b=2)
        mem_p = carve(512).rearrange("p (b m) -> p b m", b=2)
        mem_pt = carve(1024).rearrange("p (j i) -> p j i", j=MT)
        ident = sb("ident", [P, P])
        mask_f = sb("mask_f", [P, P])
        avg = sb("avg", [P, 3, P])
        gains = sb("gains", [P, 3 * KT + 8])
        cst = sb("cst", [P, 4])
        stat = sb("stat", [P, 16])
        cum = sb("cum", [FOX_HEADS, S])
        G_MIX, G_MEM, G_FFN, G_FQ, G_FK, G_MQ, G_MK = 0, KT, 2 * KT, 3 * KT, 3 * KT + 1, 3 * KT + 2, 3 * KT + 4
        B_FF = 3 * KT + 6

        ew_split = h_split[:].rearrange("p a k s -> p (a k s)").rearrange("p (a r n) -> p a r n", a=2, r=E_SPLIT)
        o_flat = o_split[:].rearrange("p a k s -> p (a k s)")
        xe_split = o_flat[:, 0:2 * KT * P].rearrange("p (a k s) -> p a k s", a=2, k=KT)
        he_split = o_flat[:, 2 * KT * P:2 * (KT + FT) * P].rearrange("p (a f s) -> p a f s", a=2, f=FT)
        e_raw = big[:, 0:BLOCK_CHUNKS * 1024].rearrange("p (r n) -> p r n", r=BLOCK_CHUNKS)
        y_a = big[:, 0:2048].rearrange("p (b n) -> p b n", b=2)
        y_b = big[:, 2048:4096].rearrange("p (b n) -> p b n", b=2)
        h2 = fvm.rearrange("p (t n) -> p t n", t=TT)
        h2T = gate
        used[0] = 0
        gain_b = carve(1024)
        scratch = carve(1024)
        x_rows = carve(1024)
        h_act, h_e = carve(512), carve(512)
        y_rows = carve(1024)
        router = carve(KT * N_EXPERTS).rearrange("p (k e) -> p k e", k=KT)
        order4 = carve(16).rearrange("p (b a) -> p b a", b=4)
        iota = carve(IDX_COLS)
        bias_b = carve(TT * N_EXPERTS)
        before, ones = carve(P), carve(P)
        sums = carve(4 * TT).rearrange("p (a t) -> p a t", a=4)
        r64 = [carve(TT * N_EXPERTS) for _ in range(10)]
        r256a, r256b = carve(256), carve(256)
        r384 = carve(IDX_COLS * N_EXPERTS)
        r16 = [carve(16) for _ in range(12)]
        token_w = carve(2 * TT).rearrange("p (a t) -> p a t", a=2)
        assert used[0] <= 9984
        slots_i = sb("slots_i", [P, 2, TT], I32)
        y_slot_i = sb("y_slot_i", [P, 2, TT], I32)
        tokens_i = sb("tokens_i", [P, TT], I32)
        blocks_i = sb("blocks_i", [P, IDX_COLS + 1], I32)
        rows_i = sb("rows_i", [P, IDX_COLS], I32)
        row_i = sb("row_i", [P, 1], I32)
        zero_i = sb("zero_i", [IDX_COLS, P], I32)

        consts_in, mem_in, xn_in = sem("consts_in"), sem("mem_in"), sem("xn_in")
        x_in = [sem(f"x_in{k}") for k in range(4)]
        rot_in, decay_in = sem("rot_in"), sem("decay_in")
        landed = [sem(f"landed{i}") for i in range(RAW)]
        hi_ready, lo_ready = sem("hi_ready"), sem("lo_ready")
        w_used = sem("w_used")
        tile_act, tile_dve = sem("tile_act"), sem("tile_dve")
        nat_read = sem("nat_read")
        x_sq, x_sum = sem("x_sq"), sem("x_sum")
        sq_ready = sem("sq_ready")
        stat_ready, stat_read = sem("stat_ready"), sem("stat_read")
        seed_ready, normed = sem("seed_ready"), sem("normed")
        h_f, h_hi, h_lo = sem("h_f"), sem("h_hi"), sem("h_lo")
        gate_log, cum_ready = sem("gate_log"), sem("cum_ready")
        sc_done, sc_read = sem("sc_done"), sem("sc_read")
        mem_min = sem("mem_min")
        prob_ready, prob_scaled = sem("prob_ready"), sem("prob_scaled")
        turned, turn_read = sem("turned"), sem("turn_read")
        pv_done = sem("pv_done")
        o_hi, o_lo = sem("o_hi"), sem("o_lo")
        rotated = sem("rotated")
        ret_silu, ret_sq, ret_gated = sem("ret_silu"), sem("ret_sq"), sem("ret_gated")
        merge_done = sem("merge_done")
        m_hi, m_lo = sem("m_hi"), sem("m_lo")
        x1_ready = sem("x1_ready")
        route_in, tab_in, gain_in = sem("route_in"), sem("tab_in"), sem("gain_in")
        row_sq, row_seed = sem("row_sq"), sem("row_seed")
        h2_ready, h2_stored = sem("h2_ready"), sem("h2_stored")
        h2_turned, h2_act, h2_dve = sem("h2_turned"), sem("h2_act"), sem("h2_dve")
        logit_done, score_ready = sem("logit_done"), sem("score_ready")
        sel_ready, pos_done = sem("sel_ready"), sem("pos_done")
        table_ready = sem("table_ready")
        zeroed, idx_zeroed, idx_stored, idx_loaded = sem("zeroed"), sem("idx_zeroed"), sem("idx_stored"), sem("idx_loaded")
        e_landed = [sem(f"e_landed{k}") for k in range(BLOCK_CHUNKS)]
        e_hi = sem("e_hi")
        e_lo = sem("e_lo")
        e_used = sem("e_used")
        row_copied, x_landed = sem("row_copied"), sem("x_landed")
        xe_turned, xe_hi, xe_lo = sem("xe_turned"), sem("xe_hi"), sem("xe_lo")
        silu_done, he_ready, he_turned, he_hi, he_lo = (
            sem("silu_done"), sem("he_ready"), sem("he_turned"), sem("he_hi"), sem("he_lo"))
        y_act, y_dve = sem("y_act"), sem("y_dve")
        y_stored = sem("y_stored")
        y_filled = sem("y_filled")
        ya_in, yb_in = [sem(f"ya_in{b}") for b in range(2)], [sem(f"yb_in{b}") for b in range(2)]
        gathers = sem("gathers")
        mixed, token_out = sem("mixed"), sem("token_out")
        cum_zero, id_ready = sem("cum_zero"), sem("id_ready")
        act_chain, dve_chain, pool_chain = sem("act_chain"), sem("dve_chain"), sem("pool_chain")
        out_done = sem("out_done")

        READ_BY_ACT = ("rk", "rq", "rg", "g_fox", "g_ret", "g_mem", "ff")
        READ_BY_DVE = ("fq", "fk", "mq", "mk", "o_fox", "o_ret", "o_mem")
        tiles = [c for c, (kind, _) in enumerate(CHUNKS) if kind not in NATURAL]
        tile_no = {c: i for i, c in enumerate(tiles)}
        fox_merged = count_before(READ_BY_DVE, FIRST["o_fox"] + KT)
        steps = [st for s in sorted(STEPS) for st in STEPS[s]]

        def numbers(names):
            return {st: i for i, st in enumerate(x for x in steps if x[0] in names)}

        stat_no = {st: i + 1 for st, i in numbers(("norm", "forget", "mem_norm")).items()}
        stat_no[("x", 0)] = 0
        sum_no = numbers(("norm", "forget"))
        norm_order = [("x", 0)] + [st for st in steps if st[0] in ("norm", "mem_norm")]
        norm_no = {st: i for i, st in enumerate(norm_order)}
        normed_by = {}
        for st in norm_order:
            normed_by[st] = (norm_tiles(st[1]) if st[0] == "norm" else 1) + (
                normed_by[norm_order[norm_no[st] - 1]] if norm_no[st] else 0)
        sc_no = numbers(("fox_score", "ret_score", "mem_score"))
        soft = {("fox", j): j for j in range(FOX_HEADS * TT)}
        soft |= {("mem", j): FOX_HEADS * TT + j for j in range(MEM_HEADS * TT)}
        sq_before = {n: sum(norm_tiles(m) for m in range(n)) for n in range(MQ_NORMS[-1] + 2)}
        last_slot = 4 * len(CHUNKS)
        assert max(STEPS) < last_slot

        def lhs_of(kind):
            return {"mk": mem_split, "mv": mem_split, "o_fox": o_split, "o_ret": o_split,
                    "o_mem": o_split}.get(kind, h_split)

        def norm_io(n):
            if n in FOX_NORMS:
                p = n // 2
                return [fox_raw[:, n % 2, :]], [(fox_q if n % 2 == 0 else fox_k)[:, p % 2, :]], S
            if n in RET_NORMS:
                return [ret_o[:, e, :] for e in range(2)], [ret_o[:, e, :] for e in range(2)], S
            if n in MK_NORMS:
                h = n - MK_NORMS[0]
                return ([mem_raw[:, e, 0:M] for e in range(2)],
                        [mkT[:, HEAD_TILES * h + e, :] for e in range(2)], M)
            return [mem_raw[:, e, :] for e in range(2)], [mem_q[:, e, :] for e in range(2)], S

        def norm_of_chunk(kind, i):
            if kind in ("fq", "fk"):
                return 2 * i + (kind == "fk"), 0
            return (MK_NORMS if kind == "mk" else MQ_NORMS)[i // 2], i % 2

        def chunk_of_norm(n):
            if n in FOX_NORMS:
                return FIRST["fq"] + n
            return (FIRST["mk"] - HEAD_TILES * MK_NORMS[0] if n in MK_NORMS else FIRST["mq"] - HEAD_TILES * MQ_NORMS[0]
                    ) + HEAD_TILES * n + 1

        def squares_by(n, e):
            return sq_before[n] + e + 1 - (HEAD_TILES * RET_HEADS if n > RET_NORMS[-1] else 0)

        block = ctx.enter_context(nc.Block())

        @block.sync
        def _(sp):
            for k in range(4):
                sp.dma_start(xT[:, 2 * k:2 * k + 2, :], dram["xT"][:, 2 * k:2 * k + 2, :]).then_inc(x_in[k], 16)
                if k == 0:
                    for dst, name in ((gains, "gains"), (avg, "avg"), (ident, "ident"), (mask_f, "mask")):
                        sp.dma_start(dst[:], dram[name]).then_inc(consts_in, 16)
            for c in range(len(CHUNKS)):
                if c >= RAW:
                    sp.wait_ge(lo_ready, c - RAW + 1)
                sp.dma_start(raw[:, c % RAW, :], dram["w"][c]).then_inc(landed[c % RAW], 16)
                kind, i = CHUNKS[c]
                if kind == "ff":
                    first = (TOP_K * S // P + 1) * P
                    sp.dma_start(dram["y"][first:, :].rearrange("(b p) n -> b p n", p=P),
                                 dram["w"][0:MAX_BLOCKS - TOP_K * S // P]).then_inc(y_filled, 16)
                if kind == "o_ret" and i == 1:
                    sp.wait_ge(pv_done, FOX_HEADS + RET_HEADS * HEAD_TILES)
                    sp.dma_start(memT, dram["memT"]).then_inc(mem_in, 16)
                if kind == "out" and i == 5:
                    sp.wait_ge(merge_done, 2 * KT)
                    sp.dma_start(x_nat, dram["x"].rearrange("(t p) n -> p t n", p=P)).then_inc(xn_in, 16)
            sp.wait_ge(o_lo, 3 * KT)
            for dst, name in ((router, "router"), (order4, "order4"), (iota, "iota"), (bias_b, "bias_b"),
                              (before, "before"), (ones, "ones"), (tokens_i[:], "tokens")):
                sp.dma_start(dst, dram[name]).then_inc(tab_in, 16)
            sp.dma_start(gain_b, dram["gain_b"]).then_inc(gain_in, 16)
            for tt in range(TT):
                sp.wait_ge(h2_ready, tt + 1)
                sp.dma_start(dram["h2"][tt * P:(tt + 1) * P, :], h2[:, tt, :]).then_inc(h2_stored, 16)
            sp.wait_ge(h2_stored, 16 * TT)
            sp.wait_ge(e_lo, BLOCK_CHUNKS)
            n_blocks = sp.value_load(blocks_i[0:1, IDX_COLS:IDX_COLS + 1], min_val=TOP_K * S // P, max_val=MAX_BLOCKS)
            with sp.Fori(0, n_blocks) as b:
                expert = sp.value_load(blocks_i[0:1, bass.ds(b, 1)], min_val=0, max_val=N_EXPERTS - 1)
                for k in range(BLOCK_CHUNKS):
                    sp.wait_ge(e_lo, b * BLOCK_CHUNKS + (k + 1))
                    sp.dma_start(e_raw[:, k, :], dram["experts"][expert, k]).then_inc(e_landed[k], 16)
            for tt in range(TT):
                sp.wait_ge(mixed, tt + 1)
                sp.dma_start(dram["out"][tt * P:(tt + 1) * P, :], x1[:, tt, :]).then_inc(out_done, 16)
            sp.wait_ge(out_done, 16 * TT)

        @block.tensor
        def _(pe):
            mm = nc.tensor.matmul

            def before_chunk(c):
                kind, i = CHUNKS[c]
                pe.wait_ge(lo_ready, c + 1)
                if kind in NATURAL:
                    if kind == "fv" and i == 0:
                        pe.wait_ge(stat_read, 1)
                    if kind == "fv" and i < 4:
                        pe.wait_ge(h_lo, 2 * i + 2)
                    if kind == "rv" and i == 0:
                        pe.wait_ge(tile_dve, count_before(READ_BY_DVE, c))
                    if kind == "mv" and i == 0:
                        pe.wait_ge(sc_read, FOX_HEADS * TT + RET_HEADS * TT)
                        pe.wait_ge(ret_sq, RET_HEADS * HEAD_TILES)
                        pe.wait_ge(ret_gated, RET_HEADS * HEAD_TILES)
                    if kind == "out" and i == 0:
                        pe.wait_ge(tile_dve, count_before(READ_BY_DVE, c))
                        pe.wait_ge(m_lo, KT)
                    return
                t = tile_no[c]
                if t >= 2:
                    a, d = (count_before(k, tiles[t - 2] + 1) for k in (READ_BY_ACT, READ_BY_DVE))
                    if a:
                        pe.wait_ge(tile_act, a)
                    if d:
                        pe.wait_ge(tile_dve, d)
                if kind == "ff":
                    pe.wait_ge(nat_read, 8)
                if kind == "rk" and i == 0:
                    pe.wait_ge(nat_read, 16)
                if kind == "mk" and i == 0:
                    pe.wait_ge(h_lo, 2 * KT)
                if kind in ("o_fox", "o_ret", "o_mem") and i == 0:
                    pe.wait_ge(o_lo, KT * (1 + ("o_fox", "o_ret", "o_mem").index(kind)))

            def quarter(c, q):
                kind, i = CHUNKS[c]
                x = lhs_of(kind)
                whi, wlo = w_split[:, 0, c % SPLIT, :], w_split[:, 1, c % SPLIT, :]
                if q == 0:
                    before_chunk(c)
                if kind in NATURAL:
                    g, kp, kk, half = i // 4, i % 4, q // 2, q % 2
                    rows = MT if kind == "mv" else TT
                    for tt in range(half * rows // 2, (half + 1) * rows // 2):
                        bank = SCORE + 2 * g + tt if kind == "mv" else 4 * g + tt
                        for n, (a, w) in enumerate(((0, whi), (0, wlo), (1, whi))):
                            last = mm(ps[:, bank, :], x[:, a, 2 * kp + kk, tt * P:(tt + 1) * P],
                                      w[:, kk * 512:(kk + 1) * 512],
                                      start=(kp == 0 and kk == 0 and n == 0), stop=(kp == 3 and kk == 1 and n == 2))
                else:
                    out = ps[:, tile_no[c] % 2, 0:M if kind == "mk" else S]
                    for k in (2 * q, 2 * q + 1):
                        for n, (w, a) in enumerate(((whi, 0), (wlo, 0), (whi, 1))):
                            last = mm(out, w[:, k * P:(k + 1) * P], x[:, a, k, :],
                                      start=(k == 0 and n == 0), stop=(k == KT - 1 and n == 2))
                if q == 3:
                    last.then_inc(w_used, 1)

            def sum_squares_of_input(width, before):
                for k in range(KT):
                    pe.wait_ge(x_sq, before + k + 1)
                    mm(ps[:, STAT, 0:width], avg[:, 2, :], sq[:, k % 2, 0:width],
                       start=(k == 0), stop=(k == KT - 1)).then_inc(x_sum, 1)

            pe.wait_ge(consts_in, 16 * 4)
            sum_squares_of_input(S, 0)
            pe.wait_ge(id_ready, 2)
            for slot in range(last_slot):
                quarter(slot // 4, slot % 4)
                for st in STEPS.get(slot, ()):
                    what, j = st
                    if what == "mem_norm":
                        pe.wait_ge(stat_read, stat_no[st])
                        sum_squares_of_input(M, KT)
                    elif what == "norm":
                        width, t = norm_io(j)[2], norm_tiles(j)
                        pe.wait_ge(stat_read, stat_no[st])
                        if j in RET_NORMS:
                            pe.wait_ge(ret_sq, HEAD_TILES * (j - RET_NORMS[0] + 1))
                        else:
                            pe.wait_ge(sq_ready, squares_by(j, t - 1))
                        for e in range(t):
                            last = mm(ps[:, STAT, 0:width], avg[:, 0 if j in FOX_NORMS else 1, :],
                                      sq[:, j % 2 if j in FOX_NORMS else e, 0:width], start=(e == 0), stop=(e == t - 1))
                        last.then_inc(stat_ready, 1)
                    elif what == "forget":
                        pe.wait_ge(stat_read, stat_no[st])
                        pe.wait_ge(cum_ready, 1)
                        mm(ps[:, STAT, :], ident[0:FOX_HEADS, j:j + 1].to_broadcast([FOX_HEADS, P]), cum[:, :],
                           start=True, stop=True).then_inc(stat_ready, 1)
                    elif what == "fox_score":
                        head, r = j // TT, j % TT
                        pair, rows = head // 2, slice(FOX_DIM * (head % 2), FOX_DIM * (head % 2) + FOX_DIM)
                        if j >= 2:
                            pe.wait_ge(sc_read, j - 1)
                        pe.wait_ge(normed, normed_by[("norm", 2 * pair + 1)])
                        out = ps[:, SCORE + j % 2, 0:P * (r + 1)]
                        mm(out, fox_q[rows, pair % 2, r * P:(r + 1) * P], fox_k[rows, pair % 2, 0:P * (r + 1)],
                           start=True, stop=True)
                        mm(out[:, P * r:], id_r[:], mask_r[:], start=False, stop=True,
                           skip_group_check=True).then_inc(sc_done, 1)
                    elif what == "fox_turn":
                        r = j % TT
                        if j >= 2:
                            pe.wait_ge(turn_read, j - 1)
                        pe.wait_ge(prob_scaled, j + 1)
                        for k in range(r + 1):
                            last = nc.tensor.transpose(ps[:, TURN + j % 2, k * P:(k + 1) * P],
                                                       prob[:, j % 2, k * P:(k + 1) * P], ident[:])
                        last.then_inc(turned, 1)
                    elif what == "fox_pv":
                        rows = slice(FOX_DIM * (j % 2), FOX_DIM * (j % 2) + FOX_DIM)
                        if j >= 2 and j % 2 == 0:
                            pe.wait_ge(o_lo, j // 2)
                        pe.wait_ge(turn_read, TT * (j + 1))
                        for k in reversed(range(TT)):
                            last = mm(ps[rows, PV, k * P:], fv[:, k, j * FOX_DIM:(j + 1) * FOX_DIM],
                                      fox_pt[:, j % 2, k, k * P:], start=(k == TT - 1), stop=(k == 0),
                                      skip_group_check=True)
                        last.then_inc(pv_done, 1)
                    elif what == "ret_score":
                        h, k = j // TT, j % TT
                        n = sc_no[st]
                        pe.wait_ge(sc_read, n - 1)
                        pe.wait_ge(rotated, 2 * h + 2)
                        for e in range(HEAD_TILES):
                            last = mm(ps[:, SCORE + n % 2, 0:S - k * P], ret_k[:, e, k * P:(k + 1) * P],
                                      ret_q[:, e, k * P:], start=(e == 0), stop=(e == HEAD_TILES - 1))
                        last.then_inc(sc_done, 1)
                    elif what == "ret_pv":
                        h, e = j // 2, j % 2
                        if h == 0:
                            pe.wait_ge(o_lo, KT)
                            pe.wait_ge(turn_read, FOX_HEADS * TT)
                        else:
                            pe.wait_ge(ret_sq, j - 1)
                            pe.wait_ge(ret_gated, j - 1)
                        pe.wait_ge(sc_read, FOX_HEADS * TT + TT * (h + 1))
                        for k in reversed(range(TT)):
                            last = mm(ps[:, PV if e == 0 else TURN, k * P:], rv[:, k, j * P:(j + 1) * P],
                                      ret_p[:, RET_AT[k]:RET_AT[k] + S - k * P],
                                      start=(k == TT - 1), stop=(k == 0), skip_group_check=True)
                        last.then_inc(pv_done, 1)
                    elif what == "mem_score":
                        h, r = j // TT, j % TT
                        n = sc_no[st]
                        pe.wait_ge(sc_read, n - 1)
                        if j == 0:
                            pe.wait_ge(nat_read, 20)
                        pe.wait_ge(normed, normed_by[("norm", MQ_NORMS[h])])
                        for e in range(HEAD_TILES):
                            last = mm(ps[:, SCORE + n % 2, 0:M], mem_q[:, e, r * P:(r + 1) * P],
                                      mkT[:, HEAD_TILES * h + e, :], start=(e == 0), stop=(e == HEAD_TILES - 1))
                        last.then_inc(sc_done, 1)
                    elif what == "mem_turn":
                        n = soft["mem", j]
                        pe.wait_ge(turn_read, n - 1)
                        pe.wait_ge(prob_scaled, n + 1)
                        for k in range(MT):
                            last = nc.tensor.transpose(ps[:, TURN + n % 2, k * P:(k + 1) * P],
                                                       mem_p[:, n % 2, k * P:(k + 1) * P], ident[:])
                        last.then_inc(turned, 1)
                    elif what == "mem_pv":
                        pe.wait_ge(o_lo, 2 * KT + j)
                        pe.wait_ge(turn_read, FOX_HEADS * TT + TT * (j // 2 + 1))
                        for k in range(MT):
                            last = mm(ps[:, PV, :], mv[:, k, j * P:(j + 1) * P], mem_pt[:, k, :],
                                      start=(k == 0), stop=(k == MT - 1))
                        last.then_inc(pv_done, 1)

            for k in range(KT):
                if k < TT:
                    pe.wait_ge(h2_ready, TT)
                else:
                    pe.wait_ge(h2_act if k % 2 == 0 else h2_dve, k // 2 - 1)
                for tt in range(TT):
                    last = nc.tensor.transpose(ps[:, k % 4, tt * P:(tt + 1) * P], h2[:, tt, k * P:(k + 1) * P], ident[:])
                last.then_inc(h2_turned, 1)
            pe.wait_ge(h2_act, KT // 2)
            pe.wait_ge(h2_dve, KT // 2)
            pe.wait_ge(tab_in, 16 * 7)
            for tt in range(TT):
                for k in range(KT):
                    last = mm(ps[:, 4, tt * N_EXPERTS:(tt + 1) * N_EXPERTS], h2T[:, k, tt * P:(tt + 1) * P],
                              router[:, k, :], start=(k == 0), stop=(k == KT - 1))
            last.then_inc(logit_done, 1)
            pe.wait_ge(sel_ready, 1)
            sel = r64[2]
            for tt in range(TT):
                for m in range(tt + 1):
                    mm(ps[:, 5, tt * N_EXPERTS:(tt + 1) * N_EXPERTS], before if m == tt else ones,
                       sel[:, m * N_EXPERTS:(m + 1) * N_EXPERTS], start=(m == 0), stop=(m == tt))
            for m in range(TT):
                last = mm(ps[:, 6, 0:N_EXPERTS], ones, sel[:, m * N_EXPERTS:(m + 1) * N_EXPERTS],
                          start=(m == 0), stop=(m == TT - 1))
            last.then_inc(pos_done, 1)

            def turn_rows():
                for k in range(KT):
                    last = nc.tensor.transpose(ps[:, 2 + k // 4, k % 4 * P:(k % 4 + 1) * P],
                                               x_rows[:, k * P:(k + 1) * P], ident[:])
                last.then_inc(xe_turned, 1)

            pe.wait_ge(x_landed, 16)
            pe.wait_ge(e_lo, BLOCK_CHUNKS)
            turn_rows()
            n_blocks = pe.value_load(blocks_i[0:1, IDX_COLS:IDX_COLS + 1], min_val=TOP_K * S // P, max_val=MAX_BLOCKS)
            with pe.Fori(0, n_blocks) as b:
                pe.wait_ge(xe_lo, b + 1)
                for k in range(BLOCK_CHUNKS):
                    if k == KT:
                        pe.wait_ge(x_landed, b * 16 + 32)
                        turn_rows()
                        pe.wait_ge(he_ready, b + 1)
                        for f_ in range(FT):
                            last = nc.tensor.transpose(ps[:, 4, f_ * P:(f_ + 1) * P], h_e[:, f_ * P:(f_ + 1) * P], ident[:])
                        last.then_inc(he_turned, 1)
                        pe.wait_ge(he_lo, b + 1)
                        pe.wait_ge(y_act, b + 1)
                        pe.wait_ge(y_dve, b + 1)
                    pe.wait_ge(e_lo, b * BLOCK_CHUNKS + (k + 1 + BLOCK_CHUNKS))
                    whi, wlo = ew_split[:, 0, k % E_SPLIT, :], ew_split[:, 1, k % E_SPLIT, :]
                    x, kk, first_bank = (xe_split, k, 0) if k < KT else (he_split, k - KT, 5)
                    depth = KT if k < KT else FT
                    for n, (a, w) in enumerate(((0, whi), (0, wlo), (1, whi))):
                        for half in range(2):
                            last = mm(ps[:, first_bank + half, :], x[:, a, kk, :], w[:, half * 512:(half + 1) * 512],
                                      start=(kk == 0 and n == 0), stop=(kk == depth - 1 and n == 2))
                    last.then_inc(e_used, 1)

        @block.scalar
        def _(act):
            links = [0]

            def link(ins):
                links[0] += 1
                ins.then_inc(act_chain, 1)
                act.wait_ge(act_chain, links[0])

            table = [None]

            def run(out, in_, func, **kw):
                need = "natural_log_exp_and_others" if func in (ACT.Exp, ACT.Ln) else (
                    None if func not in (ACT.Sigmoid, ACT.Silu) else str(func))
                if need and need != table[0]:
                    table[0] = need
                    if func in (ACT.Exp, ACT.Ln):
                        nc.scalar.preload_act_table_set(need)
                return nc.scalar.activation(out, in_, func, **kw)

            eps, one = cst[:, 0:1], cst[:, 1:2]

            def split_hi(c):
                act.wait_ge(landed[c % RAW], 16 * (c // RAW + 1))
                if c >= SPLIT:
                    act.wait_ge(w_used, c - SPLIT + 1)
                run(w_split[:, 0, c % SPLIT, :], raw[:, c % RAW, :], ACT.Copy).then_inc(hi_ready, 1)

            def squares_of_input(src, width, before):
                for k in range(KT):
                    if k >= 2:
                        act.wait_ge(x_sum, before + k - 1)
                    if before == 0 and k % 2 == 0:
                        act.wait_ge(x_in[k // 2], 16)
                    run(sq[:, k % 2, 0:width], src[:, k, :], ACT.Square).then_inc(x_sq, 1)

            def seed(st, width):
                if st != ("x", 0):
                    act.wait_ge(normed, normed_by[norm_order[norm_no[st] - 1]])
                if st[0] == "norm":
                    act.wait_ge(stat_ready, sum_no[st] + 1)
                else:
                    act.wait_ge(x_sum, KT * (1 + (st[0] == "mem_norm")))
                run(var[:, 0:width], ps[:, STAT, 0:width], ACT.Identity, bias=eps).then_inc(stat_read, 1)
                act.wait_ge(stat_read, stat_no[st] + 1)
                link(run(rstd[:, 0:width], var[:, 0:width], ACT.Ln))
                run(rstd[:, 0:width], rstd[:, 0:width], ACT.Exp, scale=-0.5).then_inc(seed_ready, 1)

            def split_normed(k, width, tmp, dst, before):
                act.wait_ge(h_f, before + k + 1)
                run(dst[:, 0, k, :], tmp[:, k % 2, 0:width], ACT.Copy).then_inc(h_hi, 1)

            def after_chunk(c):
                kind, i = CHUNKS[c]
                if kind in NATURAL:
                    g, kp = i // 4, i % 4
                    if kp < 3 or kind == "out":
                        return
                    act.wait_ge(w_used, c + 1)
                    if kind == "mv":
                        if g == 0:
                            act.wait_ge(h_lo, 2 * KT)
                        run(mv[:, 0, g * 512:(g + 1) * 512], ps[:, SCORE + 2 * g, :], ACT.Copy).then_inc(nat_read, 1)
                    else:
                        dst = fv if kind == "fv" else rv
                        for tt in (0, 1):
                            run(dst[:, tt, g * 512:(g + 1) * 512], ps[:, 4 * g + tt, :], ACT.Copy).then_inc(nat_read, 1)
                    return
                src = ps[:, tile_no[c] % 2, 0:M if kind == "mk" else S]
                if kind in ("fq", "fk", "mq", "mk"):
                    n, e = norm_of_chunk(kind, i)
                    act.wait_ge(w_used, c + 1)
                    if n in FOX_NORMS and n < 2:
                        act.wait_ge(x_sum, KT)
                    elif n == MK_NORMS[0]:
                        act.wait_ge(x_sum, 2 * KT)
                    else:
                        act.wait_ge(stat_ready, sum_no["norm", n - 2 if n in FOX_NORMS else n - 1] + 1)
                    width = M if kind == "mk" else S
                    run(sq[:, n % 2 if n in FOX_NORMS else e, 0:width], src, ACT.Square).then_inc(sq_ready, 1)
                elif kind == "ff":
                    act.wait_ge(w_used, c + 1)
                    act.wait_ge(h_lo, KT)
                    z, az, e = logits[0:FOX_HEADS, 0, :], logits[0:FOX_HEADS, 1, :], prob[0:FOX_HEADS, 0, :]
                    run(z, src[0:FOX_HEADS, :], ACT.Identity, bias=gains[0:FOX_HEADS, B_FF:B_FF + 1]).then_inc(tile_act, 1)
                    act.wait_ge(tile_act, 1)
                    link(run(az, z, ACT.Abs))
                    link(run(e, az, ACT.Exp, scale=-1.0))
                    run(e, e, ACT.Ln, bias=one[0:FOX_HEADS, :]).then_inc(gate_log, 1)
                elif kind in ("rk", "rq"):
                    n = 2 * (i // 2) + (kind == "rq")
                    act.wait_ge(w_used, c + 1)
                    if n:
                        act.wait_ge(rotated, n)
                    else:
                        act.wait_ge(tile_dve, fox_merged)
                    run(ret_raw[:, i % 2, :], src, ACT.Copy).then_inc(tile_act, 1)
                elif kind == "rg":
                    act.wait_ge(w_used, c + 1)
                    if i >= 2:
                        act.wait_ge(o_lo, KT + i // 2 * 2)
                    run(ret_o[:, i % 2, :], src, ACT.Silu).then_inc(tile_act, 1)
                elif kind in ("g_fox", "g_ret", "g_mem"):
                    act.wait_ge(w_used, c + 1)
                    b = ("g_fox", "g_ret", "g_mem").index(kind)
                    if b == 2:
                        act.wait_ge(merge_done, KT)
                    elif b:
                        act.wait_ge(tile_dve, fox_merged)
                    else:
                        act.wait_ge(h_lo, KT)
                    run(gate[:, i, :], src, ACT.Sigmoid).then_inc(tile_act, 1)
                elif kind == "o_mem":
                    act.wait_ge(merge_done, KT + i + 1)
                    run(h_split[:, 0, i, :], merged[:, i, :], ACT.Copy).then_inc(m_hi, 1)

            act.wait_ge(cum_zero, 1)
            squares_of_input(xT, S, 0)
            seed(("x", 0), S)
            act.wait_ge(consts_in, 16 * 4)
            run(id_r[:], ident[:], ACT.Copy).then_inc(id_ready, 1)
            run(mask_r[:], mask_f[:], ACT.Copy).then_inc(id_ready, 1)
            for k in range(KT):
                split_normed(k, S, logits, h_split, 0)
                if k % 2 == 1 and k // 2 < AHEAD:
                    split_hi(k // 2)
            for slot in range(last_slot + 1):
                c = slot // 4
                if slot % 4 == 0:
                    if c:
                        after_chunk(c - 1)
                    if c + AHEAD < len(CHUNKS):
                        split_hi(c + AHEAD)
                for st in STEPS.get(slot, ()):
                    what, j = st
                    if what == "norm":
                        if j == MK_NORMS[0]:
                            act.wait_ge(h_f, 2 * KT)
                        seed(st, norm_io(j)[2])
                    elif what == "mem_norm":
                        act.wait_ge(stat_ready, sum_no["norm", RET_NORMS[-1]] + 1)
                        act.wait_ge(mem_in, 16)
                        squares_of_input(memT, M, KT)
                        seed(st, M)
                    elif what == "mem_split":
                        act.wait_ge(w_used, FIRST["o_ret"] + KT)
                        for k in range(KT):
                            split_normed(k, M, ret_raw, mem_split, KT)
                    elif what == "forget":
                        act.wait_ge(stat_ready, sum_no[st] + 1)
                        if j >= 2:
                            act.wait_ge(sc_read, TT * (j - 1))
                        else:
                            act.wait_ge(cum_ready, 1)
                        run(forget[:, j % 2, :], ps[:, STAT, :], ACT.Copy).then_inc(stat_read, 1)
                    elif what == "fox_score":
                        w = P * (j % TT + 1)
                        act.wait_ge(sc_read, j + 1)
                        if j >= 2:
                            act.wait_ge(turned, j - 1)
                        run(prob[:, j % 2, 0:w], logits[:, j % 2, 0:w], ACT.Exp, scale=-1.0,
                            bias=stat[:, j % 2:j % 2 + 1], accum_out=stat[:, 2 + j % 2:3 + j % 2]).then_inc(prob_ready, 1)
                    elif what == "fox_turn":
                        head, r = j // TT, j % TT
                        act.wait_ge(turned, j + 1)
                        if head >= 2:
                            act.wait_ge(pv_done, head - 1)
                        run(fox_pt[:, head % 2, 0:r + 1, r * P:(r + 1) * P],
                            ps[:, TURN + j % 2, 0:P * (r + 1)].rearrange("p (k i) -> p k i", i=P),
                            ACT.Copy).then_inc(turn_read, 1)
                    elif what == "fox_pv" and j % 2 == 1:
                        act.wait_ge(pv_done, j + 1)
                        run(o_split[:, 0, j // 2, :], ps[:, PV, :], ACT.Copy).then_inc(o_hi, 1)
                    elif what == "ret_pv":
                        act.wait_ge(pv_done, FOX_HEADS + j + 1)
                        e = j % 2
                        n = RET_NORMS[0] + j // 2
                        act.wait_ge(stat_ready, sum_no["norm", n - 1] + 1)
                        run(sq[:, e, :], ps[:, PV if e == 0 else TURN, :], ACT.Square).then_inc(ret_sq, 1)
                    elif what == "ret_out":
                        act.wait_ge(normed, normed_by["norm", RET_NORMS[j]])
                        if j == 0:
                            act.wait_ge(w_used, FIRST["o_fox"] + KT)
                        for e in range(HEAD_TILES):
                            run(o_split[:, 0, HEAD_TILES * j + e, :], ret_o[:, e, :], ACT.Copy).then_inc(o_hi, 1)
                    elif what == "mem_score":
                        n = soft["mem", j]
                        act.wait_ge(mem_min, j + 1)
                        if j >= 2:
                            act.wait_ge(turned, n - 1)
                        run(mem_p[:, n % 2, :], ps[:, SCORE + sc_no[st] % 2, 0:M], ACT.Exp, scale=-1.0,
                            bias=stat[:, n % 2:n % 2 + 1], accum_out=stat[:, 2 + n % 2:3 + n % 2]).then_inc(sc_read, 1)
                    elif what == "mem_turn":
                        n = soft["mem", j]
                        h, r = j // TT, j % TT
                        act.wait_ge(turned, n + 1)
                        if h:
                            act.wait_ge(pv_done, FOX_HEADS + 2 * RET_HEADS + 2 * h)
                        run(mem_pt[:, :, r * P:(r + 1) * P],
                            ps[:, TURN + n % 2, 0:M].rearrange("p (k i) -> p k i", i=P), ACT.Copy).then_inc(turn_read, 1)
                    elif what == "mem_pv":
                        act.wait_ge(pv_done, FOX_HEADS + 2 * RET_HEADS + j + 1)
                        if j == 0:
                            act.wait_ge(w_used, FIRST["mq"])
                        run(o_split[:, 0, j, :], ps[:, PV, :], ACT.Copy).then_inc(o_hi, 1)

            for tt in range(TT):
                act.wait_ge(x1_ready, TT + tt + 1)
                if tt:
                    act.wait_ge(row_sq, tt)
                else:
                    act.wait_ge(o_lo, 3 * KT)
                run(scratch, x1[:, tt, :], ACT.Square, accum_out=sums[:, 0, tt:tt + 1]).then_inc(row_sq, 1)
            act.wait_ge(row_sq, TT)
            link(run(sums[:, 1, :], sums[:, 0, :], ACT.Ln, scale=1.0 / D, bias=eps))
            run(sums[:, 1, :], sums[:, 1, :], ACT.Exp, scale=-0.5).then_inc(row_seed, 1)
            for k in range(0, KT, 2):
                act.wait_ge(h2_turned, k + 1)
                act.wait_ge(merge_done, 2 * KT)
                run(h2T[:, k, :], ps[:, k % 4, :], ACT.Copy).then_inc(h2_act, 1)
            act.wait_ge(logit_done, 1)
            run(r64[0], ps[:, 4, 0:TT * N_EXPERTS], ACT.Sigmoid).then_inc(score_ready, 1)

            def split_rows():
                for h in range(2):
                    ins = run(xe_split[:, 0, 4 * h:4 * h + 4, :], ps[:, 2 + h, :].rearrange("p (k s) -> p k s", k=4), ACT.Copy)
                ins.then_inc(xe_hi, 1)

            act.wait_ge(xe_turned, 1)
            split_rows()
            act.wait_ge(y_filled, 16)
            act.wait_ge(e_lo, BLOCK_CHUNKS)
            n_blocks = act.value_load(blocks_i[0:1, IDX_COLS:IDX_COLS + 1], min_val=TOP_K * S // P, max_val=MAX_BLOCKS)

            def store_y(b):
                act.wait_ge(e_used, b * BLOCK_CHUNKS + E_SPLIT)
                act.wait_ge(y_stored, b * 16 + 16)
                run(y_rows[:, 0:512], ps[:, 5, :], ACT.Copy).then_inc(y_act, 1)
                act.wait_ge(y_act, b + 1)
                act.wait_ge(y_dve, b + 1)
                nc.scalar.dma_start(dram["y"][bass.ds(b * P, P), :], y_rows).then_inc(y_stored, 16)

            with act.Fori(0, n_blocks) as b:
                for k in range(BLOCK_CHUNKS):
                    if k == BLOCK_CHUNKS - 1:
                        act.wait_ge(e_used, b * BLOCK_CHUNKS + (KT + E_SPLIT))
                        run(h_act, ps[:, 0, :], ACT.Silu).then_inc(silu_done, 1)
                    act.wait_ge(e_landed[k], b * 16 + 16)
                    act.wait_ge(e_used, b * BLOCK_CHUNKS + (k + 1))
                    run(ew_split[:, 0, k % E_SPLIT, :], e_raw[:, k, :], ACT.Copy).then_inc(e_hi, 1)
                    if k == 3:
                        store_y(b)
                act.wait_ge(xe_turned, b + 2)
                split_rows()
                act.wait_ge(he_turned, b + 1)
                run(he_split[:, 0, :, :], ps[:, 4, :].rearrange("p (f s) -> p f s", f=FT), ACT.Copy).then_inc(he_hi, 1)
            store_y(n_blocks)

        @block.vector
        def _(dve):
            links = [0]

            def link(ins):
                links[0] += 1
                ins.then_inc(dve_chain, 1)
                dve.wait_ge(dve_chain, links[0])

            def f(ap):
                return ap.bitcast(F32)

            def split_lo(c):
                dve.wait_ge(hi_ready, c + 1)
                nc.vector.tensor_tensor(w_split[:, 1, c % SPLIT, :], raw[:, c % RAW, :],
                                        f(w_split[:, 0, c % SPLIT, :]), ALU.subtract).then_inc(lo_ready, 1)

            def norm_input(src, width, tmp, dst, g, before):
                for k in range(KT):
                    if k >= 2:
                        dve.wait_ge(h_lo, before + k - 1)
                    nc.vector.scalar_tensor_tensor(tmp[:, k % 2, 0:width], src[:, k, :], gains[:, g + k:g + k + 1],
                                                   rstd[:, 0:width], ALU.mult, ALU.mult).then_inc(h_f, 1)
                    dve.wait_ge(h_hi, before + k + 1)
                    nc.vector.tensor_tensor(dst[:, 1, k, :], tmp[:, k % 2, 0:width], f(dst[:, 0, k, :]),
                                            ALU.subtract).then_inc(h_lo, 1)
                    if before == 0 and k % 2 == 1 and k // 2 < AHEAD:
                        split_lo(k // 2)

            def after_chunk(c):
                kind, i = CHUNKS[c]
                if kind in NATURAL:
                    g, kp = i // 4, i % 4
                    if kp < 3:
                        return
                    dve.wait_ge(w_used, c + 1)
                    if kind == "mv":
                        if g == 0:
                            dve.wait_ge(h_lo, 2 * KT)
                        nc.vector.tensor_copy(mv[:, 1, g * 512:(g + 1) * 512], ps[:, SCORE + 2 * g + 1, :]).then_inc(nat_read, 1)
                    elif kind == "out":
                        dve.wait_ge(xn_in, 16)
                        for tt in range(TT):
                            cols = slice(g * 512, (g + 1) * 512)
                            nc.vector.tensor_tensor(x1[:, tt, cols], ps[:, 4 * g + tt, :], x_nat[:, tt, cols],
                                                    ALU.add).then_inc(x1_ready, 1)
                    else:
                        dst = fv if kind == "fv" else rv
                        for tt in (2, 3):
                            nc.vector.tensor_copy(dst[:, tt, g * 512:(g + 1) * 512], ps[:, 4 * g + tt, :]).then_inc(nat_read, 1)
                    return
                src = ps[:, tile_no[c] % 2, 0:M if kind == "mk" else S]
                if kind in ("fq", "fk", "mq", "mk"):
                    n, e = norm_of_chunk(kind, i)
                    dve.wait_ge(sq_ready, squares_by(n, e))
                    if n >= 2 and n in FOX_NORMS:
                        dve.wait_ge(normed, normed_by["norm", n - 2])
                    elif n not in FOX_NORMS:
                        dve.wait_ge(normed, normed_by[norm_order[norm_no["norm", n] - 1]])
                    dst = fox_raw[:, n % 2, :] if n in FOX_NORMS else mem_raw[:, e, 0:M if kind == "mk" else S]
                    g = {"fq": G_FQ, "fk": G_FK, "mq": G_MQ + e, "mk": G_MK + e}[kind]
                    scale = {"fq": -FOX_DIM ** -0.5, "mq": -(2 * P) ** -0.5}.get(kind, 1.0)
                    nc.vector.tensor_scalar(dst, src, gains[:, g:g + 1], scale, ALU.mult, ALU.mult).then_inc(tile_dve, 1)
                elif kind == "ff":
                    z, e, lf = logits[0:FOX_HEADS, 0, :], prob[0:FOX_HEADS, 0, :], prob[0:FOX_HEADS, 1, :]
                    dve.wait_ge(gate_log, 1)
                    link(nc.vector.memset(forget[0:FOX_HEADS, 0, :], 1.0))
                    link(nc.vector.scalar_tensor_tensor(lf, z, 0.0, e, ALU.min, ALU.subtract))
                    nc.vector.tensor_tensor_scan(cum[:, :], forget[0:FOX_HEADS, 0, :], lf, 0.0,
                                                 ALU.mult, ALU.add).then_inc(cum_ready, 1)
                elif kind in ("o_fox", "o_ret", "o_mem"):
                    b = ("o_fox", "o_ret", "o_mem").index(kind)
                    dve.wait_ge(w_used, c + 1)
                    dve.wait_ge(tile_act, count_before(READ_BY_ACT, FIRST[kind]))
                    if b == 0:
                        nc.vector.tensor_tensor(merged[:, i, :], src, gate[:, i, :], ALU.mult).then_inc(tile_dve, 1)
                        return
                    nc.vector.tensor_tensor(gate[:, i, :], src, gate[:, i, :], ALU.mult).then_inc(tile_dve, 1)
                    dve.wait_ge(tile_dve, count_before(READ_BY_DVE, c + 1))
                    nc.vector.tensor_tensor(merged[:, i, :], merged[:, i, :], gate[:, i, :],
                                            ALU.add).then_inc(merge_done, 1)
                    if b == 2:
                        dve.wait_ge(m_hi, i + 1)
                        nc.vector.tensor_tensor(h_split[:, 1, i, :], merged[:, i, :], f(h_split[:, 0, i, :]),
                                                ALU.subtract).then_inc(m_lo, 1)

            def lo_part(t, src):
                dve.wait_ge(o_hi, t + 1)
                nc.vector.tensor_tensor(o_split[:, 1, t % KT, :], src, f(o_split[:, 0, t % KT, :]),
                                        ALU.subtract).then_inc(o_lo, 1)

            link(nc.vector.memset(cst[:, 0:1], EPS))
            nc.vector.memset(cst[:, 1:2], 1.0).then_inc(cum_zero, 1)
            dve.wait_ge(normed, 1)
            dve.wait_ge(consts_in, 16 * 4)
            norm_input(xT, S, logits, h_split, G_MIX, 0)
            for slot in range(last_slot + 1):
                c = slot // 4
                if slot % 4 == 0:
                    if c:
                        after_chunk(c - 1)
                    if c + AHEAD < len(CHUNKS):
                        split_lo(c + AHEAD)
                for st in STEPS.get(slot, ()):
                    what, j = st
                    if what == "mem_split":
                        dve.wait_ge(normed, normed_by["mem_norm", 0])
                        dve.wait_ge(o_lo, 2 * KT)
                        norm_input(memT, M, ret_raw, mem_split, G_MEM, KT)
                    elif what == "fox_score":
                        w = P * (j % TT + 1)
                        dve.wait_ge(sc_done, j + 1)
                        if j >= 2:
                            dve.wait_ge(prob_ready, j - 1)
                        dve.wait_ge(stat_read, stat_no["forget", j // TT] + 1)
                        nc.vector.tensor_tensor_reduce(logits[:, j % 2, 0:w], ps[:, SCORE + j % 2, 0:w],
                                                       forget[:, j // TT % 2, 0:w], 1.0, 3.0e38, ALU.add, ALU.min,
                                                       stat[:, j % 2:j % 2 + 1]).then_inc(sc_read, 1)
                    elif what in ("fox_scale", "mem_scale"):
                        n = soft[what[:3], j]
                        w = P * (j % TT + 1) if what[0] == "f" else M
                        buf = (prob if what[0] == "f" else mem_p)[:, n % 2, 0:w]
                        if what[0] == "f":
                            dve.wait_ge(prob_ready, j + 1)
                        else:
                            dve.wait_ge(sc_read, sc_no["mem_score", j] + 1)
                        link(nc.vector.reciprocal(stat[:, 4 + n % 2:5 + n % 2], stat[:, 2 + n % 2:3 + n % 2]))
                        nc.vector.tensor_scalar(buf, buf, stat[:, 4 + n % 2:5 + n % 2], None,
                                                ALU.mult).then_inc(prob_scaled, 1)
                    elif what == "fox_pv" and j % 2 == 1:
                        lo_part(j // 2, ps[:, PV, :])
                    elif what == "ret_score":
                        h, k = j // TT, j % TT
                        n = sc_no[st]
                        w = S - k * P
                        at = RET_AT[k]
                        dve.wait_ge(sc_done, n + 1)
                        dve.wait_ge(decay_in, 16 * (h + 1))
                        if h:
                            dve.wait_ge(pv_done, FOX_HEADS + HEAD_TILES * h)
                        nc.vector.tensor_tensor(ret_p[:, at:at + w], ps[:, SCORE + n % 2, 0:w], decay[:, 0:w],
                                                ALU.mult).then_inc(sc_read, 1)
                    elif what == "ret_pv":
                        h, e = j // 2, j % 2
                        dve.wait_ge(pv_done, FOX_HEADS + j + 1)
                        dve.wait_ge(ret_sq, j + 1)
                        dve.wait_ge(tile_act, count_before(READ_BY_ACT, FIRST["rk"] + 6 * h + 5 + e))
                        nc.vector.tensor_tensor(ret_o[:, e, :], ret_o[:, e, :], ps[:, PV if e == 0 else TURN, :],
                                                ALU.mult).then_inc(ret_gated, 1)
                    elif what == "ret_out":
                        dve.wait_ge(normed, normed_by["norm", RET_NORMS[j]])
                        for e in range(HEAD_TILES):
                            lo_part(KT + HEAD_TILES * j + e, ret_o[:, e, :])
                    elif what == "mem_score":
                        n = soft["mem", j]
                        dve.wait_ge(sc_done, sc_no[st] + 1)
                        if j >= 2:
                            dve.wait_ge(sc_read, sc_no[st] - 1)
                        nc.vector.tensor_reduce(stat[:, n % 2:n % 2 + 1], ps[:, SCORE + sc_no[st] % 2, 0:M], AX.X,
                                                ALU.min).then_inc(mem_min, 1)
                    elif what == "mem_pv":
                        lo_part(2 * KT + j, ps[:, PV, :])

            V = nc.vector
            dve.wait_ge(o_lo, 3 * KT)
            V.memset(zero_i[:], 0).then_inc(zeroed, 1)
            dve.wait_ge(row_seed, 1)
            ms, r, t = sums[:, 2, :], sums[:, 1, :], sums[:, 3, :]
            link(V.tensor_scalar(ms, sums[:, 0, :], 1.0 / D, EPS, ALU.mult, ALU.add))
            link(V.tensor_tensor(t, ms, r, ALU.mult))
            link(V.tensor_tensor(t, t, r, ALU.mult))
            link(V.tensor_scalar(t, t, -0.5, 1.5, ALU.mult, ALU.add))
            link(V.tensor_tensor(r, r, t, ALU.mult))
            dve.wait_ge(gain_in, 16)
            dve.wait_ge(m_hi, KT)
            for tt in range(TT):
                V.scalar_tensor_tensor(h2[:, tt, :], x1[:, tt, :], r[:, tt:tt + 1], gain_b, ALU.mult,
                                       ALU.mult).then_inc(h2_ready, 1)
            for k in range(1, KT, 2):
                dve.wait_ge(h2_turned, k + 1)
                V.tensor_copy(h2T[:, k, :], ps[:, k % 4, :]).then_inc(h2_dve, 1)

            score, biased, sel, w, pos = r64[0:5]
            t64a, t64b = r64[5], r64[6]

            def experts_of(ap):
                return ap.rearrange("p (q e) -> p q e", e=PER_GROUP)

            def ranks(v, n, out):
                a4 = v.unsqueeze(2).to_broadcast([P, n, 4, 4])
                b4 = v.unsqueeze(3).to_broadcast([P, n, 4, 4])
                g4 = r256a[:, 0:n * 16].rearrange("p (q b a) -> p q b a", b=4, a=4)
                e4 = r256b[:, 0:n * 16].rearrange("p (q b a) -> p q b a", b=4, a=4)
                V.tensor_tensor(g4, a4, b4, ALU.is_gt)
                link(V.tensor_tensor(e4, a4, b4, ALU.is_equal))
                link(V.tensor_tensor(e4, e4, order4.unsqueeze(1).to_broadcast([P, n, 4, 4]), ALU.mult))
                link(V.tensor_tensor(g4, g4, e4, ALU.add))
                link(V.tensor_reduce(out, g4, AX.X, ALU.add))

            dve.wait_ge(score_ready, 1)
            dve.wait_ge(tab_in, 16 * 7)
            link(V.tensor_tensor(biased, score, bias_b, ALU.add))
            pair = biased.rearrange("p (q c d) -> p q c d", c=2, d=2)
            hi2 = t64a[:, 0:32].rearrange("p (q c) -> p q c", c=2)
            lo2 = t64a[:, 32:64].rearrange("p (q c) -> p q c", c=2)
            V.tensor_tensor(hi2, pair[:, :, :, 0], pair[:, :, :, 1], ALU.max)
            link(V.tensor_tensor(lo2, pair[:, :, :, 0], pair[:, :, :, 1], ALU.min))
            V.tensor_tensor(r16[0], hi2[:, :, 0], hi2[:, :, 1], ALU.max)
            V.tensor_tensor(r16[1], hi2[:, :, 0], hi2[:, :, 1], ALU.min)
            link(V.tensor_tensor(r16[2], lo2[:, :, 0], lo2[:, :, 1], ALU.max))
            link(V.tensor_tensor(r16[1], r16[1], r16[2], ALU.max))
            link(V.tensor_tensor(r16[3], r16[0], r16[1], ALU.add))
            ranks(r16[3].rearrange("p (t g) -> p t g", g=N_GROUPS), TT, r16[4].rearrange("p (t g) -> p t g", g=N_GROUPS))
            link(V.tensor_scalar(r16[4], r16[4], 1.0, None, ALU.is_lt))
            ranks(experts_of(biased), TT * N_GROUPS, experts_of(t64b))
            link(V.tensor_scalar(t64b, t64b, float(TOP_K), None, ALU.is_lt))
            V.tensor_tensor(experts_of(sel), experts_of(t64b), r16[4].unsqueeze(2).to_broadcast([P, TT * N_GROUPS, PER_GROUP]),
                            ALU.mult).then_inc(sel_ready, 1)
            dve.wait_ge(sel_ready, 1)
            link(V.tensor_tensor(w, score, sel, ALU.mult))
            by_token = (lambda ap: ap.rearrange("p (t e) -> p t e", e=N_EXPERTS))
            denom = r16[5][:, 0:TT]
            link(V.tensor_reduce(denom, by_token(w), AX.X, ALU.add))
            link(V.reciprocal(denom, denom))
            dve.wait_ge(pos_done, 1)
            count, blocks, ends, starts = r16[6], r16[7], r16[8], r16[9]
            link(V.tensor_copy(count, ps[:, 6, 0:N_EXPERTS]))
            link(V.tensor_scalar(blocks, count, 0.5, None, ALU.is_gt))
            for n in range(1, TT):
                link(V.scalar_tensor_tensor(blocks, count, n * P + 0.5, blocks, ALU.is_gt, ALU.add))
            link(V.tensor_tensor_scan(ends, ones[:, 0:N_EXPERTS], blocks, 0.0, ALU.mult, ALU.add))
            link(V.tensor_tensor(starts, ends, blocks, ALU.subtract))
            link(V.scalar_tensor_tensor(by_token(pos), starts.unsqueeze(1).to_broadcast([P, TT, N_EXPERTS]), float(P),
                                        by_token(ps[:, 5, 0:TT * N_EXPERTS]), ALU.mult, ALU.add))
            far = float(IDX_COLS * P)
            link(V.tensor_scalar(t64a, sel, -far, far, ALU.mult, ALU.add))
            link(V.tensor_tensor(t64a, t64a, pos, ALU.add))
            first, second = r16[10][:, 0:TT], r16[11][:, 0:TT]
            link(V.tensor_reduce(first, by_token(t64a), AX.X, ALU.min))
            link(V.scalar_tensor_tensor(t64b, pos, 1.0, sel, ALU.add, ALU.mult))
            link(V.tensor_reduce(second, by_token(t64b), AX.X, ALU.max))
            link(V.tensor_scalar(second, second, -1.0, None, ALU.add))
            for a, slot_ in ((0, first), (1, second)):
                link(V.tensor_tensor(by_token(t64a), by_token(pos), slot_.unsqueeze(2).to_broadcast([P, TT, N_EXPERTS]),
                                     ALU.is_equal))
                link(V.tensor_tensor(t64a, t64a, w, ALU.mult))
                link(V.tensor_reduce(token_w[:, a, :], by_token(t64a), AX.X, ALU.add))
                link(V.tensor_tensor(token_w[:, a, :], token_w[:, a, :], denom, ALU.mult))
                V.tensor_copy(slots_i[:, a, :], slot_).then_inc(table_ready, 1)
                V.tensor_scalar(y_slot_i[:, a, :], slot_, float(P), None, ALU.add)
            be = r384.rearrange("p (b e) -> p b e", e=N_EXPERTS)
            link(V.tensor_tensor(be, iota.unsqueeze(2).to_broadcast([P, IDX_COLS, N_EXPERTS]),
                                 ends.unsqueeze(1).to_broadcast([P, IDX_COLS, N_EXPERTS]), ALU.is_ge))
            link(V.tensor_reduce(r256a[:, 0:IDX_COLS], be, AX.X, ALU.add))
            link(V.tensor_scalar(r256a[:, 0:IDX_COLS], r256a[:, 0:IDX_COLS], float(N_EXPERTS - 1), None, ALU.min))
            link(V.tensor_copy(blocks_i[:, 0:IDX_COLS], r256a[:, 0:IDX_COLS]))
            link(V.tensor_copy(blocks_i[:, IDX_COLS:IDX_COLS + 1], ends[:, N_EXPERTS - 1:N_EXPERTS]))
            dve.wait_ge(w_used, len(CHUNKS))
            V.memset(stat[:, 0:1], 0.0).then_inc(e_lo, BLOCK_CHUNKS)
            V.memset(stat[:, 1:2], 0.0).then_inc(e_used, E_SPLIT)
            V.memset(stat[:, 2:3], 0.0).then_inc(y_stored, 16)

            def rows_lo():
                for h in range(2):
                    ins = V.tensor_tensor(xe_split[:, 1, 4 * h:4 * h + 4, :], ps[:, 2 + h, :].rearrange("p (k s) -> p k s", k=4),
                                          f(xe_split[:, 0, 4 * h:4 * h + 4, :]), ALU.subtract)
                ins.then_inc(xe_lo, 1)

            dve.wait_ge(xe_hi, 1)
            rows_lo()
            n_blocks = dve.value_load(blocks_i[0:1, IDX_COLS:IDX_COLS + 1], min_val=TOP_K * S // P, max_val=MAX_BLOCKS)

            def leave_y(b):
                dve.wait_ge(e_used, b * BLOCK_CHUNKS + E_SPLIT)
                dve.wait_ge(y_stored, b * 16 + 16)
                V.tensor_copy(y_rows[:, 512:], ps[:, 6, :]).then_inc(y_dve, 1)

            with dve.Fori(0, n_blocks) as b:
                for k in range(BLOCK_CHUNKS):
                    if k == BLOCK_CHUNKS - 1:
                        dve.wait_ge(silu_done, b + 1)
                        V.tensor_tensor(h_e, h_act, ps[:, 1, :], ALU.mult).then_inc(he_ready, 1)
                    dve.wait_ge(e_hi, b * BLOCK_CHUNKS + (k + 1))
                    V.tensor_tensor(ew_split[:, 1, k % E_SPLIT, :], e_raw[:, k, :], f(ew_split[:, 0, k % E_SPLIT, :]),
                                    ALU.subtract).then_inc(e_lo, 1)
                    if k == 3:
                        leave_y(b)
                dve.wait_ge(xe_hi, b + 2)
                rows_lo()
                dve.wait_ge(he_hi, b + 1)
                V.tensor_tensor(he_split[:, 1, :, :], ps[:, 4, :].rearrange("p (f s) -> p f s", f=FT),
                                f(he_split[:, 0, :, :]), ALU.subtract).then_inc(he_lo, 1)
            leave_y(n_blocks)

            for tt in range(TT):
                for a, (rows, landed_) in enumerate(((y_a, ya_in), (y_b, yb_in))):
                    dve.wait_ge(landed_[tt % 2], 16 * (tt // 2 + 1))
                    V.scalar_tensor_tensor(x1[:, tt, :], rows[:, tt % 2, :], token_w[:, a, tt:tt + 1], x1[:, tt, :],
                                           ALU.mult, ALU.add).then_inc(token_out if a == 0 else mixed, 1)
                    if a == 0:
                        dve.wait_ge(token_out, tt + 1)

        @block.gpsimd
        def _(pool):
            links = [0]

            def link(ins):
                links[0] += 1
                ins.then_inc(pool_chain, 1)
                pool.wait_ge(pool_chain, links[0])

            tt_ = nc.gpsimd.tensor_tensor

            def refine(st, width):
                pool.wait_ge(seed_ready, norm_no[st] + 1)
                v, r, t = var[:, 0:width], rstd[:, 0:width], newton[:, 0:width]
                link(tt_(t, v, r, ALU.mult))
                link(tt_(t, t, r, ALU.mult))
                link(nc.gpsimd.tensor_scalar(t, t, -0.5, 1.5, ALU.mult, ALU.add))
                if st[0] != "norm":
                    tt_(r, r, t, ALU.mult).then_inc(normed, 1)
                    return
                link(tt_(r, r, t, ALU.mult))
                n = st[1]
                src, dst, _ = norm_io(n)
                if n in RET_NORMS:
                    pool.wait_ge(ret_gated, HEAD_TILES * (n - RET_NORMS[0] + 1))
                else:
                    pool.wait_ge(tile_dve, count_before(READ_BY_DVE, chunk_of_norm(n) + 1))
                if n in FOX_NORMS and n >= 4:
                    pool.wait_ge(sc_done, 8 * (n // 2 - 1))
                if n == MK_NORMS[0]:
                    pool.wait_ge(pv_done, FOX_HEADS + RET_HEADS * HEAD_TILES)
                if n in MQ_NORMS and n > MQ_NORMS[0]:
                    pool.wait_ge(sc_done, TT * (FOX_HEADS + RET_HEADS + n - MQ_NORMS[0]))
                for a, b in zip(src, dst):
                    tt_(b, a, r, ALU.mult).then_inc(normed, 1)

            refine(("x", 0), S)
            for slot in range(last_slot):
                for st in STEPS.get(slot, ()):
                    what, j = st
                    if what == "norm":
                        refine(st, norm_io(j)[2])
                    elif what == "mem_norm":
                        refine(st, M)
                    elif what == "rotary":
                        h, is_q = j // 2, j % 2
                        dst = ret_q if is_q else ret_k
                        pool.wait_ge(tile_act, count_before(READ_BY_ACT, FIRST["rk"] + 6 * h + 2 * is_q + 2))
                        if j == 0:
                            pool.wait_ge(tile_dve, fox_merged)
                            nc.gpsimd.dma_start(cos, dram["cos"]).then_inc(rot_in, 16)
                            nc.gpsimd.dma_start(sin, dram["sin"]).then_inc(rot_in, 16)
                        if not is_q:
                            if h:
                                pool.wait_ge(sc_read, TT * (FOX_HEADS + h))
                            nc.gpsimd.dma_start(decay, dram["decay"][h]).then_inc(decay_in, 16)
                        pool.wait_ge(rot_in, 32)
                        if h:
                            pool.wait_ge(sc_done, TT * (FOX_HEADS + h))
                        a, b = ret_raw[:, 0, :], ret_raw[:, 1, :]
                        link(tt_(dst[:, 0, :], a, cos, ALU.mult))
                        link(tt_(rot, b, sin, ALU.mult))
                        link(tt_(dst[:, 0, :], dst[:, 0, :], rot, ALU.subtract))
                        link(tt_(dst[:, 1, :], b, cos, ALU.mult))
                        link(tt_(rot, a, sin, ALU.mult))
                        tt_(dst[:, 1, :], dst[:, 1, :], rot, ALU.add).then_inc(rotated, 1)

            row = bass.IndirectOffsetOnAxis
            pool.wait_ge(zeroed, 1)
            nc.gpsimd.dma_start(dram["idx"].rearrange("(b s) o -> b (s o)", s=P), zero_i[:]).then_inc(idx_zeroed, 16)
            pool.wait_ge(idx_zeroed, 16)
            pool.wait_ge(tab_in, 16 * 7)
            for a in range(2):
                pool.wait_ge(table_ready, a + 1)
                for tt in range(TT):
                    nc.gpsimd.indirect_dma_start(dram["idx"], row(slots_i[:, a, tt:tt + 1], 0), tokens_i[:, tt:tt + 1],
                                                 None).then_inc(idx_stored, 16)
            pool.wait_ge(idx_stored, 16 * 2 * TT)
            with nc.allow_non_contiguous_dma(reason="a few thousand words"):
                nc.gpsimd.dma_start(rows_i[:], dram["idx"].rearrange("(b s) o -> s (b o)", s=P)).then_inc(idx_loaded, 16)
            pool.wait_ge(idx_loaded, 16)
            pool.wait_ge(h2_stored, 16 * TT)

            def gather_rows(col, n):
                nc.gpsimd.tensor_copy(row_i[:, :], rows_i[:, col]).then_inc(row_copied, 1)
                pool.wait_ge(row_copied, n)
                pool.sem_inc(gathers, 1)
                nc.gpsimd.indirect_dma_start(x_rows, None, dram["h2"], row(row_i[:, 0:1], 0)).then_inc(x_landed, 16)

            gather_rows(slice(0, 1), 1)
            pool.wait_ge(e_lo, BLOCK_CHUNKS)
            n_blocks = pool.value_load(blocks_i[0:1, IDX_COLS:IDX_COLS + 1], min_val=TOP_K * S // P, max_val=MAX_BLOCKS)
            with pool.Fori(0, n_blocks) as b:
                pool.wait_ge(xe_turned, b + 1)
                gather_rows(bass.ds(b + 1, 1), b + 2)
            pool.wait_ge(y_stored, n_blocks * 16 + 32)
            pool.sem_inc(gathers, 1)
            for tt in range(TT):
                if tt >= 2:
                    pool.wait_ge(mixed, tt - 1)
                for a, (rows, landed_) in enumerate(((y_a, ya_in), (y_b, yb_in))):
                    nc.gpsimd.indirect_dma_start(rows[:, tt % 2, :], None, dram["y"],
                                                 row(y_slot_i[:, a, tt:tt + 1], 0)).then_inc(landed_[tt % 2], 16)


def columns_of(w, kind, i):
    if kind in NATURAL:
        g, kp = i // 4, i % 4
        return w[2 * P * kp:2 * P * (kp + 1), 512 * g:512 * (g + 1)].reshape(2, P, 512).transpose(1, 0, 2).reshape(P, 1024)
    return w[:, P * i:P * (i + 1)].reshape(KT, P, P).transpose(1, 0, 2).reshape(P, 1024)


def tables():
    half = P
    inv_freq = (np.float32(10000.0) ** (-np.arange(0, 2 * P, 2, dtype=np.float32) / np.float32(2 * P))).astype(np.float32)
    ang = (np.arange(S, dtype=np.float32)[None, :] * inv_freq[:, None]).astype(np.float32)
    j = np.arange(P)[:, None]
    i = np.arange(S)[None, :]
    decay = []
    for h in range(RET_HEADS):
        lg = np.log1p(-(2.0 ** (-5.0 - h)))
        decay.append(np.where(i >= j, np.exp(lg * np.maximum(i - j, 0)), 0.0) * (2 * P) ** -0.5)
    blocks = (np.arange(P)[:, None] // FOX_DIM == np.arange(P)[None, :] // FOX_DIM) / FOX_DIM
    avg = np.stack([blocks, np.full((P, P), 1.0 / (2 * P)), np.full((P, P), 1.0 / D)], 1)
    mask = np.where(np.arange(P)[None, :] > np.arange(P)[:, None], -NEG, 0.0)
    return {
        "cos": np.cos(ang), "sin": np.sin(ang), "decay": np.stack(decay), "avg": avg,
        "mask": mask, "ident": np.eye(P),
        "order4": np.broadcast_to(np.arange(4)[None, None, :] < np.arange(4)[None, :, None], (P, 4, 4)),
        "iota": np.broadcast_to(np.arange(IDX_COLS), (P, IDX_COLS)),
        "before": np.arange(P)[:, None] < np.arange(P)[None, :], "ones": np.ones((P, P)),
    }


def kernel(**inputs):
    import concourse.bacc as bacc
    from concourse.bass_utils import run_bass_kernel_spmd

    a = {k: np.asarray(v) for k, v in inputs.items()}
    f32 = np.float32
    x, mem = a["x"][0], a["mem"][0]
    w_in = a["w_in"][0]
    names = ("rq", "rk", "rv", "rg", "fq", "fk", "fv", "ff", "mq", "g_ret", "g_fox", "g_mem")
    sizes = [D] * 7 + [FOX_HEADS] + [D] * 4
    at = np.concatenate([[0], np.cumsum(sizes)])
    w = {n: w_in[:, at[i]:at[i + 1]] for i, n in enumerate(names)}
    w["ff"] = np.concatenate([w["ff"], np.zeros((D, P - FOX_HEADS), f32)], 1)
    w["mk"], w["mv"] = a["w_mem_kv"][0][:, :D], a["w_mem_kv"][0][:, D:]
    w["o_ret"], w["o_fox"], w["o_mem"], w["out"] = (a[n][0] for n in ("w_o_ret", "w_o_fox", "w_o_mem", "w_out"))
    stream = np.empty((len(CHUNKS), P, 1024), f32)
    for c, (kind, i) in enumerate(CHUNKS):
        stream[c] = columns_of(w[kind], kind, i)

    def by_tile(v):
        return v.reshape(-1, P).T

    b_ff = np.zeros((P, 1), f32)
    b_ff[:FOX_HEADS, 0] = a["b_forget"][0]
    gains = np.concatenate([
        by_tile(a["norm_mix"][0]), by_tile(a["norm_mem"][0]), by_tile(a["norm_ffn"][0]),
        by_tile(np.concatenate([a["fox_q_norm"][0]] * 2)), by_tile(np.concatenate([a["fox_k_norm"][0]] * 2)),
        by_tile(a["mem_q_norm"][0]), by_tile(a["mem_k_norm"][0]), b_ff, b_ff], 1)
    arrays = {
        "x": x, "xT": x.T.reshape(KT, P, S).transpose(1, 0, 2), "memT": mem.T.reshape(KT, P, M).transpose(1, 0, 2),
        "w": stream, "gains": gains,
    }
    arrays |= {k: v.astype(f32) for k, v in tables().items()}
    experts = np.empty((N_EXPERTS, BLOCK_CHUNKS, P, 1024), f32)
    experts[:, :KT, :, :FF] = a["w_gate"][0].reshape(N_EXPERTS, KT, P, FF)
    experts[:, :KT, :, FF:] = a["w_up"][0].reshape(N_EXPERTS, KT, P, FF)
    experts[:, KT:] = a["w_down"][0].reshape(N_EXPERTS, FT, P, D)
    arrays |= {
        "experts": experts, "router": a["router_w"].reshape(KT, P, N_EXPERTS).transpose(1, 0, 2),
        "bias_b": np.tile(a["router_bias"], (P, TT)), "gain_b": np.tile(a["norm_ffn"][0], (P, 1)),
        "tokens": (np.arange(TT)[None, :] * P + np.arange(P)[:, None]).astype(np.int32),
    }
    nc = bacc.Bacc("TRN2", target_bir_lowering=False, num_devices=1)
    sent, dram = {}, {}
    for name, v in arrays.items():
        v = np.ascontiguousarray(v)
        sent[f"in_{name}"] = v
        dram[name] = nc.dram_tensor(f"in_{name}", v.shape, mybir.dt.from_np(v.dtype), kind="ExternalInput").ap()
    dram["out"] = nc.dram_tensor("out_x", (S, D), F32, kind="ExternalOutput").ap()
    dram["h2"] = nc.dram_tensor("h2", (S, D), F32, kind="Internal").ap()
    dram["idx"] = nc.dram_tensor("idx", (IDX_COLS * P, 1), I32, kind="Internal").ap()
    dram["y"] = nc.dram_tensor("y", ((MAX_BLOCKS + 1) * P, D), F32, kind="Internal").ap()
    mixing_and_experts(nc, dram)
    r = run_bass_kernel_spmd(nc, [sent], core_ids=[0])
    return r.results[0]["out_x"].reshape(1, S, D)
```

```python
from contextlib import ExitStack

import numpy as np

import concourse.bass as bass
from concourse import mybir

F32 = mybir.dt.float32
F32R = mybir.dt.float32r
I32 = mybir.dt.int32
U32 = mybir.dt.uint32
ALU = mybir.AluOpType
ACT = mybir.ActivationFunctionType
AX = mybir.AxisListType

P = 128
D = 1024
S = 512
M = 256
KT = D // P
TT = S // P
MT = M // P
EPS = 1e-6
RET_HEADS, FOX_HEADS, MEM_HEADS = 4, 16, 4
PAIRS = FOX_HEADS // 2
FOX_DIM = D // FOX_HEADS
HEAD_TILES = 2
N_EXPERTS, N_GROUPS, PER_GROUP, FF = 16, 4, 4, 512
TOP_K = 2
MAX_BLOCKS = N_EXPERTS + TOP_K * S // P - 1
BLOCK_CHUNKS = KT + FF // P
NEG = -1.0e30

RAW, SPLIT = 6, 3
E_SPLIT = 4
FT = FF // P
IDX_COLS = MAX_BLOCKS + 1
AHEAD = 2


def chunk_list():
    out = [("fv", i) for i in range(8)] + [("ff", 0)]
    for p in range(PAIRS):
        out += [("fq", p), ("fk", p)]
    out += [("g_fox", n) for n in range(KT)] + [("o_fox", n) for n in range(KT)]
    out += [("rv", i) for i in range(8)]
    for h in range(RET_HEADS):
        out += [(k, HEAD_TILES * h + t) for k in ("rk", "rq", "rg") for t in range(HEAD_TILES)]
    out += [("g_ret", n) for n in range(KT)] + [("o_ret", n) for n in range(KT)]
    out += [("mk", n) for n in range(KT)] + [("mv", i) for i in range(8)]
    out += [("mq", n) for n in range(KT)]
    out += [("g_mem", n) for n in range(KT)] + [("o_mem", n) for n in range(KT)]
    out += [("out", i) for i in range(8)]
    return out


CHUNKS = chunk_list()
NATURAL = ("fv", "rv", "mv", "out")
FIRST = {}
for _c, (_kind, _i) in enumerate(CHUNKS):
    FIRST.setdefault(_kind, _c)


def schedule():
    steps = {}

    def put(slot, *step):
        steps.setdefault(slot, []).append(step)

    base = 4 * FIRST["fq"]
    for p in range(PAIRS):
        put(base + 8 * p + 5, "norm", 2 * p)
        put(base + 8 * p + 9, "norm", 2 * p + 1)
        for half in range(2):
            put(base + 8 * p + 12 + 4 * half, "forget", 2 * p + half)
            put(base + 8 * p + 20 + 4 * half, "fox_pv", 2 * p + half)
        for j in range(8):
            put(base + 8 * p + 14 + j, "fox_score", 8 * p + j)
            put(base + 8 * p + 15 + j, "fox_scale", 8 * p + j)
            put(base + 8 * p + 16 + j, "fox_turn", 8 * p + j)
    base = 4 * FIRST["rk"]
    for h in range(RET_HEADS):
        b = base + 24 * h
        put(b + 9, "rotary", 2 * h)
        put(b + 17, "rotary", 2 * h + 1)
        for j in range(TT):
            put(b + 22 + 2 * j, "ret_score", TT * h + j)
        for e in range(HEAD_TILES):
            put(b + 30 + 2 * e, "ret_pv", HEAD_TILES * h + e)
        put(b + 34, "norm", 16 + h)
        put(b + 39, "ret_out", h)
    base = 4 * FIRST["o_ret"]
    put(base + 2, "mem_load", 0)
    put(base + 12, "mem_norm", 0)
    put(4 * FIRST["mk"] - 1, "mem_split", 0)
    base = 4 * FIRST["mk"]
    for h in range(MEM_HEADS):
        put(base + 8 * h + 9, "norm", 20 + h)
    base = 4 * FIRST["mq"]
    for h in range(MEM_HEADS):
        b = base + 8 * h
        put(b + 9, "norm", 24 + h)
        for j in range(TT):
            put(b + 14 + j, "mem_score", TT * h + j)
            put(b + 15 + j, "mem_scale", TT * h + j)
            put(b + 16 + j, "mem_turn", TT * h + j)
        for e in range(HEAD_TILES):
            put(b + 20 + e, "mem_pv", HEAD_TILES * h + e)
    base = 4 * (FIRST["out"] + 4)
    for tt in range(TT):
        put(base + 4 + 2 * tt, "row_turn", tt)
        put(base + 6 + 2 * tt, "row_logit", tt)
    order = ("rotary", "norm", "forget", "fox_score", "mem_score", "ret_score", "fox_scale", "mem_scale",
             "fox_turn", "mem_turn", "fox_pv", "mem_pv", "ret_pv", "row_logit", "row_turn")
    for slot in steps:
        steps[slot].sort(key=lambda s: order.index(s[0]) if s[0] in order else 99)
    return steps


STEPS = schedule()
RET_AT = [sum(S - m * P for m in range(k)) for k in range(TT)]
FOX_NORMS, RET_NORMS, MK_NORMS, MQ_NORMS = range(0, 16), range(16, 20), range(20, 24), range(24, 28)


def norm_tiles(n):
    return 1 if n in FOX_NORMS else HEAD_TILES


def count_before(kinds, chunk):
    return sum(CHUNKS[c][0] in kinds for c in range(chunk))


def mixing_and_experts(nc, dram):
    assert D == 1024 and S == 512 and M == 256
    ctx = ExitStack()
    with ctx:
        def sb(name, shape, dt=F32):
            return ctx.enter_context(nc.sbuf_tensor(name, shape, dt))

        def sem(name):
            return ctx.enter_context(nc.semaphore(name))

        ps = ctx.enter_context(nc.psum_tensor("ps", [P, 8, 512], F32))
        STAT, SCORE, TURN, PV = 2, 3, 5, 7

        h_split = sb("h_split", [P, 2, KT, S], F32R)
        w_split = sb("w_split", [P, 2, SPLIT, 1024], F32R)
        o_split = sb("o_split", [P, 2, KT, S], F32R)
        id_r = sb("id_r", [P, P], F32R)
        mask_r = sb("mask_r", [P, P], F32R)
        mem_split = o_split[:].rearrange("p a k s -> p (a k s)")[:, 0:2 * KT * M].rearrange(
            "p (a k s) -> p a k s", a=2, k=KT)
        big = sb("big", [P, RAW * 1024 + 3 * 4096])
        raw = big[:, 0:RAW * 1024].rearrange("p (r n) -> p r n", r=RAW)
        fvm = big[:, RAW * 1024:RAW * 1024 + 4096]
        gat = big[:, RAW * 1024 + 4096:RAW * 1024 + 8192]
        vreg = big[:, RAW * 1024 + 8192:RAW * 1024 + 12288]
        fv = fvm.rearrange("p (t n) -> p t n", t=TT)
        merged = fvm.rearrange("p (k s) -> p k s", k=KT)
        gate = gat.rearrange("p (k s) -> p k s", k=KT)
        xT = gate
        x_nat = gat.rearrange("p (t n) -> p t n", t=TT)
        fox_pt = vreg.rearrange("p (b j i) -> p b j i", b=2, j=TT)
        x1 = vreg.rearrange("p (t n) -> p t n", t=TT)
        rv = vreg.rearrange("p (t n) -> p t n", t=TT)
        mkT = vreg[:, 0:KT * M].rearrange("p (k m) -> p k m", k=KT)
        memT = vreg[:, KT * M:2 * KT * M].rearrange("p (k m) -> p k m", k=KT)
        mv = vreg[:, KT * M:2 * KT * M].rearrange("p (t n) -> p t n", t=MT)
        work = sb("work", [P, 9984])
        used = [0]

        def carve(words):
            used[0] += words
            return work[:, used[0] - words:used[0]]

        sq = carve(1024).rearrange("p (b s) -> p b s", b=2)
        var, rstd, newton = carve(512), carve(512), carve(512)
        common = used[0]
        fox_raw = carve(1024).rearrange("p (b s) -> p b s", b=2)
        fox_q = carve(1024).rearrange("p (b s) -> p b s", b=2)
        fox_k = carve(1024).rearrange("p (b s) -> p b s", b=2)
        logits = carve(1024).rearrange("p (b s) -> p b s", b=2)
        prob = carve(1024).rearrange("p (b s) -> p b s", b=2)
        forget = carve(1024).rearrange("p (b s) -> p b s", b=2)
        used[0] = common
        ret_raw = carve(1024).rearrange("p (b s) -> p b s", b=2)
        ret_k = carve(1024).rearrange("p (b s) -> p b s", b=2)
        ret_q = carve(1024).rearrange("p (b s) -> p b s", b=2)
        ret_o = carve(1024).rearrange("p (b s) -> p b s", b=2)
        ret_p = carve(1280)
        rot = carve(512)
        cos = carve(512)
        sin = carve(512)
        decay = carve(512)
        used[0] = common
        mem_raw = carve(1024).rearrange("p (b s) -> p b s", b=2)
        mem_q = carve(1024).rearrange("p (b s) -> p b s", b=2)
        mem_p = carve(512).rearrange("p (b m) -> p b m", b=2)
        mem_pt = carve(1024).rearrange("p (j i) -> p j i", j=MT)
        ident = sb("ident", [P, P])
        mask_f = sb("mask_f", [P, P])
        avg = sb("avg", [P, 3, P])
        gains = sb("gains", [P, 3 * KT + 8])
        cst = sb("cst", [P, 4])
        stat = sb("stat", [P, 16])
        cum = sb("cum", [FOX_HEADS, S])
        G_MIX, G_MEM, G_FFN, G_FQ, G_FK, G_MQ, G_MK = 0, KT, 2 * KT, 3 * KT, 3 * KT + 1, 3 * KT + 2, 3 * KT + 4
        B_FF = 3 * KT + 6

        ew_split = h_split[:].rearrange("p a k s -> p (a k s)").rearrange("p (a r n) -> p a r n", a=2, r=E_SPLIT)
        o_flat = o_split[:].rearrange("p a k s -> p (a k s)")
        xe_split = o_flat[:, 0:2 * KT * P].rearrange("p (a k s) -> p a k s", a=2, k=KT)
        he_split = o_flat[:, 2 * KT * P:2 * (KT + FT) * P].rearrange("p (a f s) -> p a f s", a=2, f=FT)
        e_raw = [big[:, (k - FT) % BLOCK_CHUNKS * 1024:((k - FT) % BLOCK_CHUNKS + 1) * 1024] for k in range(BLOCK_CHUNKS)]
        y_a = big[:, 0:2048].rearrange("p (b n) -> p b n", b=2)
        y_b = big[:, 2048:4096].rearrange("p (b n) -> p b n", b=2)
        h2 = fvm.rearrange("p (t n) -> p t n", t=TT)
        lane_hot = o_flat[:, 0:2 * TT * P].rearrange("p (j s) -> p j s", s=P)
        block_ids = o_flat[:, 1024:1024 + 2 * TT * IDX_COLS].rearrange("p (j b) -> p j b", b=IDX_COLS)
        before_r, ones_r = o_flat[:, 3072:3072 + P], o_flat[:, 3072 + P:3072 + 2 * P]
        sel_r = o_flat[:, 3072 + 2 * P:3072 + 2 * P + TT * N_EXPERTS]
        used[0] = 0
        gain_b = carve(1024)
        scratch = carve(1024)
        xgT = carve(2048).rearrange("p (k s) -> p k s", s=S)
        used[0] -= 2048
        x_rows = carve(1024)
        h_act, h_e = carve(512), carve(512)
        y_rows = carve(1024)
        router = carve(KT * N_EXPERTS).rearrange("p (k e) -> p k e", k=KT)
        order4 = carve(16).rearrange("p (b a) -> p b a", b=4)
        iota = carve(IDX_COLS)
        bias_b = carve(TT * N_EXPERTS)
        before, ones = carve(P), carve(P)
        lanes, block_at = carve(P), carve(IDX_COLS)
        token_f = carve(2 * TT)
        sums = carve(6 * TT).rearrange("p (a t) -> p a t", a=6)
        r64 = [carve(TT * N_EXPERTS) for _ in range(10)]
        r256a, r256b = carve(256), carve(256)
        r384 = carve(IDX_COLS * N_EXPERTS)
        r16 = [carve(16) for _ in range(12)]
        token_w = carve(2 * TT).rearrange("p (a t) -> p a t", a=2)
        assert used[0] <= 9984
        y_slot_i = sb("y_slot_i", [P, 2, TT], I32)
        blocks_i = sb("blocks_i", [P, IDX_COLS + 1], I32)
        rows_i = sb("rows_i", [P, IDX_COLS], I32)
        row_i = sb("row_i", [P, 1], I32)

        consts_in, mem_in, xn_in = sem("consts_in"), sem("mem_in"), sem("xn_in")
        x_in = [sem(f"x_in{k}") for k in range(4)]
        rot_in, decay_in = sem("rot_in"), sem("decay_in")
        landed = [sem(f"landed{i}") for i in range(RAW)]
        hi_ready, lo_ready = sem("hi_ready"), sem("lo_ready")
        w_used = sem("w_used")
        tile_act, tile_dve = sem("tile_act"), sem("tile_dve")
        nat_read = sem("nat_read")
        x_sq, x_sum = sem("x_sq"), sem("x_sum")
        sq_ready = sem("sq_ready")
        stat_ready, stat_read = sem("stat_ready"), sem("stat_read")
        seed_ready, normed = sem("seed_ready"), sem("normed")
        h_f, h_hi, h_lo = sem("h_f"), sem("h_hi"), sem("h_lo")
        gate_log, cum_ready = sem("gate_log"), sem("cum_ready")
        sc_done, sc_read = sem("sc_done"), sem("sc_read")
        mem_min = sem("mem_min")
        prob_ready, prob_scaled = sem("prob_ready"), sem("prob_scaled")
        turned, turn_read = sem("turned"), sem("turn_read")
        pv_done = sem("pv_done")
        o_hi, o_lo = sem("o_hi"), sem("o_lo")
        rotated = sem("rotated")
        ret_silu, ret_sq, ret_gated = sem("ret_silu"), sem("ret_sq"), sem("ret_gated")
        merge_done = sem("merge_done")
        m_hi, m_lo = sem("m_hi"), sem("m_lo")
        x1_ready = sem("x1_ready")
        route_in, tab_in, gain_in = sem("route_in"), sem("tab_in"), sem("gain_in")
        row_sq, row_sum, row_seed, row_rstd = sem("row_sq"), sem("row_sum"), sem("row_seed"), sem("row_rstd")
        xg_ready, xg_turned, xg_copied = sem("xg_ready"), sem("xg_turned"), sem("xg_copied")
        h2_ready, h2_stored = sem("h2_ready"), sem("h2_stored")
        logit_done, logit_ready, score_ready = sem("logit_done"), sem("logit_ready"), sem("score_ready")
        tab_r, sel_ready, pos_done = sem("tab_r"), sem("sel_ready"), sem("pos_done")
        hot_ready, rows_done, rows_ready = sem("hot_ready"), sem("rows_done"), sem("rows_ready")
        table_ready = sem("table_ready")
        e_landed = [sem(f"e_landed{k}") for k in range(BLOCK_CHUNKS)]
        e_hi = sem("e_hi")
        e_lo = sem("e_lo")
        e_used = sem("e_used")
        row_copied, x_landed = sem("row_copied"), sem("x_landed")
        xe_turned, xe_hi, xe_lo = sem("xe_turned"), sem("xe_hi"), sem("xe_lo")
        silu_done, he_ready, he_turned, he_hi, he_lo = (
            sem("silu_done"), sem("he_ready"), sem("he_turned"), sem("he_hi"), sem("he_lo"))
        y_act, y_dve = sem("y_act"), sem("y_dve")
        y_stored = sem("y_stored")
        y_filled = sem("y_filled")
        ya_in, yb_in = [sem(f"ya_in{b}") for b in range(2)], [sem(f"yb_in{b}") for b in range(2)]
        gathers = sem("gathers")
        mixed, token_out = sem("mixed"), sem("token_out")
        cum_zero, id_ready = sem("cum_zero"), sem("id_ready")
        act_chain, dve_chain, pool_chain = sem("act_chain"), sem("dve_chain"), sem("pool_chain")
        out_done = sem("out_done")

        READ_BY_ACT = ("rk", "rq", "rg", "g_fox", "g_ret", "g_mem", "ff")
        READ_BY_DVE = ("fq", "fk", "mq", "mk", "o_fox", "o_ret", "o_mem")
        tiles = [c for c, (kind, _) in enumerate(CHUNKS) if kind not in NATURAL]
        tile_no = {c: i for i, c in enumerate(tiles)}
        fox_merged = count_before(READ_BY_DVE, FIRST["o_fox"] + KT)
        steps = [st for s in sorted(STEPS) for st in STEPS[s]]

        def numbers(names):
            return {st: i for i, st in enumerate(x for x in steps if x[0] in names)}

        stat_no = {st: i + 1 for st, i in numbers(("norm", "forget", "mem_norm")).items()}
        stat_no[("x", 0)] = 0
        sum_no = numbers(("norm", "forget"))
        norm_order = [("x", 0)] + [st for st in steps if st[0] in ("norm", "mem_norm")]
        norm_no = {st: i for i, st in enumerate(norm_order)}
        normed_by = {}
        for st in norm_order:
            normed_by[st] = (norm_tiles(st[1]) if st[0] == "norm" else 1) + (
                normed_by[norm_order[norm_no[st] - 1]] if norm_no[st] else 0)
        sc_no = numbers(("fox_score", "ret_score", "mem_score"))
        soft = {("fox", j): j for j in range(FOX_HEADS * TT)}
        soft |= {("mem", j): FOX_HEADS * TT + j for j in range(MEM_HEADS * TT)}
        sq_before = {n: sum(norm_tiles(m) for m in range(n)) for n in range(MQ_NORMS[-1] + 2)}
        last_slot = 4 * len(CHUNKS)
        assert max(STEPS) < last_slot

        def lhs_of(kind):
            return {"mk": mem_split, "mv": mem_split, "o_fox": o_split, "o_ret": o_split,
                    "o_mem": o_split}.get(kind, h_split)

        def norm_io(n):
            if n in FOX_NORMS:
                p = n // 2
                return [fox_raw[:, n % 2, :]], [(fox_q if n % 2 == 0 else fox_k)[:, p % 2, :]], S
            if n in RET_NORMS:
                return [ret_o[:, e, :] for e in range(2)], [ret_o[:, e, :] for e in range(2)], S
            if n in MK_NORMS:
                h = n - MK_NORMS[0]
                return ([mem_raw[:, e, 0:M] for e in range(2)],
                        [mkT[:, HEAD_TILES * h + e, :] for e in range(2)], M)
            return [mem_raw[:, e, :] for e in range(2)], [mem_q[:, e, :] for e in range(2)], S

        def norm_of_chunk(kind, i):
            if kind in ("fq", "fk"):
                return 2 * i + (kind == "fk"), 0
            return (MK_NORMS if kind == "mk" else MQ_NORMS)[i // 2], i % 2

        def chunk_of_norm(n):
            if n in FOX_NORMS:
                return FIRST["fq"] + n
            return (FIRST["mk"] - HEAD_TILES * MK_NORMS[0] if n in MK_NORMS else FIRST["mq"] - HEAD_TILES * MQ_NORMS[0]
                    ) + HEAD_TILES * n + 1

        def squares_by(n, e):
            return sq_before[n] + e + 1 - (HEAD_TILES * RET_HEADS if n > RET_NORMS[-1] else 0)

        def landed_by(b, k):
            return b * 16 + (16 if k >= FT else 0)

        block = ctx.enter_context(nc.Block())

        @block.sync
        def _(sp):
            for k in range(4):
                sp.dma_start(xT[:, 2 * k:2 * k + 2, :], dram["xT"][:, 2 * k:2 * k + 2, :]).then_inc(x_in[k], 16)
                if k == 0:
                    for dst, name in ((gains, "gains"), (avg, "avg"), (ident, "ident"), (mask_f, "mask")):
                        sp.dma_start(dst[:], dram[name]).then_inc(consts_in, 16)
            for c in range(len(CHUNKS)):
                if c >= RAW:
                    sp.wait_ge(lo_ready, c - RAW + 1)
                sp.dma_start(raw[:, c % RAW, :], dram["w"][c]).then_inc(landed[c % RAW], 16)
                kind, i = CHUNKS[c]
                if kind == "ff":
                    first = (TOP_K * S // P + 1) * P
                    sp.dma_start(dram["y"][first:, :].rearrange("(b p) n -> b p n", p=P),
                                 dram["w"][0:MAX_BLOCKS - TOP_K * S // P]).then_inc(y_filled, 16)
                if kind == "o_ret" and i == 1:
                    sp.wait_ge(pv_done, FOX_HEADS + RET_HEADS * HEAD_TILES)
                    sp.dma_start(memT, dram["memT"]).then_inc(mem_in, 16)
                if kind == "out" and i == 5:
                    sp.wait_ge(merge_done, 2 * KT)
                    sp.dma_start(x_nat, dram["x"].rearrange("(t p) n -> p t n", p=P)).then_inc(xn_in, 16)
            sp.wait_ge(o_lo, 3 * KT)
            for dst, name in ((router, "router"), (order4, "order4"), (iota, "iota"), (bias_b, "bias_b"),
                              (before, "before"), (ones, "ones"), (lanes, "lanes"), (block_at, "block_at"),
                              (token_f, "tokens"), (gain_b, "gain_b")):
                sp.dma_start(dst, dram[name]).then_inc(tab_in, 16)
            sp.wait_ge(lo_ready, len(CHUNKS))
            for k in range(RAW):
                sp.dma_start(e_raw[FT + k], dram["experts"][0, k]).then_inc(e_landed[FT + k], 16)
            for tt in range(TT):
                sp.wait_ge(h2_ready, tt + 1)
                sp.dma_start(dram["h2"][tt * P:(tt + 1) * P, :], h2[:, tt, :]).then_inc(h2_stored, 16)
            sp.wait_ge(h2_stored, 16 * TT)
            for k in range(RAW, KT):
                sp.dma_start(e_raw[FT + k], dram["experts"][0, k]).then_inc(e_landed[FT + k], 16)
            sp.wait_ge(e_lo, FT)
            turns = sp.value_load(blocks_i[0:1, IDX_COLS:IDX_COLS + 1], min_val=TOP_K * S // P - 1, max_val=MAX_BLOCKS - 1)
            n_blocks = turns + 1
            with sp.Fori(0, turns) as turn:
                b = turn + 1
                expert = sp.value_load(blocks_i[0:1, bass.ds(b, 1)], min_val=0, max_val=N_EXPERTS - 1)
                last_expert = sp.value_load(blocks_i[0:1, bass.ds(turn, 1)], min_val=0, max_val=N_EXPERTS - 1)
                for k in range(BLOCK_CHUNKS):
                    sp.wait_ge(e_lo, turn * BLOCK_CHUNKS + (k + 1))
                    sp.dma_start(e_raw[k], dram["experts"][expert if k < KT else last_expert, k]).then_inc(e_landed[k], 16)
            last_expert = sp.value_load(blocks_i[0:1, bass.ds(turns, 1)], min_val=0, max_val=N_EXPERTS - 1)
            for k in range(FT):
                sp.wait_ge(e_lo, turns * BLOCK_CHUNKS + (k + 1))
                sp.dma_start(e_raw[k], dram["experts"][last_expert, KT + k]).then_inc(e_landed[k], 16)
            for tt in range(TT):
                sp.wait_ge(mixed, tt + 1)
                sp.dma_start(dram["out"][tt * P:(tt + 1) * P, :], x1[:, tt, :]).then_inc(out_done, 16)
            sp.wait_ge(out_done, 16 * TT)

        @block.tensor
        def _(pe):
            mm = nc.tensor.matmul

            def before_chunk(c):
                kind, i = CHUNKS[c]
                pe.wait_ge(lo_ready, c + 1)
                if kind in NATURAL:
                    if kind == "fv" and i == 0:
                        pe.wait_ge(stat_read, 1)
                    if kind == "fv" and i < 4:
                        pe.wait_ge(h_lo, 2 * i + 2)
                    if kind == "rv" and i == 0:
                        pe.wait_ge(tile_dve, count_before(READ_BY_DVE, c))
                    if kind == "mv" and i == 0:
                        pe.wait_ge(sc_read, FOX_HEADS * TT + RET_HEADS * TT)
                        pe.wait_ge(ret_sq, RET_HEADS * HEAD_TILES)
                        pe.wait_ge(ret_gated, RET_HEADS * HEAD_TILES)
                    if kind == "out" and i == 0:
                        pe.wait_ge(tile_dve, count_before(READ_BY_DVE, c))
                        pe.wait_ge(m_lo, KT)
                    return
                t = tile_no[c]
                if t >= 2:
                    a, d = (count_before(k, tiles[t - 2] + 1) for k in (READ_BY_ACT, READ_BY_DVE))
                    if a:
                        pe.wait_ge(tile_act, a)
                    if d:
                        pe.wait_ge(tile_dve, d)
                if kind == "ff":
                    pe.wait_ge(nat_read, 8)
                if kind == "rk" and i == 0:
                    pe.wait_ge(nat_read, 16)
                if kind == "mk" and i == 0:
                    pe.wait_ge(h_lo, 2 * KT)
                if kind in ("o_fox", "o_ret", "o_mem") and i == 0:
                    pe.wait_ge(o_lo, KT * (1 + ("o_fox", "o_ret", "o_mem").index(kind)))

            def quarter(c, q):
                kind, i = CHUNKS[c]
                x = lhs_of(kind)
                whi, wlo = w_split[:, 0, c % SPLIT, :], w_split[:, 1, c % SPLIT, :]
                if q == 0:
                    before_chunk(c)
                if kind in NATURAL:
                    g, kp, kk, half = i // 4, i % 4, q // 2, q % 2
                    rows = MT if kind == "mv" else TT
                    for tt in range(half * rows // 2, (half + 1) * rows // 2):
                        bank = SCORE + 2 * g + tt if kind == "mv" else 4 * g + tt
                        for n, (a, w) in enumerate(((0, whi), (0, wlo), (1, whi))):
                            last = mm(ps[:, bank, :], x[:, a, 2 * kp + kk, tt * P:(tt + 1) * P],
                                      w[:, kk * 512:(kk + 1) * 512],
                                      start=(kp == 0 and kk == 0 and n == 0), stop=(kp == 3 and kk == 1 and n == 2))
                else:
                    out = ps[:, tile_no[c] % 2, 0:M if kind == "mk" else S]
                    for k in (2 * q, 2 * q + 1):
                        for n, (w, a) in enumerate(((whi, 0), (wlo, 0), (whi, 1))):
                            last = mm(out, w[:, k * P:(k + 1) * P], x[:, a, k, :],
                                      start=(k == 0 and n == 0), stop=(k == KT - 1 and n == 2))
                if q == 3:
                    last.then_inc(w_used, 1)

            def sum_squares_of_input(width, before):
                for k in range(KT):
                    pe.wait_ge(x_sq, before + k + 1)
                    mm(ps[:, STAT, 0:width], avg[:, 2, :], sq[:, k % 2, 0:width],
                       start=(k == 0), stop=(k == KT - 1)).then_inc(x_sum, 1)

            def row_turn(g, tt):
                n = g * TT + tt
                pe.wait_ge(x1_ready, TT)
                pe.wait_ge(xg_ready, n + 1)
                if n >= 3:
                    pe.wait_ge(xg_copied, n - 2)
                for k in range(4):
                    last = nc.tensor.transpose(ps[:, n % 3, k * P:(k + 1) * P], h2[:, tt, (4 * g + k) * P:(4 * g + k + 1) * P],
                                               ident[:])
                last.then_inc(xg_turned, 1)

            def row_logit(g, tt):
                n = g * TT + tt
                pe.wait_ge(xg_copied, n + 1)
                pe.wait_ge(tab_in, 16 * 10)
                for k in range(4):
                    last = mm(ps[:, 3, n * N_EXPERTS:(n + 1) * N_EXPERTS], xgT[:, k, tt * P:(tt + 1) * P],
                              router[:, 4 * g + k, :], start=(k == 0), stop=(k == 3))
                last.then_inc(logit_done, 1)

            pe.wait_ge(consts_in, 16 * 4)
            sum_squares_of_input(S, 0)
            pe.wait_ge(id_ready, 2)
            for slot in range(last_slot):
                quarter(slot // 4, slot % 4)
                for st in STEPS.get(slot, ()):
                    what, j = st
                    if what == "row_turn":
                        row_turn(0, j)
                    elif what == "row_logit":
                        row_logit(0, j)
                    elif what == "mem_norm":
                        pe.wait_ge(stat_read, stat_no[st])
                        sum_squares_of_input(M, KT)
                    elif what == "norm":
                        width, t = norm_io(j)[2], norm_tiles(j)
                        pe.wait_ge(stat_read, stat_no[st])
                        if j in RET_NORMS:
                            pe.wait_ge(ret_sq, HEAD_TILES * (j - RET_NORMS[0] + 1))
                        else:
                            pe.wait_ge(sq_ready, squares_by(j, t - 1))
                        for e in range(t):
                            last = mm(ps[:, STAT, 0:width], avg[:, 0 if j in FOX_NORMS else 1, :],
                                      sq[:, j % 2 if j in FOX_NORMS else e, 0:width], start=(e == 0), stop=(e == t - 1))
                        last.then_inc(stat_ready, 1)
                    elif what == "forget":
                        pe.wait_ge(stat_read, stat_no[st])
                        pe.wait_ge(cum_ready, 1)
                        mm(ps[:, STAT, :], ident[0:FOX_HEADS, j:j + 1].to_broadcast([FOX_HEADS, P]), cum[:, :],
                           start=True, stop=True).then_inc(stat_ready, 1)
                    elif what == "fox_score":
                        head, r = j // TT, j % TT
                        pair, rows = head // 2, slice(FOX_DIM * (head % 2), FOX_DIM * (head % 2) + FOX_DIM)
                        if j >= 2:
                            pe.wait_ge(sc_read, j - 1)
                        pe.wait_ge(normed, normed_by[("norm", 2 * pair + 1)])
                        out = ps[:, SCORE + j % 2, 0:P * (r + 1)]
                        mm(out, fox_q[rows, pair % 2, r * P:(r + 1) * P], fox_k[rows, pair % 2, 0:P * (r + 1)],
                           start=True, stop=True)
                        mm(out[:, P * r:], id_r[:], mask_r[:], start=False, stop=True,
                           skip_group_check=True).then_inc(sc_done, 1)
                    elif what == "fox_turn":
                        r = j % TT
                        if j >= 2:
                            pe.wait_ge(turn_read, j - 1)
                        pe.wait_ge(prob_scaled, j + 1)
                        for k in range(r + 1):
                            last = nc.tensor.transpose(ps[:, TURN + j % 2, k * P:(k + 1) * P],
                                                       prob[:, j % 2, k * P:(k + 1) * P], ident[:])
                        last.then_inc(turned, 1)
                    elif what == "fox_pv":
                        rows = slice(FOX_DIM * (j % 2), FOX_DIM * (j % 2) + FOX_DIM)
                        if j >= 2 and j % 2 == 0:
                            pe.wait_ge(o_lo, j // 2)
                        pe.wait_ge(turn_read, TT * (j + 1))
                        for k in reversed(range(TT)):
                            last = mm(ps[rows, PV, k * P:], fv[:, k, j * FOX_DIM:(j + 1) * FOX_DIM],
                                      fox_pt[:, j % 2, k, k * P:], start=(k == TT - 1), stop=(k == 0),
                                      skip_group_check=True)
                        last.then_inc(pv_done, 1)
                    elif what == "ret_score":
                        h, k = j // TT, j % TT
                        n = sc_no[st]
                        pe.wait_ge(sc_read, n - 1)
                        pe.wait_ge(rotated, 2 * h + 2)
                        for e in range(HEAD_TILES):
                            last = mm(ps[:, SCORE + n % 2, 0:S - k * P], ret_k[:, e, k * P:(k + 1) * P],
                                      ret_q[:, e, k * P:], start=(e == 0), stop=(e == HEAD_TILES - 1))
                        last.then_inc(sc_done, 1)
                    elif what == "ret_pv":
                        h, e = j // 2, j % 2
                        if h == 0:
                            pe.wait_ge(o_lo, KT)
                            pe.wait_ge(turn_read, FOX_HEADS * TT)
                        else:
                            pe.wait_ge(ret_sq, j - 1)
                            pe.wait_ge(ret_gated, j - 1)
                        pe.wait_ge(sc_read, FOX_HEADS * TT + TT * (h + 1))
                        for k in reversed(range(TT)):
                            last = mm(ps[:, PV if e == 0 else TURN, k * P:], rv[:, k, j * P:(j + 1) * P],
                                      ret_p[:, RET_AT[k]:RET_AT[k] + S - k * P],
                                      start=(k == TT - 1), stop=(k == 0), skip_group_check=True)
                        last.then_inc(pv_done, 1)
                    elif what == "mem_score":
                        h, r = j // TT, j % TT
                        n = sc_no[st]
                        pe.wait_ge(sc_read, n - 1)
                        if j == 0:
                            pe.wait_ge(nat_read, 20)
                        pe.wait_ge(normed, normed_by[("norm", MQ_NORMS[h])])
                        for e in range(HEAD_TILES):
                            last = mm(ps[:, SCORE + n % 2, 0:M], mem_q[:, e, r * P:(r + 1) * P],
                                      mkT[:, HEAD_TILES * h + e, :], start=(e == 0), stop=(e == HEAD_TILES - 1))
                        last.then_inc(sc_done, 1)
                    elif what == "mem_turn":
                        n = soft["mem", j]
                        pe.wait_ge(turn_read, n - 1)
                        pe.wait_ge(prob_scaled, n + 1)
                        for k in range(MT):
                            last = nc.tensor.transpose(ps[:, TURN + n % 2, k * P:(k + 1) * P],
                                                       mem_p[:, n % 2, k * P:(k + 1) * P], ident[:])
                        last.then_inc(turned, 1)
                    elif what == "mem_pv":
                        pe.wait_ge(o_lo, 2 * KT + j)
                        pe.wait_ge(turn_read, FOX_HEADS * TT + TT * (j // 2 + 1))
                        for k in range(MT):
                            last = mm(ps[:, PV, :], mv[:, k, j * P:(j + 1) * P], mem_pt[:, k, :],
                                      start=(k == 0), stop=(k == MT - 1))
                        last.then_inc(pv_done, 1)

            for tt in range(TT):
                row_turn(1, tt)
                if tt:
                    row_logit(1, tt - 1)
            row_logit(1, TT - 1)
            pe.wait_ge(tab_r, 2)
            pe.wait_ge(sel_ready, 1)
            for tt in range(TT):
                for m in range(tt + 1):
                    mm(ps[:, 5, tt * N_EXPERTS:(tt + 1) * N_EXPERTS], before_r if m == tt else ones_r,
                       sel_r[:, m * N_EXPERTS:(m + 1) * N_EXPERTS], start=(m == 0), stop=(m == tt))
            for m in range(TT):
                last = mm(ps[:, 6, 0:N_EXPERTS], ones_r, sel_r[:, m * N_EXPERTS:(m + 1) * N_EXPERTS],
                          start=(m == 0), stop=(m == TT - 1))
            last.then_inc(pos_done, 1)
            for j in range(2 * TT):
                pe.wait_ge(hot_ready, j + 1)
                last = mm(ps[:, 4, 0:IDX_COLS], lane_hot[:, j, :], block_ids[:, j, :], start=(j == 0), stop=(j == 2 * TT - 1))
            last.then_inc(rows_done, 1)

            def turn_rows():
                for k in range(KT):
                    last = nc.tensor.transpose(ps[:, 2 + k // 4, k % 4 * P:(k % 4 + 1) * P],
                                               x_rows[:, k * P:(k + 1) * P], ident[:])
                last.then_inc(xe_turned, 1)

            pe.wait_ge(x_landed, 16)
            pe.wait_ge(e_lo, FT)
            turn_rows()
            turns = pe.value_load(blocks_i[0:1, IDX_COLS:IDX_COLS + 1], min_val=TOP_K * S // P - 1, max_val=MAX_BLOCKS - 1)
            n_blocks = turns + 1

            def use_chunk(at, slot, x, kk, depth, first_bank):
                pe.wait_ge(e_lo, at + (slot + 1))
                whi, wlo = ew_split[:, 0, slot % E_SPLIT, :], ew_split[:, 1, slot % E_SPLIT, :]
                for n, (a, w) in enumerate(((0, whi), (0, wlo), (1, whi))):
                    for half in range(2):
                        last = mm(ps[:, first_bank + half, :], x[:, a, kk, :], w[:, half * 512:(half + 1) * 512],
                                  start=(kk == 0 and n == 0), stop=(kk == depth - 1 and n == 2))
                last.then_inc(e_used, 1)

            def turn_hidden(b):
                pe.wait_ge(he_ready, b + 1)
                for f_ in range(FT):
                    last = nc.tensor.transpose(ps[:, 4, f_ * P:(f_ + 1) * P], h_e[:, f_ * P:(f_ + 1) * P], ident[:])
                last.then_inc(he_turned, 1)

            pe.wait_ge(xe_lo, 1)
            for k in range(KT):
                use_chunk(0, FT + k, xe_split, k, KT, 0)
            pe.wait_ge(x_landed, 32)
            turn_rows()
            turn_hidden(0)
            with pe.Fori(0, turns) as turn:
                b = turn + 1
                pe.wait_ge(xe_lo, b + 1)
                for k in range(KT):
                    use_chunk(b * BLOCK_CHUNKS, k, xe_split, k, KT, 0)
                pe.wait_ge(x_landed, b * 16 + 32)
                turn_rows()
                pe.wait_ge(he_lo, b)
                pe.wait_ge(y_act, b)
                pe.wait_ge(y_dve, b)
                for k in range(KT, BLOCK_CHUNKS):
                    use_chunk(b * BLOCK_CHUNKS, k, he_split, k - KT, FT, 5)
                turn_hidden(b)
            pe.wait_ge(he_lo, n_blocks)
            pe.wait_ge(y_act, n_blocks)
            pe.wait_ge(y_dve, n_blocks)
            for k in range(FT):
                use_chunk(n_blocks * BLOCK_CHUNKS, k, he_split, k, FT, 5)

        @block.scalar
        def _(act):
            links = [0]

            def link(ins):
                links[0] += 1
                ins.then_inc(act_chain, 1)
                act.wait_ge(act_chain, links[0])

            table = [None]

            def run(out, in_, func, **kw):
                need = "natural_log_exp_and_others" if func in (ACT.Exp, ACT.Ln) else (
                    None if func not in (ACT.Sigmoid, ACT.Silu) else str(func))
                if need and need != table[0]:
                    table[0] = need
                    if func in (ACT.Exp, ACT.Ln):
                        nc.scalar.preload_act_table_set(need)
                return nc.scalar.activation(out, in_, func, **kw)

            eps, one = cst[:, 0:1], cst[:, 1:2]

            def split_hi(c):
                act.wait_ge(landed[c % RAW], 16 * (c // RAW + 1))
                if c >= SPLIT:
                    act.wait_ge(w_used, c - SPLIT + 1)
                run(w_split[:, 0, c % SPLIT, :], raw[:, c % RAW, :], ACT.Copy).then_inc(hi_ready, 1)

            def squares_of_input(src, width, before):
                for k in range(KT):
                    if k >= 2:
                        act.wait_ge(x_sum, before + k - 1)
                    if before == 0 and k % 2 == 0:
                        act.wait_ge(x_in[k // 2], 16)
                    run(sq[:, k % 2, 0:width], src[:, k, :], ACT.Square).then_inc(x_sq, 1)

            def seed(st, width):
                if st != ("x", 0):
                    act.wait_ge(normed, normed_by[norm_order[norm_no[st] - 1]])
                if st[0] == "norm":
                    act.wait_ge(stat_ready, sum_no[st] + 1)
                else:
                    act.wait_ge(x_sum, KT * (1 + (st[0] == "mem_norm")))
                run(var[:, 0:width], ps[:, STAT, 0:width], ACT.Identity, bias=eps).then_inc(stat_read, 1)
                act.wait_ge(stat_read, stat_no[st] + 1)
                link(run(rstd[:, 0:width], var[:, 0:width], ACT.Ln))
                run(rstd[:, 0:width], rstd[:, 0:width], ACT.Exp, scale=-0.5).then_inc(seed_ready, 1)

            def split_normed(k, width, tmp, dst, before):
                act.wait_ge(h_f, before + k + 1)
                run(dst[:, 0, k, :], tmp[:, k % 2, 0:width], ACT.Copy).then_inc(h_hi, 1)

            def after_chunk(c):
                kind, i = CHUNKS[c]
                if kind in NATURAL:
                    g, kp = i // 4, i % 4
                    if kp < 3 or kind == "out":
                        return
                    act.wait_ge(w_used, c + 1)
                    if kind == "mv":
                        if g == 0:
                            act.wait_ge(h_lo, 2 * KT)
                        run(mv[:, 0, g * 512:(g + 1) * 512], ps[:, SCORE + 2 * g, :], ACT.Copy).then_inc(nat_read, 1)
                    else:
                        dst = fv if kind == "fv" else rv
                        for tt in (0, 1):
                            run(dst[:, tt, g * 512:(g + 1) * 512], ps[:, 4 * g + tt, :], ACT.Copy).then_inc(nat_read, 1)
                    return
                src = ps[:, tile_no[c] % 2, 0:M if kind == "mk" else S]
                if kind in ("fq", "fk", "mq", "mk"):
                    n, e = norm_of_chunk(kind, i)
                    act.wait_ge(w_used, c + 1)
                    if n in FOX_NORMS and n < 2:
                        act.wait_ge(x_sum, KT)
                    elif n == MK_NORMS[0]:
                        act.wait_ge(x_sum, 2 * KT)
                    else:
                        act.wait_ge(stat_ready, sum_no["norm", n - 2 if n in FOX_NORMS else n - 1] + 1)
                    width = M if kind == "mk" else S
                    run(sq[:, n % 2 if n in FOX_NORMS else e, 0:width], src, ACT.Square).then_inc(sq_ready, 1)
                elif kind == "ff":
                    act.wait_ge(w_used, c + 1)
                    act.wait_ge(h_lo, KT)
                    z, az, e = logits[0:FOX_HEADS, 0, :], logits[0:FOX_HEADS, 1, :], prob[0:FOX_HEADS, 0, :]
                    run(z, src[0:FOX_HEADS, :], ACT.Identity, bias=gains[0:FOX_HEADS, B_FF:B_FF + 1]).then_inc(tile_act, 1)
                    act.wait_ge(tile_act, 1)
                    link(run(az, z, ACT.Abs))
                    link(run(e, az, ACT.Exp, scale=-1.0))
                    run(e, e, ACT.Ln, bias=one[0:FOX_HEADS, :]).then_inc(gate_log, 1)
                elif kind in ("rk", "rq"):
                    n = 2 * (i // 2) + (kind == "rq")
                    act.wait_ge(w_used, c + 1)
                    if n:
                        act.wait_ge(rotated, n)
                    else:
                        act.wait_ge(tile_dve, fox_merged)
                    run(ret_raw[:, i % 2, :], src, ACT.Copy).then_inc(tile_act, 1)
                elif kind == "rg":
                    act.wait_ge(w_used, c + 1)
                    if i >= 2:
                        act.wait_ge(o_lo, KT + i // 2 * 2)
                    run(ret_o[:, i % 2, :], src, ACT.Silu).then_inc(tile_act, 1)
                elif kind in ("g_fox", "g_ret", "g_mem"):
                    act.wait_ge(w_used, c + 1)
                    b = ("g_fox", "g_ret", "g_mem").index(kind)
                    if b == 2:
                        act.wait_ge(merge_done, KT)
                    elif b:
                        act.wait_ge(tile_dve, fox_merged)
                    else:
                        act.wait_ge(h_lo, KT)
                    run(gate[:, i, :], src, ACT.Sigmoid).then_inc(tile_act, 1)
                elif kind == "o_mem":
                    act.wait_ge(merge_done, KT + i + 1)
                    run(h_split[:, 0, i, :], merged[:, i, :], ACT.Copy).then_inc(m_hi, 1)

            def row_square(g, tt):
                n = g * TT + tt
                act.wait_ge(x1_ready, n + 1)
                if n:
                    act.wait_ge(row_sq, n)
                else:
                    act.wait_ge(o_lo, 3 * KT)
                run(scratch[:, 0:512], x1[:, tt, g * 512:(g + 1) * 512], ACT.Square,
                    accum_out=sums[:, 4 * g, tt:tt + 1]).then_inc(row_sq, 1)

            def row_copy(g, tt):
                n = g * TT + tt
                act.wait_ge(xg_turned, n + 1)
                if g:
                    act.wait_ge(logit_done, tt + 1)
                run(xgT[:, :, tt * P:(tt + 1) * P], ps[:, n % 3, :].rearrange("p (k s) -> p k s", s=P),
                    ACT.Copy).then_inc(xg_copied, 1)

            act.wait_ge(cum_zero, 1)
            squares_of_input(xT, S, 0)
            seed(("x", 0), S)
            act.wait_ge(consts_in, 16 * 4)
            run(id_r[:], ident[:], ACT.Copy).then_inc(id_ready, 1)
            run(mask_r[:], mask_f[:], ACT.Copy).then_inc(id_ready, 1)
            for k in range(KT):
                split_normed(k, S, logits, h_split, 0)
                if k % 2 == 1 and k // 2 < AHEAD:
                    split_hi(k // 2)
            for slot in range(last_slot + 1):
                c = slot // 4
                if slot % 4 == 0:
                    if c:
                        after_chunk(c - 1)
                    if c + AHEAD < len(CHUNKS):
                        split_hi(c + AHEAD)
                for st in STEPS.get(slot, ()):
                    what, j = st
                    if what == "row_turn":
                        row_square(0, j)
                        row_copy(0, j)
                    elif what == "norm":
                        if j == MK_NORMS[0]:
                            act.wait_ge(h_f, 2 * KT)
                        seed(st, norm_io(j)[2])
                    elif what == "mem_norm":
                        act.wait_ge(stat_ready, sum_no["norm", RET_NORMS[-1]] + 1)
                        act.wait_ge(mem_in, 16)
                        squares_of_input(memT, M, KT)
                        seed(st, M)
                    elif what == "mem_split":
                        act.wait_ge(w_used, FIRST["o_ret"] + KT)
                        for k in range(KT):
                            split_normed(k, M, ret_raw, mem_split, KT)
                    elif what == "forget":
                        act.wait_ge(stat_ready, sum_no[st] + 1)
                        if j >= 2:
                            act.wait_ge(sc_read, TT * (j - 1))
                        else:
                            act.wait_ge(cum_ready, 1)
                        run(forget[:, j % 2, :], ps[:, STAT, :], ACT.Copy).then_inc(stat_read, 1)
                    elif what == "fox_score":
                        w = P * (j % TT + 1)
                        act.wait_ge(sc_read, j + 1)
                        if j >= 2:
                            act.wait_ge(turned, j - 1)
                        run(prob[:, j % 2, 0:w], logits[:, j % 2, 0:w], ACT.Exp, scale=-1.0,
                            bias=stat[:, j % 2:j % 2 + 1], accum_out=stat[:, 2 + j % 2:3 + j % 2]).then_inc(prob_ready, 1)
                    elif what == "fox_turn":
                        head, r = j // TT, j % TT
                        act.wait_ge(turned, j + 1)
                        if head >= 2:
                            act.wait_ge(pv_done, head - 1)
                        run(fox_pt[:, head % 2, 0:r + 1, r * P:(r + 1) * P],
                            ps[:, TURN + j % 2, 0:P * (r + 1)].rearrange("p (k i) -> p k i", i=P),
                            ACT.Copy).then_inc(turn_read, 1)
                    elif what == "fox_pv" and j % 2 == 1:
                        act.wait_ge(pv_done, j + 1)
                        run(o_split[:, 0, j // 2, :], ps[:, PV, :], ACT.Copy).then_inc(o_hi, 1)
                    elif what == "ret_pv":
                        act.wait_ge(pv_done, FOX_HEADS + j + 1)
                        e = j % 2
                        n = RET_NORMS[0] + j // 2
                        act.wait_ge(stat_ready, sum_no["norm", n - 1] + 1)
                        run(sq[:, e, :], ps[:, PV if e == 0 else TURN, :], ACT.Square).then_inc(ret_sq, 1)
                    elif what == "ret_out":
                        act.wait_ge(normed, normed_by["norm", RET_NORMS[j]])
                        if j == 0:
                            act.wait_ge(w_used, FIRST["o_fox"] + KT)
                        for e in range(HEAD_TILES):
                            run(o_split[:, 0, HEAD_TILES * j + e, :], ret_o[:, e, :], ACT.Copy).then_inc(o_hi, 1)
                    elif what == "mem_score":
                        n = soft["mem", j]
                        act.wait_ge(mem_min, j + 1)
                        if j >= 2:
                            act.wait_ge(turned, n - 1)
                        run(mem_p[:, n % 2, :], ps[:, SCORE + sc_no[st] % 2, 0:M], ACT.Exp, scale=-1.0,
                            bias=stat[:, n % 2:n % 2 + 1], accum_out=stat[:, 2 + n % 2:3 + n % 2]).then_inc(sc_read, 1)
                    elif what == "mem_turn":
                        n = soft["mem", j]
                        h, r = j // TT, j % TT
                        act.wait_ge(turned, n + 1)
                        if h:
                            act.wait_ge(pv_done, FOX_HEADS + 2 * RET_HEADS + 2 * h)
                        run(mem_pt[:, :, r * P:(r + 1) * P],
                            ps[:, TURN + n % 2, 0:M].rearrange("p (k i) -> p k i", i=P), ACT.Copy).then_inc(turn_read, 1)
                    elif what == "mem_pv":
                        act.wait_ge(pv_done, FOX_HEADS + 2 * RET_HEADS + j + 1)
                        if j == 0:
                            act.wait_ge(w_used, FIRST["mq"])
                        run(o_split[:, 0, j, :], ps[:, PV, :], ACT.Copy).then_inc(o_hi, 1)

            for tt in range(TT):
                row_square(1, tt)
                if tt:
                    row_copy(1, tt - 1)
            act.wait_ge(row_sum, 1)
            link(run(sums[:, 1, :], sums[:, 5, :], ACT.Ln, scale=1.0 / D, bias=eps))
            run(sums[:, 1, :], sums[:, 1, :], ACT.Exp, scale=-0.5).then_inc(row_seed, 1)
            row_copy(1, TT - 1)
            run(before_r, before, ACT.Copy).then_inc(tab_r, 1)
            run(ones_r, ones, ACT.Copy).then_inc(tab_r, 1)
            act.wait_ge(logit_ready, 1)
            run(r64[0], r64[7], ACT.Sigmoid).then_inc(score_ready, 1)
            act.wait_ge(row_rstd, 1)
            act.wait_ge(xg_turned, 2 * TT)
            for tt in range(TT):
                run(h2[:, tt, :], h2[:, tt, :], ACT.Copy, scale=sums[:, 1, tt:tt + 1]).then_inc(h2_ready, 1)

            def split_rows():
                for h in range(2):
                    ins = run(xe_split[:, 0, 4 * h:4 * h + 4, :], ps[:, 2 + h, :].rearrange("p (k s) -> p k s", k=4), ACT.Copy)
                ins.then_inc(xe_hi, 1)

            nc.scalar.preload_act_table_set("silu_and_others")
            act.wait_ge(xe_turned, 1)
            split_rows()
            act.wait_ge(y_filled, 16)
            act.wait_ge(e_lo, FT)
            turns = act.value_load(blocks_i[0:1, IDX_COLS:IDX_COLS + 1], min_val=TOP_K * S // P - 1, max_val=MAX_BLOCKS - 1)
            n_blocks = turns + 1

            def expert_hi(at, k, landed_value):
                act.wait_ge(e_landed[k], landed_value)
                act.wait_ge(e_used, at + (k + 1 - E_SPLIT))
                run(ew_split[:, 0, k % E_SPLIT, :], e_raw[k], ACT.Copy).then_inc(e_hi, 1)

            def silu_gate(b, used):
                act.wait_ge(e_used, used)
                run(h_act, ps[:, 0, :], ACT.Silu).then_inc(silu_done, 1)

            def hidden_hi(b):
                act.wait_ge(he_turned, b + 1)
                run(he_split[:, 0, :, :], ps[:, 4, :].rearrange("p (f s) -> p f s", f=FT), ACT.Copy).then_inc(he_hi, 1)

            def store_y(b, used):
                act.wait_ge(e_used, used)
                act.wait_ge(y_stored, b * 16 + 16)
                run(y_rows[:, 0:512], ps[:, 5, :], ACT.Copy).then_inc(y_act, 1)
                act.wait_ge(y_act, b + 1)
                act.wait_ge(y_dve, b + 1)
                nc.scalar.dma_start(dram["y"][bass.ds(b * P, P), :], y_rows).then_inc(y_stored, 16)

            for k in range(FT, BLOCK_CHUNKS):
                expert_hi(0, k, landed_by(0, k))
            silu_gate(0, BLOCK_CHUNKS)
            act.wait_ge(xe_turned, 2)
            split_rows()
            with act.Fori(0, turns) as turn:
                b = turn + 1
                for k in range(BLOCK_CHUNKS):
                    if k == BLOCK_CHUNKS - 1:
                        silu_gate(b, b * BLOCK_CHUNKS + KT)
                    expert_hi(b * BLOCK_CHUNKS, k, landed_by(b, k))
                    if k == 3:
                        hidden_hi(b - 1)
                        store_y(b - 1, b * BLOCK_CHUNKS)
                act.wait_ge(xe_turned, b + 2)
                split_rows()
            for k in range(FT):
                expert_hi(n_blocks * BLOCK_CHUNKS, k, landed_by(n_blocks, k))
            hidden_hi(n_blocks - 1)
            store_y(n_blocks - 1, n_blocks * BLOCK_CHUNKS)
            store_y(n_blocks, n_blocks * BLOCK_CHUNKS + FT)

        @block.vector
        def _(dve):
            links = [0]

            def link(ins):
                links[0] += 1
                ins.then_inc(dve_chain, 1)
                dve.wait_ge(dve_chain, links[0])

            def f(ap):
                return ap.bitcast(F32)

            def split_lo(c):
                dve.wait_ge(hi_ready, c + 1)
                nc.vector.tensor_tensor(w_split[:, 1, c % SPLIT, :], raw[:, c % RAW, :],
                                        f(w_split[:, 0, c % SPLIT, :]), ALU.subtract).then_inc(lo_ready, 1)

            def norm_input(src, width, tmp, dst, g, before):
                for k in range(KT):
                    if k >= 2:
                        dve.wait_ge(h_lo, before + k - 1)
                    nc.vector.scalar_tensor_tensor(tmp[:, k % 2, 0:width], src[:, k, :], gains[:, g + k:g + k + 1],
                                                   rstd[:, 0:width], ALU.mult, ALU.mult).then_inc(h_f, 1)
                    dve.wait_ge(h_hi, before + k + 1)
                    nc.vector.tensor_tensor(dst[:, 1, k, :], tmp[:, k % 2, 0:width], f(dst[:, 0, k, :]),
                                            ALU.subtract).then_inc(h_lo, 1)
                    if before == 0 and k % 2 == 1 and k // 2 < AHEAD:
                        split_lo(k // 2)

            def after_chunk(c):
                kind, i = CHUNKS[c]
                if kind in NATURAL:
                    g, kp = i // 4, i % 4
                    if kp < 3:
                        return
                    dve.wait_ge(w_used, c + 1)
                    if kind == "mv":
                        if g == 0:
                            dve.wait_ge(h_lo, 2 * KT)
                        nc.vector.tensor_copy(mv[:, 1, g * 512:(g + 1) * 512], ps[:, SCORE + 2 * g + 1, :]).then_inc(nat_read, 1)
                    elif kind == "out":
                        dve.wait_ge(xn_in, 16)
                        dve.wait_ge(tab_in, 16 * 10)
                        dve.wait_ge(m_hi, KT)
                        for tt in range(TT):
                            cols = slice(g * 512, (g + 1) * 512)
                            nc.vector.tensor_tensor(x1[:, tt, cols], ps[:, 4 * g + tt, :], x_nat[:, tt, cols],
                                                    ALU.add).then_inc(x1_ready, 1)
                            dve.wait_ge(x1_ready, g * TT + tt + 1)
                            nc.vector.tensor_tensor(h2[:, tt, cols], x1[:, tt, cols], gain_b[:, cols],
                                                    ALU.mult).then_inc(xg_ready, 1)
                    else:
                        dst = fv if kind == "fv" else rv
                        for tt in (2, 3):
                            nc.vector.tensor_copy(dst[:, tt, g * 512:(g + 1) * 512], ps[:, 4 * g + tt, :]).then_inc(nat_read, 1)
                    return
                src = ps[:, tile_no[c] % 2, 0:M if kind == "mk" else S]
                if kind in ("fq", "fk", "mq", "mk"):
                    n, e = norm_of_chunk(kind, i)
                    dve.wait_ge(sq_ready, squares_by(n, e))
                    if n >= 2 and n in FOX_NORMS:
                        dve.wait_ge(normed, normed_by["norm", n - 2])
                    elif n not in FOX_NORMS:
                        dve.wait_ge(normed, normed_by[norm_order[norm_no["norm", n] - 1]])
                    dst = fox_raw[:, n % 2, :] if n in FOX_NORMS else mem_raw[:, e, 0:M if kind == "mk" else S]
                    g = {"fq": G_FQ, "fk": G_FK, "mq": G_MQ + e, "mk": G_MK + e}[kind]
                    scale = {"fq": -FOX_DIM ** -0.5, "mq": -(2 * P) ** -0.5}.get(kind, 1.0)
                    nc.vector.tensor_scalar(dst, src, gains[:, g:g + 1], scale, ALU.mult, ALU.mult).then_inc(tile_dve, 1)
                elif kind == "ff":
                    z, e, lf = logits[0:FOX_HEADS, 0, :], prob[0:FOX_HEADS, 0, :], prob[0:FOX_HEADS, 1, :]
                    dve.wait_ge(gate_log, 1)
                    link(nc.vector.memset(forget[0:FOX_HEADS, 0, :], 1.0))
                    link(nc.vector.scalar_tensor_tensor(lf, z, 0.0, e, ALU.min, ALU.subtract))
                    nc.vector.tensor_tensor_scan(cum[:, :], forget[0:FOX_HEADS, 0, :], lf, 0.0,
                                                 ALU.mult, ALU.add).then_inc(cum_ready, 1)
                elif kind in ("o_fox", "o_ret", "o_mem"):
                    b = ("o_fox", "o_ret", "o_mem").index(kind)
                    dve.wait_ge(w_used, c + 1)
                    dve.wait_ge(tile_act, count_before(READ_BY_ACT, FIRST[kind]))
                    if b == 0:
                        nc.vector.tensor_tensor(merged[:, i, :], src, gate[:, i, :], ALU.mult).then_inc(tile_dve, 1)
                        return
                    nc.vector.tensor_tensor(gate[:, i, :], src, gate[:, i, :], ALU.mult).then_inc(tile_dve, 1)
                    dve.wait_ge(tile_dve, count_before(READ_BY_DVE, c + 1))
                    nc.vector.tensor_tensor(merged[:, i, :], merged[:, i, :], gate[:, i, :],
                                            ALU.add).then_inc(merge_done, 1)
                    if b == 2:
                        dve.wait_ge(m_hi, i + 1)
                        nc.vector.tensor_tensor(h_split[:, 1, i, :], merged[:, i, :], f(h_split[:, 0, i, :]),
                                                ALU.subtract).then_inc(m_lo, 1)

            def lo_part(t, src):
                dve.wait_ge(o_hi, t + 1)
                nc.vector.tensor_tensor(o_split[:, 1, t % KT, :], src, f(o_split[:, 0, t % KT, :]),
                                        ALU.subtract).then_inc(o_lo, 1)

            link(nc.vector.memset(cst[:, 0:1], EPS))
            nc.vector.memset(cst[:, 1:2], 1.0).then_inc(cum_zero, 1)
            dve.wait_ge(normed, 1)
            dve.wait_ge(consts_in, 16 * 4)
            norm_input(xT, S, logits, h_split, G_MIX, 0)
            for slot in range(last_slot + 1):
                c = slot // 4
                if slot % 4 == 0:
                    if c:
                        after_chunk(c - 1)
                    if c + AHEAD < len(CHUNKS):
                        split_lo(c + AHEAD)
                for st in STEPS.get(slot, ()):
                    what, j = st
                    if what == "mem_split":
                        dve.wait_ge(normed, normed_by["mem_norm", 0])
                        dve.wait_ge(o_lo, 2 * KT)
                        norm_input(memT, M, ret_raw, mem_split, G_MEM, KT)
                    elif what == "fox_score":
                        w = P * (j % TT + 1)
                        dve.wait_ge(sc_done, j + 1)
                        if j >= 2:
                            dve.wait_ge(prob_ready, j - 1)
                        dve.wait_ge(stat_read, stat_no["forget", j // TT] + 1)
                        nc.vector.tensor_tensor_reduce(logits[:, j % 2, 0:w], ps[:, SCORE + j % 2, 0:w],
                                                       forget[:, j // TT % 2, 0:w], 1.0, 3.0e38, ALU.add, ALU.min,
                                                       stat[:, j % 2:j % 2 + 1]).then_inc(sc_read, 1)
                    elif what in ("fox_scale", "mem_scale"):
                        n = soft[what[:3], j]
                        w = P * (j % TT + 1) if what[0] == "f" else M
                        buf = (prob if what[0] == "f" else mem_p)[:, n % 2, 0:w]
                        if what[0] == "f":
                            dve.wait_ge(prob_ready, j + 1)
                        else:
                            dve.wait_ge(sc_read, sc_no["mem_score", j] + 1)
                        link(nc.vector.reciprocal(stat[:, 4 + n % 2:5 + n % 2], stat[:, 2 + n % 2:3 + n % 2]))
                        nc.vector.tensor_scalar(buf, buf, stat[:, 4 + n % 2:5 + n % 2], None,
                                                ALU.mult).then_inc(prob_scaled, 1)
                    elif what == "fox_pv" and j % 2 == 1:
                        lo_part(j // 2, ps[:, PV, :])
                    elif what == "ret_score":
                        h, k = j // TT, j % TT
                        n = sc_no[st]
                        w = S - k * P
                        at = RET_AT[k]
                        dve.wait_ge(sc_done, n + 1)
                        dve.wait_ge(decay_in, 16 * (h + 1))
                        if h:
                            dve.wait_ge(pv_done, FOX_HEADS + HEAD_TILES * h)
                        nc.vector.tensor_tensor(ret_p[:, at:at + w], ps[:, SCORE + n % 2, 0:w], decay[:, 0:w],
                                                ALU.mult).then_inc(sc_read, 1)
                    elif what == "ret_pv":
                        h, e = j // 2, j % 2
                        dve.wait_ge(pv_done, FOX_HEADS + j + 1)
                        dve.wait_ge(ret_sq, j + 1)
                        dve.wait_ge(tile_act, count_before(READ_BY_ACT, FIRST["rk"] + 6 * h + 5 + e))
                        nc.vector.tensor_tensor(ret_o[:, e, :], ret_o[:, e, :], ps[:, PV if e == 0 else TURN, :],
                                                ALU.mult).then_inc(ret_gated, 1)
                    elif what == "ret_out":
                        dve.wait_ge(normed, normed_by["norm", RET_NORMS[j]])
                        for e in range(HEAD_TILES):
                            lo_part(KT + HEAD_TILES * j + e, ret_o[:, e, :])
                    elif what == "mem_score":
                        n = soft["mem", j]
                        dve.wait_ge(sc_done, sc_no[st] + 1)
                        if j >= 2:
                            dve.wait_ge(sc_read, sc_no[st] - 1)
                        nc.vector.tensor_reduce(stat[:, n % 2:n % 2 + 1], ps[:, SCORE + sc_no[st] % 2, 0:M], AX.X,
                                                ALU.min).then_inc(mem_min, 1)
                    elif what == "mem_pv":
                        lo_part(2 * KT + j, ps[:, PV, :])

            V = nc.vector
            ms, r, t = sums[:, 2, :], sums[:, 1, :], sums[:, 3, :]
            dve.wait_ge(row_sq, 2 * TT)
            V.tensor_tensor(sums[:, 5, :], sums[:, 0, :], sums[:, 4, :], ALU.add).then_inc(row_sum, 1)
            dve.wait_ge(row_sum, 1)
            link(V.tensor_scalar(ms, sums[:, 5, :], 1.0 / D, EPS, ALU.mult, ALU.add))
            dve.wait_ge(row_seed, 1)
            link(V.tensor_tensor(t, ms, r, ALU.mult))
            link(V.tensor_tensor(t, t, r, ALU.mult))
            link(V.tensor_scalar(t, t, -0.5, 1.5, ALU.mult, ALU.add))
            V.tensor_tensor(r, r, t, ALU.mult).then_inc(row_rstd, 1)
            dve.wait_ge(row_rstd, 1)
            dve.wait_ge(logit_done, 2 * TT)
            link(V.tensor_copy(r64[8], ps[:, 3, 0:TT * N_EXPERTS]))
            link(V.tensor_tensor(r64[7], r64[8], ps[:, 3, TT * N_EXPERTS:2 * TT * N_EXPERTS], ALU.add))
            V.tensor_tensor(r64[7].rearrange("p (t e) -> p t e", t=TT), r64[7].rearrange("p (t e) -> p t e", t=TT),
                            r.unsqueeze(2).to_broadcast([P, TT, N_EXPERTS]), ALU.mult).then_inc(logit_ready, 1)

            score, biased, sel, w, pos = r64[0:5]
            t64a, t64b = r64[5], r64[6]

            def experts_of(ap):
                return ap.rearrange("p (q e) -> p q e", e=PER_GROUP)

            def ranks(v, n, out):
                a4 = v.unsqueeze(2).to_broadcast([P, n, 4, 4])
                b4 = v.unsqueeze(3).to_broadcast([P, n, 4, 4])
                g4 = r256a[:, 0:n * 16].rearrange("p (q b a) -> p q b a", b=4, a=4)
                e4 = r256b[:, 0:n * 16].rearrange("p (q b a) -> p q b a", b=4, a=4)
                V.tensor_tensor(g4, a4, b4, ALU.is_gt)
                link(V.tensor_tensor(e4, a4, b4, ALU.is_equal))
                link(V.tensor_tensor(e4, e4, order4.unsqueeze(1).to_broadcast([P, n, 4, 4]), ALU.mult))
                link(V.tensor_tensor(g4, g4, e4, ALU.add))
                link(V.tensor_reduce(out, g4, AX.X, ALU.add))

            dve.wait_ge(score_ready, 1)
            link(V.tensor_tensor(biased, score, bias_b, ALU.add))
            pair = biased.rearrange("p (q c d) -> p q c d", c=2, d=2)
            hi2 = t64a[:, 0:32].rearrange("p (q c) -> p q c", c=2)
            lo2 = t64a[:, 32:64].rearrange("p (q c) -> p q c", c=2)
            V.tensor_tensor(hi2, pair[:, :, :, 0], pair[:, :, :, 1], ALU.max)
            link(V.tensor_tensor(lo2, pair[:, :, :, 0], pair[:, :, :, 1], ALU.min))
            V.tensor_tensor(r16[0], hi2[:, :, 0], hi2[:, :, 1], ALU.max)
            V.tensor_tensor(r16[1], hi2[:, :, 0], hi2[:, :, 1], ALU.min)
            link(V.tensor_tensor(r16[2], lo2[:, :, 0], lo2[:, :, 1], ALU.max))
            link(V.tensor_tensor(r16[1], r16[1], r16[2], ALU.max))
            link(V.tensor_tensor(r16[3], r16[0], r16[1], ALU.add))
            ranks(r16[3].rearrange("p (t g) -> p t g", g=N_GROUPS), TT, r16[4].rearrange("p (t g) -> p t g", g=N_GROUPS))
            link(V.tensor_scalar(r16[4], r16[4], 1.0, None, ALU.is_lt))
            ranks(experts_of(biased), TT * N_GROUPS, experts_of(t64b))
            link(V.tensor_scalar(t64b, t64b, float(TOP_K), None, ALU.is_lt))
            link(V.tensor_tensor(experts_of(sel), experts_of(t64b),
                                 r16[4].unsqueeze(2).to_broadcast([P, TT * N_GROUPS, PER_GROUP]), ALU.mult))
            V.tensor_copy(sel_r, sel).then_inc(sel_ready, 1)
            link(V.tensor_tensor(w, score, sel, ALU.mult))
            by_token = (lambda ap: ap.rearrange("p (t e) -> p t e", e=N_EXPERTS))
            denom = r16[5][:, 0:TT]
            link(V.tensor_reduce(denom, by_token(w), AX.X, ALU.add))
            link(V.reciprocal(denom, denom))
            dve.wait_ge(pos_done, 1)
            count, blocks, ends, starts = r16[6], r16[7], r16[8], r16[9]
            link(V.tensor_copy(count, ps[:, 6, 0:N_EXPERTS]))
            link(V.tensor_scalar(blocks, count, 0.5, None, ALU.is_gt))
            for n in range(1, TT):
                link(V.scalar_tensor_tensor(blocks, count, n * P + 0.5, blocks, ALU.is_gt, ALU.add))
            link(V.tensor_scalar(blocks[:, 0:1], blocks[:, 0:1], 1.0, None, ALU.max))
            link(V.tensor_tensor_scan(ends, ones[:, 0:N_EXPERTS], blocks, 0.0, ALU.mult, ALU.add))
            link(V.tensor_tensor(starts, ends, blocks, ALU.subtract))
            link(V.scalar_tensor_tensor(by_token(pos), starts.unsqueeze(1).to_broadcast([P, TT, N_EXPERTS]), float(P),
                                        by_token(ps[:, 5, 0:TT * N_EXPERTS]), ALU.mult, ALU.add))
            far = float(IDX_COLS * P)
            link(V.tensor_scalar(t64a, sel, -far, far, ALU.mult, ALU.add))
            link(V.tensor_tensor(t64a, t64a, pos, ALU.add))
            slots = r16[10][:, 0:2 * TT]
            first, second = slots[:, 0:TT], slots[:, TT:]
            link(V.tensor_reduce(first, by_token(t64a), AX.X, ALU.min))
            link(V.scalar_tensor_tensor(t64b, pos, 1.0, sel, ALU.add, ALU.mult))
            link(V.tensor_reduce(second, by_token(t64b), AX.X, ALU.max))
            link(V.tensor_scalar(second, second, -1.0, None, ALU.add))
            by_block = (lambda ap: ap[:, 0:2 * TT * IDX_COLS].rearrange("p (j b) -> p j b", b=IDX_COLS))
            lane_in, in_block, start_in = by_block(r256a), by_block(r384), by_block(r256b)
            link(V.tensor_tensor(lane_in, slots.unsqueeze(2).to_broadcast([P, 2 * TT, IDX_COLS]),
                                 block_at.unsqueeze(1).to_broadcast([P, 2 * TT, IDX_COLS]), ALU.subtract))
            link(V.tensor_scalar(start_in, lane_in, 0.0, None, ALU.is_ge))
            link(V.scalar_tensor_tensor(in_block, lane_in, float(P), start_in, ALU.is_lt, ALU.mult))
            link(V.tensor_tensor(lane_in, lane_in, in_block, ALU.mult))
            lane = r16[11][:, 0:2 * TT]
            link(V.tensor_reduce(lane, lane_in, AX.X, ALU.add))
            link(V.tensor_tensor(block_ids, in_block, token_f.unsqueeze(2).to_broadcast([P, 2 * TT, IDX_COLS]), ALU.mult))
            for j in range(2 * TT):
                V.tensor_scalar(lane_hot[:, j, :], lanes, lane[:, j:j + 1], None, ALU.is_equal).then_inc(hot_ready, 1)
            be = r384.rearrange("p (b e) -> p b e", e=N_EXPERTS)
            link(V.tensor_tensor(be, iota.unsqueeze(2).to_broadcast([P, IDX_COLS, N_EXPERTS]),
                                 ends.unsqueeze(1).to_broadcast([P, IDX_COLS, N_EXPERTS]), ALU.is_ge))
            link(V.tensor_reduce(r256a[:, 0:IDX_COLS], be, AX.X, ALU.add))
            link(V.tensor_scalar(r256a[:, 0:IDX_COLS], r256a[:, 0:IDX_COLS], float(N_EXPERTS - 1), None, ALU.min))
            link(V.tensor_copy(blocks_i[:, 0:IDX_COLS], r256a[:, 0:IDX_COLS]))
            link(V.tensor_scalar(blocks_i[:, IDX_COLS:IDX_COLS + 1], ends[:, N_EXPERTS - 1:N_EXPERTS], -1.0, None, ALU.add))
            dve.wait_ge(rows_done, 1)
            V.tensor_copy(rows_i[:], ps[:, 4, 0:IDX_COLS]).then_inc(rows_ready, 1)
            dve.wait_ge(w_used, len(CHUNKS))
            V.memset(stat[:, 3:4], 0.0).then_inc(e_hi, FT)
            V.memset(stat[:, 0:1], 0.0).then_inc(e_lo, FT)
            V.memset(stat[:, 1:2], 0.0).then_inc(e_used, FT)
            V.memset(stat[:, 2:3], 0.0).then_inc(y_stored, 16)
            for a, slot_ in ((0, first), (1, second)):
                link(V.tensor_tensor(by_token(t64a), by_token(pos), slot_.unsqueeze(2).to_broadcast([P, TT, N_EXPERTS]),
                                     ALU.is_equal))
                link(V.tensor_tensor(t64a, t64a, w, ALU.mult))
                link(V.tensor_reduce(token_w[:, a, :], by_token(t64a), AX.X, ALU.add))
                link(V.tensor_tensor(token_w[:, a, :], token_w[:, a, :], denom, ALU.mult))
                V.tensor_scalar(y_slot_i[:, a, :], slot_, float(P), None, ALU.add).then_inc(table_ready, 1)

            def rows_lo():
                for h in range(2):
                    ins = V.tensor_tensor(xe_split[:, 1, 4 * h:4 * h + 4, :], ps[:, 2 + h, :].rearrange("p (k s) -> p k s", k=4),
                                          f(xe_split[:, 0, 4 * h:4 * h + 4, :]), ALU.subtract)
                ins.then_inc(xe_lo, 1)

            dve.wait_ge(xe_hi, 1)
            rows_lo()
            turns = dve.value_load(blocks_i[0:1, IDX_COLS:IDX_COLS + 1], min_val=TOP_K * S // P - 1, max_val=MAX_BLOCKS - 1)
            n_blocks = turns + 1

            def expert_lo(at, k):
                dve.wait_ge(e_hi, at + (k + 1))
                V.tensor_tensor(ew_split[:, 1, k % E_SPLIT, :], e_raw[k], f(ew_split[:, 0, k % E_SPLIT, :]),
                                ALU.subtract).then_inc(e_lo, 1)

            def hidden(b):
                dve.wait_ge(silu_done, b + 1)
                V.tensor_tensor(h_e, h_act, ps[:, 1, :], ALU.mult).then_inc(he_ready, 1)

            def hidden_lo(b):
                dve.wait_ge(he_hi, b + 1)
                V.tensor_tensor(he_split[:, 1, :, :], ps[:, 4, :].rearrange("p (f s) -> p f s", f=FT),
                                f(he_split[:, 0, :, :]), ALU.subtract).then_inc(he_lo, 1)

            def leave_y(b, used):
                dve.wait_ge(e_used, used)
                dve.wait_ge(y_stored, b * 16 + 16)
                V.tensor_copy(y_rows[:, 512:], ps[:, 6, :]).then_inc(y_dve, 1)

            for k in range(FT, BLOCK_CHUNKS):
                expert_lo(0, k)
            hidden(0)
            dve.wait_ge(xe_hi, 2)
            rows_lo()
            with dve.Fori(0, turns) as turn:
                b = turn + 1
                for k in range(BLOCK_CHUNKS):
                    if k == BLOCK_CHUNKS - 1:
                        hidden(b)
                    expert_lo(b * BLOCK_CHUNKS, k)
                    if k == 3:
                        hidden_lo(b - 1)
                        leave_y(b - 1, b * BLOCK_CHUNKS)
                dve.wait_ge(xe_hi, b + 2)
                rows_lo()
            for k in range(FT):
                expert_lo(n_blocks * BLOCK_CHUNKS, k)
            hidden_lo(n_blocks - 1)
            leave_y(n_blocks - 1, n_blocks * BLOCK_CHUNKS)
            leave_y(n_blocks, n_blocks * BLOCK_CHUNKS + FT)

            for tt in range(TT):
                for a, (rows, landed_) in enumerate(((y_a, ya_in), (y_b, yb_in))):
                    dve.wait_ge(landed_[tt % 2], 16 * (tt // 2 + 1))
                    V.scalar_tensor_tensor(x1[:, tt, :], rows[:, tt % 2, :], token_w[:, a, tt:tt + 1], x1[:, tt, :],
                                           ALU.mult, ALU.add).then_inc(token_out if a == 0 else mixed, 1)
                    if a == 0:
                        dve.wait_ge(token_out, tt + 1)

        @block.gpsimd
        def _(pool):
            links = [0]

            def link(ins):
                links[0] += 1
                ins.then_inc(pool_chain, 1)
                pool.wait_ge(pool_chain, links[0])

            tt_ = nc.gpsimd.tensor_tensor

            def refine(st, width):
                pool.wait_ge(seed_ready, norm_no[st] + 1)
                v, r, t = var[:, 0:width], rstd[:, 0:width], newton[:, 0:width]
                link(tt_(t, v, r, ALU.mult))
                link(tt_(t, t, r, ALU.mult))
                link(nc.gpsimd.tensor_scalar(t, t, -0.5, 1.5, ALU.mult, ALU.add))
                if st[0] != "norm":
                    tt_(r, r, t, ALU.mult).then_inc(normed, 1)
                    return
                link(tt_(r, r, t, ALU.mult))
                n = st[1]
                src, dst, _ = norm_io(n)
                if n in RET_NORMS:
                    pool.wait_ge(ret_gated, HEAD_TILES * (n - RET_NORMS[0] + 1))
                else:
                    pool.wait_ge(tile_dve, count_before(READ_BY_DVE, chunk_of_norm(n) + 1))
                if n in FOX_NORMS and n >= 4:
                    pool.wait_ge(sc_done, 8 * (n // 2 - 1))
                if n == MK_NORMS[0]:
                    pool.wait_ge(pv_done, FOX_HEADS + RET_HEADS * HEAD_TILES)
                if n in MQ_NORMS and n > MQ_NORMS[0]:
                    pool.wait_ge(sc_done, TT * (FOX_HEADS + RET_HEADS + n - MQ_NORMS[0]))
                for a, b in zip(src, dst):
                    tt_(b, a, r, ALU.mult).then_inc(normed, 1)

            refine(("x", 0), S)
            for slot in range(last_slot):
                for st in STEPS.get(slot, ()):
                    what, j = st
                    if what == "norm":
                        refine(st, norm_io(j)[2])
                    elif what == "mem_norm":
                        refine(st, M)
                    elif what == "rotary":
                        h, is_q = j // 2, j % 2
                        dst = ret_q if is_q else ret_k
                        pool.wait_ge(tile_act, count_before(READ_BY_ACT, FIRST["rk"] + 6 * h + 2 * is_q + 2))
                        if j == 0:
                            pool.wait_ge(tile_dve, fox_merged)
                            nc.gpsimd.dma_start(cos, dram["cos"]).then_inc(rot_in, 16)
                            nc.gpsimd.dma_start(sin, dram["sin"]).then_inc(rot_in, 16)
                        if not is_q:
                            if h:
                                pool.wait_ge(sc_read, TT * (FOX_HEADS + h))
                            nc.gpsimd.dma_start(decay, dram["decay"][h]).then_inc(decay_in, 16)
                        pool.wait_ge(rot_in, 32)
                        if h:
                            pool.wait_ge(sc_done, TT * (FOX_HEADS + h))
                        a, b = ret_raw[:, 0, :], ret_raw[:, 1, :]
                        link(tt_(dst[:, 0, :], a, cos, ALU.mult))
                        link(tt_(rot, b, sin, ALU.mult))
                        link(tt_(dst[:, 0, :], dst[:, 0, :], rot, ALU.subtract))
                        link(tt_(dst[:, 1, :], b, cos, ALU.mult))
                        link(tt_(rot, a, sin, ALU.mult))
                        tt_(dst[:, 1, :], dst[:, 1, :], rot, ALU.add).then_inc(rotated, 1)

            row = bass.IndirectOffsetOnAxis
            pool.wait_ge(h2_stored, 16 * TT)

            def gather_rows(col, n):
                nc.gpsimd.tensor_copy(row_i[:, :], rows_i[:, col]).then_inc(row_copied, 1)
                pool.wait_ge(row_copied, n)
                pool.sem_inc(gathers, 1)
                nc.gpsimd.indirect_dma_start(x_rows, None, dram["h2"], row(row_i[:, 0:1], 0)).then_inc(x_landed, 16)

            pool.wait_ge(rows_ready, 1)
            gather_rows(slice(0, 1), 1)
            pool.wait_ge(e_lo, FT)
            turns = pool.value_load(blocks_i[0:1, IDX_COLS:IDX_COLS + 1], min_val=TOP_K * S // P - 1, max_val=MAX_BLOCKS - 1)
            n_blocks = turns + 1
            with pool.Fori(0, n_blocks) as b:
                pool.wait_ge(xe_turned, b + 1)
                gather_rows(bass.ds(b + 1, 1), b + 2)
            pool.wait_ge(y_stored, n_blocks * 16 + 32)
            pool.sem_inc(gathers, 1)
            for tt in range(TT):
                if tt >= 2:
                    pool.wait_ge(mixed, tt - 1)
                for a, (rows, landed_) in enumerate(((y_a, ya_in), (y_b, yb_in))):
                    nc.gpsimd.indirect_dma_start(rows[:, tt % 2, :], None, dram["y"],
                                                 row(y_slot_i[:, a, tt:tt + 1], 0)).then_inc(landed_[tt % 2], 16)


def columns_of(w, kind, i):
    if kind in NATURAL:
        g, kp = i // 4, i % 4
        return w[2 * P * kp:2 * P * (kp + 1), 512 * g:512 * (g + 1)].reshape(2, P, 512).transpose(1, 0, 2).reshape(P, 1024)
    return w[:, P * i:P * (i + 1)].reshape(KT, P, P).transpose(1, 0, 2).reshape(P, 1024)


def tables():
    half = P
    inv_freq = (np.float32(10000.0) ** (-np.arange(0, 2 * P, 2, dtype=np.float32) / np.float32(2 * P))).astype(np.float32)
    ang = (np.arange(S, dtype=np.float32)[None, :] * inv_freq[:, None]).astype(np.float32)
    j = np.arange(P)[:, None]
    i = np.arange(S)[None, :]
    decay = []
    for h in range(RET_HEADS):
        lg = np.log1p(-(2.0 ** (-5.0 - h)))
        decay.append(np.where(i >= j, np.exp(lg * np.maximum(i - j, 0)), 0.0) * (2 * P) ** -0.5)
    blocks = (np.arange(P)[:, None] // FOX_DIM == np.arange(P)[None, :] // FOX_DIM) / FOX_DIM
    avg = np.stack([blocks, np.full((P, P), 1.0 / (2 * P)), np.full((P, P), 1.0 / D)], 1)
    mask = np.where(np.arange(P)[None, :] > np.arange(P)[:, None], -NEG, 0.0)
    return {
        "cos": np.cos(ang), "sin": np.sin(ang), "decay": np.stack(decay), "avg": avg,
        "mask": mask, "ident": np.eye(P),
        "order4": np.broadcast_to(np.arange(4)[None, None, :] < np.arange(4)[None, :, None], (P, 4, 4)),
        "iota": np.broadcast_to(np.arange(IDX_COLS), (P, IDX_COLS)),
        "before": np.arange(P)[:, None] < np.arange(P)[None, :], "ones": np.ones((P, P)),
        "lanes": np.broadcast_to(np.arange(P), (P, P)), "block_at": np.broadcast_to(P * np.arange(IDX_COLS), (P, IDX_COLS)),
        "tokens": np.tile(np.arange(TT)[None, :] * P + np.arange(P)[:, None], (1, 2)),
    }


def kernel(**inputs):
    import concourse.bacc as bacc
    from concourse.bass_utils import run_bass_kernel_spmd

    a = {k: np.asarray(v) for k, v in inputs.items()}
    f32 = np.float32
    x, mem = a["x"][0], a["mem"][0]
    w_in = a["w_in"][0]
    names = ("rq", "rk", "rv", "rg", "fq", "fk", "fv", "ff", "mq", "g_ret", "g_fox", "g_mem")
    sizes = [D] * 7 + [FOX_HEADS] + [D] * 4
    at = np.concatenate([[0], np.cumsum(sizes)])
    w = {n: w_in[:, at[i]:at[i + 1]] for i, n in enumerate(names)}
    w["ff"] = np.concatenate([w["ff"], np.zeros((D, P - FOX_HEADS), f32)], 1)
    w["mk"], w["mv"] = a["w_mem_kv"][0][:, :D], a["w_mem_kv"][0][:, D:]
    w["o_ret"], w["o_fox"], w["o_mem"], w["out"] = (a[n][0] for n in ("w_o_ret", "w_o_fox", "w_o_mem", "w_out"))
    stream = np.empty((len(CHUNKS), P, 1024), f32)
    for c, (kind, i) in enumerate(CHUNKS):
        stream[c] = columns_of(w[kind], kind, i)

    def by_tile(v):
        return v.reshape(-1, P).T

    b_ff = np.zeros((P, 1), f32)
    b_ff[:FOX_HEADS, 0] = a["b_forget"][0]
    gains = np.concatenate([
        by_tile(a["norm_mix"][0]), by_tile(a["norm_mem"][0]), by_tile(a["norm_ffn"][0]),
        by_tile(np.concatenate([a["fox_q_norm"][0]] * 2)), by_tile(np.concatenate([a["fox_k_norm"][0]] * 2)),
        by_tile(a["mem_q_norm"][0]), by_tile(a["mem_k_norm"][0]), b_ff, b_ff], 1)
    arrays = {
        "x": x, "xT": x.T.reshape(KT, P, S).transpose(1, 0, 2), "memT": mem.T.reshape(KT, P, M).transpose(1, 0, 2),
        "w": stream, "gains": gains,
    }
    arrays |= {k: v.astype(f32) for k, v in tables().items()}
    experts = np.empty((N_EXPERTS, BLOCK_CHUNKS, P, 1024), f32)
    experts[:, :KT, :, :FF] = a["w_gate"][0].reshape(N_EXPERTS, KT, P, FF)
    experts[:, :KT, :, FF:] = a["w_up"][0].reshape(N_EXPERTS, KT, P, FF)
    experts[:, KT:] = a["w_down"][0].reshape(N_EXPERTS, FT, P, D)
    arrays |= {
        "experts": experts, "router": a["router_w"].reshape(KT, P, N_EXPERTS).transpose(1, 0, 2),
        "bias_b": np.tile(a["router_bias"], (P, TT)), "gain_b": np.tile(a["norm_ffn"][0], (P, 1)),
    }
    nc = bacc.Bacc("TRN2", target_bir_lowering=False, num_devices=1)
    sent, dram = {}, {}
    for name, v in arrays.items():
        v = np.ascontiguousarray(v)
        sent[f"in_{name}"] = v
        dram[name] = nc.dram_tensor(f"in_{name}", v.shape, mybir.dt.from_np(v.dtype), kind="ExternalInput").ap()
    dram["out"] = nc.dram_tensor("out_x", (S, D), F32, kind="ExternalOutput").ap()
    dram["h2"] = nc.dram_tensor("h2", (S, D), F32, kind="Internal").ap()
    dram["y"] = nc.dram_tensor("y", ((MAX_BLOCKS + 1) * P, D), F32, kind="Internal").ap()
    mixing_and_experts(nc, dram)
    r = run_bass_kernel_spmd(nc, [sent], core_ids=[0])
    return r.results[0]["out_x"].reshape(1, S, D)
```

```python
from contextlib import ExitStack

import numpy as np

import concourse.bass as bass
from concourse import mybir

F32 = mybir.dt.float32
F32R = mybir.dt.float32r
I32 = mybir.dt.int32
U32 = mybir.dt.uint32
ALU = mybir.AluOpType
ACT = mybir.ActivationFunctionType
AX = mybir.AxisListType

P = 128
D = 1024
S = 512
M = 256
KT = D // P
TT = S // P
MT = M // P
EPS = 1e-6
RET_HEADS, FOX_HEADS, MEM_HEADS = 4, 16, 4
PAIRS = FOX_HEADS // 2
FOX_DIM = D // FOX_HEADS
HEAD_TILES = 2
N_EXPERTS, N_GROUPS, PER_GROUP, FF = 16, 4, 4, 512
TOP_K = 2
MAX_BLOCKS = N_EXPERTS + TOP_K * S // P - 1
BLOCK_CHUNKS = KT + FF // P
NEG = -1.0e30

RAW, SPLIT = 4, 3
E_SPLIT = 4
FT = FF // P
IDX_COLS = MAX_BLOCKS + 1
AHEAD = 2


def chunk_list():
    out = [("fv", i) for i in range(8)] + [("ff", 0)]
    for p in range(PAIRS):
        out += [("fq", p), ("fk", p)]
    out += [("g_fox", n) for n in range(KT)] + [("o_fox", n) for n in range(KT)]
    out += [("rv", i) for i in range(8)]
    for h in range(RET_HEADS):
        out += [(k, HEAD_TILES * h + t) for k in ("rk", "rq", "rg") for t in range(HEAD_TILES)]
    out += [("g_ret", n) for n in range(KT)] + [("o_ret", n) for n in range(KT)]
    out += [("g_mem", n) for n in range(3)]
    out += [("mk", n) for n in range(KT)] + [("mv", i) for i in range(8)]
    out += [("mq", n) for n in range(KT)]
    out += [("g_mem", n) for n in range(3, KT)] + [("o_mem", n) for n in range(KT)]
    out += [("out", i) for i in range(8)]
    return out


CHUNKS = chunk_list()
NATURAL = ("fv", "rv", "mv", "out")
FIRST = {}
for _c, (_kind, _i) in enumerate(CHUNKS):
    FIRST.setdefault(_kind, _c)


def schedule():
    steps = {}

    def put(slot, *step):
        steps.setdefault(slot, []).append(step)

    base = 4 * FIRST["fq"]
    for p in range(PAIRS):
        put(base + 8 * p + 5, "norm", 2 * p)
        put(base + 8 * p + 9, "norm", 2 * p + 1)
        for half in range(2):
            put(base + 8 * p + 12 + 4 * half, "forget", 2 * p + half)
            put(base + 8 * p + 20 + 4 * half, "fox_pv", 2 * p + half)
        for j in range(8):
            put(base + 8 * p + 14 + j, "fox_score", 8 * p + j)
            put(base + 8 * p + 15 + j, "fox_scale", 8 * p + j)
            put(base + 8 * p + 16 + j, "fox_turn", 8 * p + j)
    base = 4 * FIRST["rk"]
    for h in range(RET_HEADS):
        b = base + 24 * h
        put(b + 9, "rotary", 2 * h)
        put(b + 17, "rotary", 2 * h + 1)
        for j in range(TT):
            put(b + 23 + 2 * j, "ret_score", TT * h + j)
        for e in range(HEAD_TILES):
            put(b + 31 + 2 * e, "ret_pv", HEAD_TILES * h + e)
        put(b + 35, "norm", 16 + h)
        put(b + 41, "ret_out", h)
    base = 4 * FIRST["o_ret"]
    for k in range(KT):
        put(base + 5 + k, "mem_sq", k)
    put(base + 13, "mem_norm", 0)
    for k in range(KT):
        put(4 * FIRST["g_mem"] + 1 + k, "mem_split", k)
    base = 4 * FIRST["mk"]
    for h in range(MEM_HEADS):
        put(base + 8 * h + 10, "norm", 20 + h)
    base = 4 * FIRST["mq"]
    for h in range(MEM_HEADS):
        b = base + 8 * h
        put(b + 9, "norm", 24 + h)
        for j in range(TT):
            put(b + 18 + j, "mem_score", TT * h + j)
            put(b + 19 + j, "mem_scale", TT * h + j)
            put(b + 20 + j, "mem_turn", TT * h + j)
        for e in range(HEAD_TILES):
            put(b + 25 + e, "mem_pv", HEAD_TILES * h + e)
    base = 4 * (FIRST["out"] + 4)
    for tt in range(TT):
        put(base + 4 + 2 * tt, "row_turn", tt)
        put(base + 6 + 2 * tt, "row_logit", tt)
    order = ("rotary", "norm", "forget", "fox_score", "mem_score", "ret_score", "fox_scale", "mem_scale",
             "fox_turn", "mem_turn", "fox_pv", "mem_pv", "ret_pv", "row_logit", "row_turn")
    for slot in steps:
        steps[slot].sort(key=lambda s: order.index(s[0]) if s[0] in order else 99)
    return steps


STEPS = schedule()
RET_AT = [sum(S - m * P for m in range(k)) for k in range(TT)]
FOX_NORMS, RET_NORMS, MK_NORMS, MQ_NORMS = range(0, 16), range(16, 20), range(20, 24), range(24, 28)


def norm_tiles(n):
    return 1 if n in FOX_NORMS else HEAD_TILES


def count_before(kinds, chunk):
    return sum(CHUNKS[c][0] in kinds for c in range(chunk))


def mixing_and_experts(nc, dram):
    assert D == 1024 and S == 512 and M == 256
    ctx = ExitStack()
    with ctx:
        def sb(name, shape, dt=F32):
            return ctx.enter_context(nc.sbuf_tensor(name, shape, dt))

        def sem(name):
            return ctx.enter_context(nc.semaphore(name))

        ps = ctx.enter_context(nc.psum_tensor("ps", [P, 8, 512], F32))
        STAT, SCORE, TURN, PV = 2, 3, 5, 7

        h_split = sb("h_split", [P, 2, KT, S], F32R)
        w_split = sb("w_split", [P, 2, SPLIT, 1024], F32R)
        o_split = sb("o_split", [P, 2, KT, S], F32R)
        id_r = sb("id_r", [P, P], F32R)
        mask_r = sb("mask_r", [P, P], F32R)
        sq_r = sb("sq_r", [P, 2, 2, 512], F32R)
        cum_r = sq_r[0:FOX_HEADS, :, 0, :]
        avg_r = sb("avg_r", [P, 3, P], F32R)
        mem_split = o_split[:].rearrange("p a k s -> p (a k s)")[:, 0:2 * KT * M].rearrange(
            "p (a k s) -> p a k s", a=2, k=KT)
        big = sb("big", [P, RAW * 1024 + 3 * 4096])
        raw = big[:, 0:RAW * 1024].rearrange("p (r n) -> p r n", r=RAW)
        fvm = big[:, RAW * 1024:RAW * 1024 + 4096]
        gat = big[:, RAW * 1024 + 4096:RAW * 1024 + 8192]
        vreg = big[:, RAW * 1024 + 8192:RAW * 1024 + 12288]
        fv = fvm.rearrange("p (t n) -> p t n", t=TT)
        merged = fvm.rearrange("p (k s) -> p k s", k=KT)
        gate = gat.rearrange("p (k s) -> p k s", k=KT)
        xT = gate
        x_nat = gat.rearrange("p (t n) -> p t n", t=TT)
        fox_pt = vreg.rearrange("p (b j i) -> p b j i", b=2, j=TT)
        x1 = vreg.rearrange("p (t n) -> p t n", t=TT)
        rv = vreg.rearrange("p (t n) -> p t n", t=TT)
        mkT = vreg[:, 0:KT * M].rearrange("p (k m) -> p k m", k=KT)
        memT = vreg[:, KT * M:2 * KT * M].rearrange("p (k m) -> p k m", k=KT)
        mv = vreg[:, KT * M:2 * KT * M].rearrange("p (t n) -> p t n", t=MT)
        work = sb("work", [P, 9984])
        used = [0]

        def carve(words):
            used[0] += words
            return work[:, used[0] - words:used[0]]

        sq = carve(1024).rearrange("p (b s) -> p b s", b=2)
        var, rstd, newton = carve(512), carve(512), carve(512)
        common = used[0]
        fox_raw = carve(1024).rearrange("p (b s) -> p b s", b=2)
        fox_q = carve(1024).rearrange("p (b s) -> p b s", b=2)
        fox_k = carve(1024).rearrange("p (b s) -> p b s", b=2)
        logits = carve(1024).rearrange("p (b s) -> p b s", b=2)
        prob = carve(1024).rearrange("p (b s) -> p b s", b=2)
        forget = carve(1024).rearrange("p (b s) -> p b s", b=2)
        used[0] = common
        ret_raw = carve(1024).rearrange("p (b s) -> p b s", b=2)
        ret_k = carve(1024).rearrange("p (b s) -> p b s", b=2)
        ret_q = carve(1024).rearrange("p (b s) -> p b s", b=2)
        ret_o = carve(1024).rearrange("p (b s) -> p b s", b=2)
        ret_p = carve(1280)
        rot = carve(512)
        cos = carve(512)
        sin = carve(512)
        decay = carve(512)
        used[0] = common
        mem_raw = carve(2048).rearrange("p (h b s) -> p h b s", h=2, b=2)
        mem_q = carve(2048).rearrange("p (h b s) -> p h b s", h=2, b=2)
        mem_p = carve(512).rearrange("p (b m) -> p b m", b=2)
        mem_pt = carve(1024).rearrange("p (j i) -> p j i", j=MT)
        rot2 = sb("rot2", [P, 512])
        ident = sb("ident", [P, P])
        mask_f = sb("mask_f", [P, P])
        avg = sb("avg", [P, 3, P])
        gains = sb("gains", [P, 2 * KT + 7])
        cst = sb("cst", [P, 4])
        stat = sb("stat", [P, 16])
        G_MIX, G_MEM, G_FQ, G_FK, G_MQ, G_MK, B_FF = 0, KT, 2 * KT, 2 * KT + 1, 2 * KT + 2, 2 * KT + 4, 2 * KT + 6

        ew_split = h_split[:].rearrange("p a k s -> p (a k s)").rearrange("p (a r n) -> p a r n", a=2, r=E_SPLIT)
        o_flat = o_split[:].rearrange("p a k s -> p (a k s)")
        xe_split = o_flat[:, 0:2 * KT * P].rearrange("p (a k s) -> p a k s", a=2, k=KT)
        he_split = o_flat[:, 2 * KT * P:2 * (KT + FT) * P].rearrange("p (a f s) -> p a f s", a=2, f=FT)
        e_raw = [big[:, (k - FT) % BLOCK_CHUNKS * 1024:((k - FT) % BLOCK_CHUNKS + 1) * 1024] for k in range(BLOCK_CHUNKS)]
        y_a = big[:, 0:4096].rearrange("p (t n) -> p t n", t=TT)
        y_b = big[:, 4096:8192].rearrange("p (t n) -> p t n", t=TT)
        h2 = fvm.rearrange("p (t n) -> p t n", t=TT)
        lane_hot = o_flat[:, 0:2 * TT * P].rearrange("p (j s) -> p j s", s=P)
        block_ids = o_flat[:, 1024:1024 + 2 * TT * IDX_COLS].rearrange("p (j b) -> p j b", b=IDX_COLS)
        before_r, ones_r = o_flat[:, 3072:3072 + P], o_flat[:, 3072 + P:3072 + 2 * P]
        sel_wide = o_flat[:, 3072 + 2 * P:3072 + 2 * P + (2 * TT + 1) * N_EXPERTS]
        sel_r = sel_wide[:, TT * N_EXPERTS:2 * TT * N_EXPERTS]
        used[0] = 0
        gain_b = carve(1024)
        scratch = carve(1024)
        xgT = carve(2048).rearrange("p (k s) -> p k s", s=S)
        used[0] -= 2048
        x_rows = carve(1024)
        h_act, h_e = carve(512), carve(512)
        y_rows = carve(1024)
        router = carve(KT * N_EXPERTS).rearrange("p (k e) -> p k e", k=KT)
        order4 = carve(16).rearrange("p (b a) -> p b a", b=4)
        iota = carve(IDX_COLS)
        bias_b = carve(TT * N_EXPERTS)
        before, ones = carve(P), carve(P)
        lanes, block_at = carve(P), carve(IDX_COLS)
        token_f = carve(2 * TT)
        sums = carve(6 * TT).rearrange("p (a t) -> p a t", a=6)
        r64 = [carve(TT * N_EXPERTS) for _ in range(10)]
        r256a, r256b = carve(256), carve(256)
        r384 = carve(IDX_COLS * N_EXPERTS)
        r16 = [carve(16) for _ in range(12)]
        token_w = carve(2 * TT).rearrange("p (a t) -> p a t", a=2)
        assert used[0] <= 9984
        y_slot_i = sb("y_slot_i", [P, 2, TT], I32)
        blocks_i = sb("blocks_i", [P, IDX_COLS + 1], I32)
        rows_i = sb("rows_i", [P, IDX_COLS], I32)
        row_i = sb("row_i", [P, 1], I32)

        consts_in, avg_in, mem_in, xn_in = sem("consts_in"), sem("avg_in"), sem("mem_in"), sem("xn_in")
        x_in = [sem(f"x_in{k}") for k in range(4)]
        rot_in, decay_in = sem("rot_in"), sem("decay_in")
        landed = [sem(f"landed{i}") for i in range(RAW)]
        hi_ready, lo_ready = sem("hi_ready"), sem("lo_ready")
        w_used = sem("w_used")
        tile_act, tile_dve = sem("tile_act"), sem("tile_dve")
        nat_read = sem("nat_read")
        x_sq, x_sum = sem("x_sq"), sem("x_sum")
        sq_ready = sem("sq_ready")
        stat_ready, stat_read = sem("stat_ready"), sem("stat_read")
        seed_ready, normed = sem("seed_ready"), sem("normed")
        h_f, h_hi, h_lo = sem("h_f"), sem("h_hi"), sem("h_lo")
        gate_log, cum_ready = sem("gate_log"), sem("cum_ready")
        sc_done, sc_read = sem("sc_done"), sem("sc_read")
        mem_min = sem("mem_min")
        prob_ready, prob_scaled = sem("prob_ready"), sem("prob_scaled")
        turned, turn_read = sem("turned"), sem("turn_read")
        pv_done = sem("pv_done")
        o_hi, o_lo = sem("o_hi"), sem("o_lo")
        rotated, rotated_dve = sem("rotated"), sem("rotated_dve")
        ret_sq, ret_gated = sem("ret_sq"), sem("ret_gated")
        sq_hi, sq_lo = sem("sq_hi"), sem("sq_lo")
        merge_done = sem("merge_done")
        m_hi, m_lo = sem("m_hi"), sem("m_lo")
        out_tile = sem("out_tile")
        x1_ready = sem("x1_ready")
        tab_in = sem("tab_in")
        row_sq, row_sum, row_seed, row_rstd = sem("row_sq"), sem("row_sum"), sem("row_seed"), sem("row_rstd")
        xg_ready, xg_turned, xg_copied = sem("xg_ready"), sem("xg_turned"), sem("xg_copied")
        h2_ready, h2_stored = sem("h2_ready"), sem("h2_stored")
        logit_done, logit_ready, score_ready = sem("logit_done"), sem("logit_ready"), sem("score_ready")
        tab_r, sel_ready, pos_done = sem("tab_r"), sem("sel_ready"), sem("pos_done")
        hot_ready, rows_done, rows_ready = sem("hot_ready"), sem("rows_done"), sem("rows_ready")
        table_ready = sem("table_ready")
        e_landed = [sem(f"e_landed{k}") for k in range(BLOCK_CHUNKS)]
        e_hi = sem("e_hi")
        e_lo = sem("e_lo")
        e_used = sem("e_used")
        row_copied, x_landed = sem("row_copied"), sem("x_landed")
        xe_turned, xe_hi, xe_lo = sem("xe_turned"), sem("xe_hi"), sem("xe_lo")
        silu_done, he_ready, he_turned, he_hi, he_lo = (
            sem("silu_done"), sem("he_ready"), sem("he_turned"), sem("he_hi"), sem("he_lo"))
        y_act, y_dve = sem("y_act"), sem("y_dve")
        y_stored = sem("y_stored")
        y_filled = sem("y_filled")
        ya_in, yb_in = [sem(f"ya_in{tt}") for tt in range(TT)], [sem(f"yb_in{tt}") for tt in range(TT)]
        gathers = sem("gathers")
        mixed, token_out = sem("mixed"), sem("token_out")
        cum_zero, id_ready = sem("cum_zero"), sem("id_ready")
        act_chain, dve_chain, pool_chain = sem("act_chain"), sem("dve_chain"), sem("pool_chain")
        out_done = sem("out_done")

        READ_BY_ACT = ("rk", "rq", "rg", "g_fox", "g_ret", "g_mem", "ff")
        READ_BY_DVE = ("fq", "fk", "mq", "mk", "o_fox", "o_ret", "o_mem")
        tiles = [c for c, (kind, _) in enumerate(CHUNKS) if kind not in NATURAL]
        tile_no = {c: i for i, c in enumerate(tiles)}
        fox_merged = count_before(READ_BY_DVE, FIRST["o_fox"] + KT)
        steps = [st for s in sorted(STEPS) for st in STEPS[s]]

        def numbers(names):
            return {st: i for i, st in enumerate(x for x in steps if x[0] in names)}

        stat_no = {st: i + 1 for st, i in numbers(("norm", "forget", "mem_norm")).items()}
        stat_no[("x", 0)] = 0
        sum_no = numbers(("norm", "forget"))
        norm_order = [("x", 0)] + [st for st in steps if st[0] in ("norm", "mem_norm")]
        norm_no = {st: i for i, st in enumerate(norm_order)}
        normed_by = {}
        for st in norm_order:
            normed_by[st] = (norm_tiles(st[1]) if st[0] == "norm" else 1) + (
                normed_by[norm_order[norm_no[st] - 1]] if norm_no[st] else 0)
        sc_no = numbers(("fox_score", "ret_score", "mem_score"))
        soft = {("fox", j): j for j in range(FOX_HEADS * TT)}
        soft |= {("mem", j): FOX_HEADS * TT + j for j in range(MEM_HEADS * TT)}
        sq_before = {n: sum(norm_tiles(m) for m in range(n)) for n in range(MQ_NORMS[-1] + 2)}
        last_slot = 4 * len(CHUNKS)
        assert max(STEPS) < last_slot

        def lhs_of(kind):
            return {"mk": mem_split, "mv": mem_split, "o_fox": o_split, "o_ret": o_split,
                    "o_mem": o_split}.get(kind, h_split)

        def norm_io(n):
            if n in FOX_NORMS:
                p = n // 2
                return [fox_raw[:, n % 2, :]], [(fox_q if n % 2 == 0 else fox_k)[:, p % 2, :]], S
            if n in RET_NORMS:
                return [ret_o[:, e, :] for e in range(2)], [ret_o[:, e, :] for e in range(2)], S
            if n in MK_NORMS:
                h = n - MK_NORMS[0]
                return ([mem_raw[:, n % 2, e, 0:M] for e in range(2)],
                        [mkT[:, HEAD_TILES * h + e, :] for e in range(2)], M)
            return [mem_raw[:, n % 2, e, :] for e in range(2)], [mem_q[:, n % 2, e, :] for e in range(2)], S

        def norm_of_chunk(kind, i):
            if kind in ("fq", "fk"):
                return 2 * i + (kind == "fk"), 0
            return (MK_NORMS if kind == "mk" else MQ_NORMS)[i // 2], i % 2

        def chunk_of_norm(n):
            if n in FOX_NORMS:
                return FIRST["fq"] + n
            return (FIRST["mk"] - HEAD_TILES * MK_NORMS[0] if n in MK_NORMS else FIRST["mq"] - HEAD_TILES * MQ_NORMS[0]
                    ) + HEAD_TILES * n + 1

        def squares_by(n, e):
            return sq_before[n] + e + 1 - (HEAD_TILES * RET_HEADS if n > RET_NORMS[-1] else 0)

        def split_squares_by(n, e):
            return RET_HEADS * HEAD_TILES + KT + HEAD_TILES * (n - MK_NORMS[0]) + e + 1

        def landed_by(b, k):
            return b * 16 + (16 if k >= FT else 0)

        block = ctx.enter_context(nc.Block())

        @block.sync
        def _(sp):
            for k in range(4):
                sp.dma_start(xT[:, 2 * k:2 * k + 2, :], dram["xT"][:, 2 * k:2 * k + 2, :]).then_inc(x_in[k], 16)
            for dst, name in ((gains, "gains"), (ident, "ident"), (mask_f, "mask")):
                sp.dma_start(dst[:], dram[name]).then_inc(consts_in, 16)
            for c in range(len(CHUNKS)):
                if c >= RAW:
                    sp.wait_ge(lo_ready, c - RAW + 1)
                sp.dma_start(raw[:, c % RAW, :], dram["w"][c]).then_inc(landed[c % RAW], 16)
                kind, i = CHUNKS[c]
                n = c - FIRST["g_ret"]
                if 0 <= n < MAX_BLOCKS - TOP_K * S // P:
                    first = (TOP_K * S // P + 1 + n) * P
                    sp.dma_start(dram["y"][first:first + P, :], dram["w"][c]).then_inc(y_filled, 16)
                if kind == "o_ret" and i == 1:
                    sp.wait_ge(pv_done, FOX_HEADS + RET_HEADS * HEAD_TILES)
                    sp.dma_start(memT, dram["memT"]).then_inc(mem_in, 16)
                if kind == "out" and i == 5:
                    sp.wait_ge(merge_done, 2 * KT)
                    sp.dma_start(x_nat, dram["x"].rearrange("(t p) n -> p t n", p=P)).then_inc(xn_in, 16)
            sp.wait_ge(o_lo, 3 * KT)
            for dst, name in ((router, "router"), (order4, "order4"), (iota, "iota"), (bias_b, "bias_b"),
                              (before, "before"), (ones, "ones"), (lanes, "lanes"), (block_at, "block_at"),
                              (token_f, "tokens"), (gain_b, "gain_b")):
                sp.dma_start(dst, dram[name]).then_inc(tab_in, 16)
            sp.wait_ge(lo_ready, len(CHUNKS))
            for k in range(RAW):
                sp.dma_start(e_raw[FT + k], dram["experts"][0, k]).then_inc(e_landed[FT + k], 16)
            for tt in range(TT):
                sp.wait_ge(h2_ready, tt + 1)
                sp.dma_start(dram["h2"][tt * P:(tt + 1) * P, :], h2[:, tt, :]).then_inc(h2_stored, 16)
            sp.wait_ge(h2_stored, 16 * TT)
            for k in range(RAW, KT):
                sp.dma_start(e_raw[FT + k], dram["experts"][0, k]).then_inc(e_landed[FT + k], 16)
            sp.wait_ge(e_lo, FT)
            turns = sp.value_load(blocks_i[0:1, IDX_COLS:IDX_COLS + 1], min_val=TOP_K * S // P - 1, max_val=MAX_BLOCKS - 1)
            n_blocks = turns + 1
            with sp.Fori(0, turns) as turn:
                b = turn + 1
                expert = sp.value_load(blocks_i[0:1, bass.ds(b, 1)], min_val=0, max_val=N_EXPERTS - 1)
                last_expert = sp.value_load(blocks_i[0:1, bass.ds(turn, 1)], min_val=0, max_val=N_EXPERTS - 1)
                for k in range(BLOCK_CHUNKS):
                    sp.wait_ge(e_lo, turn * BLOCK_CHUNKS + (k + 1))
                    sp.dma_start(e_raw[k], dram["experts"][expert if k < KT else last_expert, k]).then_inc(e_landed[k], 16)
            last_expert = sp.value_load(blocks_i[0:1, bass.ds(turns, 1)], min_val=0, max_val=N_EXPERTS - 1)
            for k in range(FT):
                sp.wait_ge(e_lo, turns * BLOCK_CHUNKS + (k + 1))
                sp.dma_start(e_raw[k], dram["experts"][last_expert, KT + k]).then_inc(e_landed[k], 16)
            for tt in range(TT):
                sp.wait_ge(mixed, tt + 1)
                sp.dma_start(dram["out"][tt * P:(tt + 1) * P, :], x1[:, tt, :]).then_inc(out_done, 16)
            sp.wait_ge(out_done, 16 * TT)

        @block.tensor
        def _(pe):
            mm = nc.tensor.matmul

            def before_chunk(c):
                kind, i = CHUNKS[c]
                pe.wait_ge(lo_ready, c + 1)
                if kind in NATURAL:
                    if kind == "fv" and i == 0:
                        pe.wait_ge(stat_read, 1)
                    if kind == "rv" and i == 0:
                        pe.wait_ge(tile_dve, count_before(READ_BY_DVE, c))
                    if kind == "mv" and i == 0:
                        pe.wait_ge(sc_read, FOX_HEADS * TT + RET_HEADS * TT)
                        pe.wait_ge(ret_sq, RET_HEADS * HEAD_TILES)
                        pe.wait_ge(ret_gated, RET_HEADS * HEAD_TILES)
                    if kind == "out" and i == 0:
                        pe.wait_ge(tile_dve, count_before(READ_BY_DVE, c))
                    return
                t = tile_no[c]
                if t >= 2:
                    a, d = (count_before(k, tiles[t - 2] + 1) for k in (READ_BY_ACT, READ_BY_DVE))
                    if a:
                        pe.wait_ge(tile_act, a)
                    if d:
                        pe.wait_ge(tile_dve, d)
                if kind == "ff":
                    pe.wait_ge(nat_read, 8)
                if kind == "rk" and i == 0:
                    pe.wait_ge(nat_read, 16)
                if kind == "mk" and i == 0:
                    pe.wait_ge(h_lo, 2 * KT)
                if kind in ("o_fox", "o_ret", "o_mem") and i == 0:
                    pe.wait_ge(o_lo, KT * (1 + ("o_fox", "o_ret", "o_mem").index(kind)))

            def quarter(c, q):
                kind, i = CHUNKS[c]
                x = lhs_of(kind)
                whi, wlo = w_split[:, 0, c % SPLIT, :], w_split[:, 1, c % SPLIT, :]
                if q == 0:
                    before_chunk(c)
                if kind == "fv" and i < 4 and q % 2 == 0:
                    pe.wait_ge(h_lo, 2 * i + q // 2 + 1)
                if kind == "out" and i < 4 and q % 2 == 0:
                    pe.wait_ge(m_lo, 2 * i + q // 2 + 1 if i < 3 else KT)
                if kind == "out" and i % 4 == 3:
                    bank = 4 * (i // 4) + q
                    for kk in range(2):
                        for n, (a, w) in enumerate(((0, whi), (0, wlo), (1, whi))):
                            last = mm(ps[:, bank, :], x[:, a, 6 + kk, q * P:(q + 1) * P], w[:, kk * 512:(kk + 1) * 512],
                                      start=False, stop=(kk == 1 and n == 2))
                    if q < 3:
                        last.then_inc(out_tile, 1)
                elif kind in NATURAL:
                    g, kp, kk, half = i // 4, i % 4, q // 2, q % 2
                    rows = MT if kind == "mv" else TT
                    for tt in range(half * rows // 2, (half + 1) * rows // 2):
                        bank = SCORE + 2 * g + tt if kind == "mv" else 4 * g + tt
                        for n, (a, w) in enumerate(((0, whi), (0, wlo), (1, whi))):
                            last = mm(ps[:, bank, :], x[:, a, 2 * kp + kk, tt * P:(tt + 1) * P],
                                      w[:, kk * 512:(kk + 1) * 512],
                                      start=(kp == 0 and kk == 0 and n == 0), stop=(kp == 3 and kk == 1 and n == 2))
                else:
                    out = ps[:, tile_no[c] % 2, 0:M if kind == "mk" else S]
                    for k in (2 * q, 2 * q + 1):
                        for n, (w, a) in enumerate(((whi, 0), (wlo, 0), (whi, 1))):
                            last = mm(out, w[:, k * P:(k + 1) * P], x[:, a, k, :],
                                      start=(k == 0 and n == 0), stop=(k == KT - 1 and n == 2))
                if q == 3:
                    last.then_inc(w_used, 1)

            def turn_prob(n, tiles):
                for k in range(tiles):
                    last = nc.tensor.transpose(ps[:, TURN + n % 2, k * P:(k + 1) * P],
                                               (prob if n < soft["mem", 0] else mem_p)[:, n % 2, k * P:(k + 1) * P], ident[:])
                last.then_inc(turned, 1)

            def row_turn(g, tt):
                n = g * TT + tt
                pe.wait_ge(x1_ready, TT)
                pe.wait_ge(xg_ready, n + 1)
                if n >= 3:
                    pe.wait_ge(xg_copied, n - 2)
                for k in range(4):
                    last = nc.tensor.transpose(ps[:, n % 3, k * P:(k + 1) * P], h2[:, tt, (4 * g + k) * P:(4 * g + k + 1) * P],
                                               ident[:])
                last.then_inc(xg_turned, 1)

            def row_logit(g, tt):
                n = g * TT + tt
                pe.wait_ge(xg_copied, n + 1)
                pe.wait_ge(tab_in, 16 * 10)
                for k in range(4):
                    last = mm(ps[:, 3, n * N_EXPERTS:(n + 1) * N_EXPERTS], xgT[:, k, tt * P:(tt + 1) * P],
                              router[:, 4 * g + k, :], start=(k == 0), stop=(k == 3))
                last.then_inc(logit_done, 1)

            pe.wait_ge(avg_in, 16)
            for k in range(KT):
                pe.wait_ge(x_sq, k + 1)
                mm(ps[:, STAT, :], avg[:, 2, :], sq[:, k % 2, :], start=(k == 0), stop=(k == KT - 1)).then_inc(x_sum, 1)
            pe.wait_ge(consts_in, 16 * 3)
            pe.wait_ge(id_ready, 3)
            for slot in range(last_slot):
                quarter(slot // 4, slot % 4)
                for st in STEPS.get(slot, ()):
                    what, j = st
                    if what == "row_turn":
                        row_turn(0, j)
                    elif what == "row_logit":
                        row_logit(0, j)
                    elif what == "mem_sq":
                        if j == 0:
                            pe.wait_ge(stat_read, stat_no["mem_norm", 0])
                        pe.wait_ge(sq_lo, RET_HEADS * HEAD_TILES + j + 1)
                        for a in range(2):
                            last = mm(ps[:, STAT, 0:M], avg_r[:, 2, :], sq_r[:, a, j % 2, 0:M],
                                      start=(j == 0 and a == 0), stop=(j == KT - 1 and a == 1))
                        last.then_inc(x_sum, 1)
                    elif what == "norm":
                        width, t = norm_io(j)[2], norm_tiles(j)
                        pe.wait_ge(stat_read, stat_no[st])
                        if j in RET_NORMS:
                            pe.wait_ge(sq_lo, HEAD_TILES * (j - RET_NORMS[0] + 1))
                        elif j in FOX_NORMS:
                            pe.wait_ge(sq_ready, squares_by(j, 0))
                        else:
                            pe.wait_ge(sq_lo, split_squares_by(j, t - 1))
                        for e in range(t):
                            if j in FOX_NORMS:
                                last = mm(ps[:, STAT, :], avg[:, 0, :], sq[:, j % 2, :], start=True, stop=True)
                                continue
                            for a in range(2):
                                last = mm(ps[:, STAT, 0:width], avg_r[:, 1, :], sq_r[:, a, e, 0:width],
                                          start=(e == 0 and a == 0), stop=(e == t - 1 and a == 1))
                        last.then_inc(stat_ready, 1)
                    elif what == "forget":
                        pe.wait_ge(stat_read, stat_no[st])
                        pe.wait_ge(cum_ready, 1)
                        for a in range(2):
                            last = mm(ps[:, STAT, :], id_r[0:FOX_HEADS, j:j + 1].to_broadcast([FOX_HEADS, P]), cum_r[:, a, :],
                                      start=(a == 0), stop=(a == 1))
                        last.then_inc(stat_ready, 1)
                    elif what == "fox_score":
                        head, r = j // TT, j % TT
                        pair, rows = head // 2, slice(FOX_DIM * (head % 2), FOX_DIM * (head % 2) + FOX_DIM)
                        if j >= 2:
                            pe.wait_ge(sc_read, j - 1)
                        pe.wait_ge(normed, normed_by[("norm", 2 * pair + 1)])
                        out = ps[:, SCORE + j % 2, 0:P * (r + 1)]
                        mm(out, fox_q[rows, pair % 2, r * P:(r + 1) * P], fox_k[rows, pair % 2, 0:P * (r + 1)],
                           start=True, stop=True)
                        mm(out[:, P * r:], id_r[:], mask_r[:], start=False, stop=True,
                           skip_group_check=True).then_inc(sc_done, 1)
                    elif what == "fox_turn":
                        r = j % TT
                        if j >= 2:
                            pe.wait_ge(turn_read, j - 1)
                        pe.wait_ge(prob_scaled, j + 1)
                        turn_prob(j, r + 1)
                    elif what == "fox_pv":
                        rows = slice(FOX_DIM * (j % 2), FOX_DIM * (j % 2) + FOX_DIM)
                        if j >= 2 and j % 2 == 0:
                            pe.wait_ge(o_lo, j // 2)
                        pe.wait_ge(turn_read, TT * (j + 1))
                        for k in reversed(range(TT)):
                            last = mm(ps[rows, PV, k * P:], fv[:, k, j * FOX_DIM:(j + 1) * FOX_DIM],
                                      fox_pt[:, j % 2, k, k * P:], start=(k == TT - 1), stop=(k == 0),
                                      skip_group_check=True)
                        last.then_inc(pv_done, 1)
                    elif what == "ret_score":
                        h, k = j // TT, j % TT
                        n = sc_no[st]
                        pe.wait_ge(sc_read, n - 1)
                        pe.wait_ge(rotated, 2 * h + 2)
                        pe.wait_ge(rotated_dve, 2 * h + 2)
                        for e in range(HEAD_TILES):
                            last = mm(ps[:, SCORE + n % 2, 0:S - k * P], ret_k[:, e, k * P:(k + 1) * P],
                                      ret_q[:, e, k * P:], start=(e == 0), stop=(e == HEAD_TILES - 1))
                        last.then_inc(sc_done, 1)
                    elif what == "ret_pv":
                        h, e = j // 2, j % 2
                        if h == 0:
                            pe.wait_ge(o_lo, KT)
                            pe.wait_ge(turn_read, FOX_HEADS * TT)
                        else:
                            pe.wait_ge(ret_sq, j - 1)
                            pe.wait_ge(ret_gated, j - 1)
                        pe.wait_ge(sc_read, FOX_HEADS * TT + TT * (h + 1))
                        for k in reversed(range(TT)):
                            last = mm(ps[:, PV if e == 0 else TURN, k * P:], rv[:, k, j * P:(j + 1) * P],
                                      ret_p[:, RET_AT[k]:RET_AT[k] + S - k * P],
                                      start=(k == TT - 1), stop=(k == 0), skip_group_check=True)
                        last.then_inc(pv_done, 1)
                    elif what == "mem_score":
                        h, r = j // TT, j % TT
                        n = sc_no[st]
                        pe.wait_ge(sc_read, n - 1)
                        if j == 0:
                            pe.wait_ge(nat_read, 20)
                        pe.wait_ge(normed, normed_by[("norm", MQ_NORMS[h])])
                        for e in range(HEAD_TILES):
                            last = mm(ps[:, SCORE + n % 2, 0:M], mem_q[:, (j // TT) % 2, e, r * P:(r + 1) * P],
                                      mkT[:, HEAD_TILES * h + e, :], start=(e == 0), stop=(e == HEAD_TILES - 1))
                        last.then_inc(sc_done, 1)
                    elif what == "mem_turn":
                        n = soft["mem", j]
                        pe.wait_ge(turn_read, n - 1)
                        pe.wait_ge(prob_scaled, n + 1)
                        turn_prob(n, MT)
                    elif what == "mem_pv":
                        pe.wait_ge(o_lo, 2 * KT + j)
                        pe.wait_ge(turn_read, FOX_HEADS * TT + TT * (j // 2 + 1))
                        for k in range(MT):
                            last = mm(ps[:, PV, :], mv[:, k, j * P:(j + 1) * P], mem_pt[:, k, :],
                                      start=(k == 0), stop=(k == MT - 1))
                        last.then_inc(pv_done, 1)

            for tt in range(TT):
                row_turn(1, tt)
                if tt:
                    row_logit(1, tt - 1)
            row_logit(1, TT - 1)
            pe.wait_ge(tab_r, 2)
            pe.wait_ge(sel_ready, 1)
            for d in range(TT + 1):
                first = (TT - d) * N_EXPERTS
                last = mm(ps[:, 5, 0:(TT + 1) * N_EXPERTS], ones_r if d else before_r,
                          sel_wide[:, first:first + (TT + 1) * N_EXPERTS], start=(d == 0), stop=(d == TT))
            last.then_inc(pos_done, 1)
            for j in range(2 * TT):
                pe.wait_ge(hot_ready, j + 1)
                last = mm(ps[:, 4, 0:IDX_COLS], lane_hot[:, j, :], block_ids[:, j, :], start=(j == 0), stop=(j == 2 * TT - 1))
            last.then_inc(rows_done, 1)

            def turn_rows():
                for k in range(KT):
                    last = nc.tensor.transpose(ps[:, 2 + k // 4, k % 4 * P:(k % 4 + 1) * P],
                                               x_rows[:, k * P:(k + 1) * P], ident[:])
                last.then_inc(xe_turned, 1)

            pe.wait_ge(x_landed, 16)
            pe.wait_ge(e_lo, FT)
            turn_rows()
            turns = pe.value_load(blocks_i[0:1, IDX_COLS:IDX_COLS + 1], min_val=TOP_K * S // P - 1, max_val=MAX_BLOCKS - 1)
            n_blocks = turns + 1

            def use_chunk(at, slot, x, kk, depth, first_bank):
                pe.wait_ge(e_lo, at + (slot + 1))
                whi, wlo = ew_split[:, 0, slot % E_SPLIT, :], ew_split[:, 1, slot % E_SPLIT, :]
                for n, (a, w) in enumerate(((0, whi), (0, wlo), (1, whi))):
                    for half in range(2):
                        last = mm(ps[:, first_bank + half, :], x[:, a, kk, :], w[:, half * 512:(half + 1) * 512],
                                  start=(kk == 0 and n == 0), stop=(kk == depth - 1 and n == 2))
                last.then_inc(e_used, 1)

            def turn_hidden(b):
                pe.wait_ge(he_ready, b + 1)
                for f_ in range(FT):
                    last = nc.tensor.transpose(ps[:, 4, f_ * P:(f_ + 1) * P], h_e[:, f_ * P:(f_ + 1) * P], ident[:])
                last.then_inc(he_turned, 1)

            pe.wait_ge(xe_lo, 1)
            for k in range(KT):
                use_chunk(0, FT + k, xe_split, k, KT, 0)
            pe.wait_ge(x_landed, 32)
            turn_rows()
            turn_hidden(0)
            with pe.Fori(0, turns) as turn:
                b = turn + 1
                pe.wait_ge(xe_lo, b + 1)
                for k in range(KT):
                    use_chunk(b * BLOCK_CHUNKS, k, xe_split, k, KT, 0)
                pe.wait_ge(x_landed, b * 16 + 32)
                turn_rows()
                pe.wait_ge(he_lo, b)
                pe.wait_ge(y_act, b)
                pe.wait_ge(y_dve, b)
                for k in range(KT, BLOCK_CHUNKS):
                    use_chunk(b * BLOCK_CHUNKS, k, he_split, k - KT, FT, 5)
                turn_hidden(b)
            pe.wait_ge(he_lo, n_blocks)
            pe.wait_ge(y_act, n_blocks)
            pe.wait_ge(y_dve, n_blocks)
            for k in range(FT):
                use_chunk(n_blocks * BLOCK_CHUNKS, k, he_split, k, FT, 5)

        @block.scalar
        def _(act):
            links = [0]

            def link(ins):
                links[0] += 1
                ins.then_inc(act_chain, 1)
                act.wait_ge(act_chain, links[0])

            table = [None]

            def run(out, in_, func, **kw):
                need = "natural_log_exp_and_others" if func in (ACT.Exp, ACT.Ln) else (
                    None if func not in (ACT.Sigmoid, ACT.Silu) else str(func))
                if need and need != table[0]:
                    table[0] = need
                    if func in (ACT.Exp, ACT.Ln):
                        nc.scalar.preload_act_table_set(need)
                return nc.scalar.activation(out, in_, func, **kw)

            eps, one = cst[:, 0:1], cst[:, 1:2]

            def split_hi(c):
                act.wait_ge(landed[c % RAW], 16 * (c // RAW + 1))
                if c >= SPLIT:
                    act.wait_ge(w_used, c - SPLIT + 1)
                run(w_split[:, 0, c % SPLIT, :], raw[:, c % RAW, :], ACT.Copy).then_inc(hi_ready, 1)

            def square_hi(e, width):
                run(sq_r[:, 0, e, 0:width], sq[:, e, 0:width], ACT.Copy).then_inc(sq_hi, 1)

            def squares_of_x():
                for k in range(KT):
                    if k >= 2:
                        act.wait_ge(x_sum, k - 1)
                    if k % 2 == 0:
                        act.wait_ge(x_in[k // 2], 16)
                    run(sq[:, k % 2, :], xT[:, k, :], ACT.Square).then_inc(x_sq, 1)
                    if k - 5 in range(AHEAD):
                        split_hi(k - 5)

            def seed(st, width):
                if st != ("x", 0):
                    act.wait_ge(normed, normed_by[norm_order[norm_no[st] - 1]])
                if st[0] == "norm":
                    act.wait_ge(stat_ready, sum_no[st] + 1)
                else:
                    act.wait_ge(x_sum, KT * (1 + (st[0] == "mem_norm")))
                run(var[:, 0:width], ps[:, STAT, 0:width], ACT.Identity, bias=eps).then_inc(stat_read, 1)
                act.wait_ge(stat_read, stat_no[st] + 1)
                link(run(rstd[:, 0:width], var[:, 0:width], ACT.Ln))
                run(rstd[:, 0:width], rstd[:, 0:width], ACT.Exp, scale=-0.5).then_inc(seed_ready, 1)

            def split_normed(k, width, tmp, dst, before):
                act.wait_ge(h_f, before + k + 1)
                run(dst[:, 0, k, :], tmp[:, k % 2, 0:width], ACT.Copy).then_inc(h_hi, 1)

            def after_chunk(c):
                kind, i = CHUNKS[c]
                if kind in NATURAL:
                    g, kp = i // 4, i % 4
                    if kp < 3 or kind == "out":
                        return
                    act.wait_ge(w_used, c + 1)
                    if kind == "mv":
                        if g == 0:
                            act.wait_ge(h_lo, 2 * KT)
                        run(mv[:, 0, g * 512:(g + 1) * 512], ps[:, SCORE + 2 * g, :], ACT.Copy).then_inc(nat_read, 1)
                    else:
                        dst = fv if kind == "fv" else rv
                        for tt in (0, 1):
                            run(dst[:, tt, g * 512:(g + 1) * 512], ps[:, 4 * g + tt, :], ACT.Copy).then_inc(nat_read, 1)
                    return
                src = ps[:, tile_no[c] % 2, 0:M if kind == "mk" else S]
                if kind in ("fq", "fk", "mq", "mk"):
                    n, e = norm_of_chunk(kind, i)
                    act.wait_ge(w_used, c + 1)
                    if n in FOX_NORMS and n < 2:
                        act.wait_ge(x_sum, KT)
                    elif n == MK_NORMS[0]:
                        act.wait_ge(x_sum, 2 * KT)
                    else:
                        act.wait_ge(stat_ready, sum_no["norm", n - 2 if n in FOX_NORMS else n - 1] + 1)
                    width = M if kind == "mk" else S
                    run(sq[:, n % 2 if n in FOX_NORMS else e, 0:width], src, ACT.Square).then_inc(sq_ready, 1)
                    if n not in FOX_NORMS:
                        act.wait_ge(sq_ready, squares_by(n, e))
                        square_hi(e, width)
                elif kind == "ff":
                    act.wait_ge(w_used, c + 1)
                    act.wait_ge(h_lo, KT)
                    z, az, e = logits[0:FOX_HEADS, 0, :], logits[0:FOX_HEADS, 1, :], prob[0:FOX_HEADS, 0, :]
                    run(z, src[0:FOX_HEADS, :], ACT.Identity, bias=gains[0:FOX_HEADS, B_FF:B_FF + 1]).then_inc(tile_act, 1)
                    act.wait_ge(tile_act, 1)
                    link(run(az, z, ACT.Abs))
                    link(run(e, az, ACT.Exp, scale=-1.0))
                    run(e, e, ACT.Ln, bias=one[0:FOX_HEADS, :]).then_inc(gate_log, 1)
                elif kind in ("rk", "rq"):
                    n = 2 * (i // 2) + (kind == "rq")
                    act.wait_ge(w_used, c + 1)
                    if n:
                        act.wait_ge(rotated, n)
                        act.wait_ge(rotated_dve, n)
                    else:
                        act.wait_ge(tile_dve, fox_merged)
                    run(ret_raw[:, i % 2, :], src, ACT.Copy).then_inc(tile_act, 1)
                elif kind == "rg":
                    act.wait_ge(w_used, c + 1)
                    if i >= 2:
                        act.wait_ge(o_lo, KT + i // 2 * 2)
                    run(ret_o[:, i % 2, :], src, ACT.Silu).then_inc(tile_act, 1)
                elif kind in ("g_fox", "g_ret", "g_mem"):
                    act.wait_ge(w_used, c + 1)
                    b = ("g_fox", "g_ret", "g_mem").index(kind)
                    if b == 2:
                        act.wait_ge(merge_done, KT)
                    elif b:
                        act.wait_ge(tile_dve, fox_merged)
                    else:
                        act.wait_ge(h_lo, KT)
                    run(gate[:, i, :], src, ACT.Sigmoid).then_inc(tile_act, 1)
                elif kind == "o_mem":
                    act.wait_ge(merge_done, KT + i + 1)
                    run(h_split[:, 0, i, :], merged[:, i, :], ACT.Copy).then_inc(m_hi, 1)

            def row_square(g, tt):
                n = g * TT + tt
                act.wait_ge(x1_ready, n + 1)
                if n:
                    act.wait_ge(row_sq, n)
                else:
                    act.wait_ge(o_lo, 3 * KT)
                run(scratch[:, 0:512], x1[:, tt, g * 512:(g + 1) * 512], ACT.Square,
                    accum_out=sums[:, 4 * g, tt:tt + 1]).then_inc(row_sq, 1)

            def row_copy(g, tt):
                n = g * TT + tt
                act.wait_ge(xg_turned, n + 1)
                if g:
                    act.wait_ge(logit_done, tt + 1)
                run(xgT[:, :, tt * P:(tt + 1) * P], ps[:, n % 3, :].rearrange("p (k s) -> p k s", s=P),
                    ACT.Copy).then_inc(xg_copied, 1)

            nc.scalar.dma_start(avg[:], dram["avg"]).then_inc(avg_in, 16)
            nc.scalar.preload_act_table_set("natural_log_exp_and_others")
            table[0] = "natural_log_exp_and_others"
            act.wait_ge(cum_zero, 1)
            squares_of_x()
            seed(("x", 0), S)
            act.wait_ge(consts_in, 16 * 3)
            run(id_r[:], ident[:], ACT.Copy).then_inc(id_ready, 1)
            run(mask_r[:], mask_f[:], ACT.Copy).then_inc(id_ready, 1)
            run(avg_r[:], avg[:], ACT.Copy).then_inc(id_ready, 1)
            for k in range(KT):
                split_normed(k, S, logits, h_split, 0)
            for slot in range(last_slot + 1):
                c = slot // 4
                if slot % 4 == 0:
                    if c:
                        after_chunk(c - 1)
                    if c + AHEAD < len(CHUNKS):
                        split_hi(c + AHEAD)
                for st in STEPS.get(slot, ()):
                    what, j = st
                    if what == "row_turn":
                        row_square(0, j)
                        row_copy(0, j)
                    elif what == "norm":
                        if j == MK_NORMS[0]:
                            act.wait_ge(h_f, 2 * KT)
                        seed(st, norm_io(j)[2])
                    elif what == "mem_sq":
                        if j == 0:
                            act.wait_ge(stat_ready, sum_no["norm", RET_NORMS[-1]] + 1)
                            act.wait_ge(mem_in, 16)
                        elif j >= 2:
                            act.wait_ge(x_sum, KT + j - 1)
                        run(sq[:, j % 2, 0:M], memT[:, j, :], ACT.Square).then_inc(x_sq, 1)
                        act.wait_ge(x_sq, KT + j + 1)
                        square_hi(j % 2, M)
                    elif what == "mem_norm":
                        seed(st, M)
                    elif what == "mem_split":
                        act.wait_ge(w_used, FIRST["o_ret"] + KT)
                        split_normed(j, M, ret_raw, mem_split, KT)
                    elif what == "forget":
                        act.wait_ge(stat_ready, sum_no[st] + 1)
                        if j >= 2:
                            act.wait_ge(sc_read, TT * (j - 1))
                        else:
                            act.wait_ge(cum_ready, 1)
                        run(forget[:, j % 2, :], ps[:, STAT, :], ACT.Copy).then_inc(stat_read, 1)
                    elif what == "fox_score":
                        w = P * (j % TT + 1)
                        act.wait_ge(sc_read, j + 1)
                        if j >= 2:
                            act.wait_ge(turned, j - 1)
                        run(prob[:, j % 2, 0:w], logits[:, j % 2, 0:w], ACT.Exp, scale=-1.0,
                            bias=stat[:, j % 2:j % 2 + 1], accum_out=stat[:, 2 + j % 2:3 + j % 2]).then_inc(prob_ready, 1)
                    elif what == "fox_turn":
                        head, r = j // TT, j % TT
                        act.wait_ge(turned, j + 1)
                        if head >= 2:
                            act.wait_ge(pv_done, head - 1)
                        run(fox_pt[:, head % 2, 0:r + 1, r * P:(r + 1) * P],
                            ps[:, TURN + j % 2, 0:P * (r + 1)].rearrange("p (k i) -> p k i", i=P),
                            ACT.Copy).then_inc(turn_read, 1)
                    elif what == "fox_pv" and j % 2 == 1:
                        act.wait_ge(pv_done, j + 1)
                        run(o_split[:, 0, j // 2, :], ps[:, PV, :], ACT.Copy).then_inc(o_hi, 1)
                    elif what == "ret_pv":
                        act.wait_ge(pv_done, FOX_HEADS + j + 1)
                        e = j % 2
                        n = RET_NORMS[0] + j // 2
                        act.wait_ge(stat_ready, sum_no["norm", n - 1] + 1)
                        run(sq[:, e, :], ps[:, PV if e == 0 else TURN, :], ACT.Square).then_inc(ret_sq, 1)
                        act.wait_ge(ret_sq, j + 1)
                        square_hi(e, S)
                    elif what == "ret_out":
                        act.wait_ge(normed, normed_by["norm", RET_NORMS[j]])
                        if j == 0:
                            act.wait_ge(w_used, FIRST["o_fox"] + KT)
                        for e in range(HEAD_TILES):
                            run(o_split[:, 0, HEAD_TILES * j + e, :], ret_o[:, e, :], ACT.Copy).then_inc(o_hi, 1)
                    elif what == "mem_score":
                        n = soft["mem", j]
                        act.wait_ge(mem_min, j + 1)
                        if j >= 2:
                            act.wait_ge(turned, n - 1)
                        run(mem_p[:, n % 2, :], ps[:, SCORE + sc_no[st] % 2, 0:M], ACT.Exp, scale=-1.0,
                            bias=stat[:, n % 2:n % 2 + 1], accum_out=stat[:, 2 + n % 2:3 + n % 2]).then_inc(sc_read, 1)
                    elif what == "mem_turn":
                        n = soft["mem", j]
                        h, r = j // TT, j % TT
                        act.wait_ge(turned, n + 1)
                        if h:
                            act.wait_ge(pv_done, FOX_HEADS + 2 * RET_HEADS + 2 * h)
                        run(mem_pt[:, :, r * P:(r + 1) * P],
                            ps[:, TURN + n % 2, 0:M].rearrange("p (k i) -> p k i", i=P), ACT.Copy).then_inc(turn_read, 1)
                    elif what == "mem_pv":
                        act.wait_ge(pv_done, FOX_HEADS + 2 * RET_HEADS + j + 1)
                        if j == 0:
                            act.wait_ge(w_used, FIRST["mq"])
                        run(o_split[:, 0, j, :], ps[:, PV, :], ACT.Copy).then_inc(o_hi, 1)

            for tt in range(TT):
                row_square(1, tt)
                if tt:
                    row_copy(1, tt - 1)
            act.wait_ge(row_sum, 1)
            link(run(sums[:, 1, :], sums[:, 5, :], ACT.Ln, scale=1.0 / D, bias=eps))
            run(sums[:, 1, :], sums[:, 1, :], ACT.Exp, scale=-0.5).then_inc(row_seed, 1)
            row_copy(1, TT - 1)
            run(before_r, before, ACT.Copy).then_inc(tab_r, 1)
            run(ones_r, ones, ACT.Copy).then_inc(tab_r, 1)
            act.wait_ge(logit_ready, 1)
            run(r64[0], r64[7], ACT.Sigmoid).then_inc(score_ready, 1)
            act.wait_ge(row_rstd, 1)
            act.wait_ge(xg_turned, 2 * TT)
            for tt in range(TT):
                run(h2[:, tt, :], h2[:, tt, :], ACT.Copy, scale=sums[:, 1, tt:tt + 1]).then_inc(h2_ready, 1)

            def split_rows():
                for h in range(2):
                    ins = run(xe_split[:, 0, 4 * h:4 * h + 4, :], ps[:, 2 + h, :].rearrange("p (k s) -> p k s", k=4), ACT.Copy)
                ins.then_inc(xe_hi, 1)

            nc.scalar.preload_act_table_set("silu_and_others")
            act.wait_ge(y_filled, 16 * (MAX_BLOCKS - TOP_K * S // P))
            act.wait_ge(e_lo, FT)
            turns = act.value_load(blocks_i[0:1, IDX_COLS:IDX_COLS + 1], min_val=TOP_K * S // P - 1, max_val=MAX_BLOCKS - 1)
            n_blocks = turns + 1

            def expert_hi(at, k, landed_value):
                act.wait_ge(e_landed[k], landed_value)
                act.wait_ge(e_used, at + (k + 1 - E_SPLIT))
                run(ew_split[:, 0, k % E_SPLIT, :], e_raw[k], ACT.Copy).then_inc(e_hi, 1)

            def silu_gate(b, used):
                act.wait_ge(e_used, used)
                run(h_act, ps[:, 0, :], ACT.Silu).then_inc(silu_done, 1)

            def hidden_hi(b):
                act.wait_ge(he_turned, b + 1)
                run(he_split[:, 0, :, :], ps[:, 4, :].rearrange("p (f s) -> p f s", f=FT), ACT.Copy).then_inc(he_hi, 1)

            def store_y(b, used):
                act.wait_ge(e_used, used)
                act.wait_ge(y_stored, b * 16 + 16)
                run(y_rows[:, 0:512], ps[:, 5, :], ACT.Copy).then_inc(y_act, 1)
                act.wait_ge(y_act, b + 1)
                act.wait_ge(y_dve, b + 1)
                nc.scalar.dma_start(dram["y"][bass.ds(b * P, P), :], y_rows).then_inc(y_stored, 16)

            for k in range(FT, BLOCK_CHUNKS):
                if k == FT + E_SPLIT:
                    act.wait_ge(xe_turned, 1)
                    split_rows()
                expert_hi(0, k, landed_by(0, k))
            silu_gate(0, BLOCK_CHUNKS)
            act.wait_ge(xe_turned, 2)
            split_rows()
            with act.Fori(0, turns) as turn:
                b = turn + 1
                for k in range(BLOCK_CHUNKS):
                    if k == BLOCK_CHUNKS - 1:
                        silu_gate(b, b * BLOCK_CHUNKS + KT)
                    expert_hi(b * BLOCK_CHUNKS, k, landed_by(b, k))
                    if k == 3:
                        hidden_hi(b - 1)
                        store_y(b - 1, b * BLOCK_CHUNKS)
                act.wait_ge(xe_turned, b + 2)
                split_rows()
            for k in range(FT):
                if k == FT - 1:
                    hidden_hi(n_blocks - 1)
                    store_y(n_blocks - 1, n_blocks * BLOCK_CHUNKS)
                expert_hi(n_blocks * BLOCK_CHUNKS, k, landed_by(n_blocks, k))
            store_y(n_blocks, n_blocks * BLOCK_CHUNKS + FT)

        @block.vector
        def _(dve):
            links = [0]

            def link(ins):
                links[0] += 1
                ins.then_inc(dve_chain, 1)
                dve.wait_ge(dve_chain, links[0])

            def f(ap):
                return ap.bitcast(F32)

            def split_lo(c):
                dve.wait_ge(hi_ready, c + 1)
                nc.vector.tensor_tensor(w_split[:, 1, c % SPLIT, :], raw[:, c % RAW, :],
                                        f(w_split[:, 0, c % SPLIT, :]), ALU.subtract).then_inc(lo_ready, 1)

            squares = [0]

            def square_lo(e, width):
                squares[0] += 1
                dve.wait_ge(sq_hi, squares[0])
                nc.vector.tensor_tensor(sq_r[:, 1, e, 0:width], sq[:, e, 0:width], f(sq_r[:, 0, e, 0:width]),
                                        ALU.subtract).then_inc(sq_lo, 1)

            def norm_input(k, src, width, tmp, dst, g, before):
                for n in ([0, 1] if k == 0 else [k + 1] if k + 1 < KT else []):
                    if n >= 2:
                        dve.wait_ge(h_lo, before + n - 1)
                    nc.vector.scalar_tensor_tensor(tmp[:, n % 2, 0:width], src[:, n, :], gains[:, g + n:g + n + 1],
                                                   rstd[:, 0:width], ALU.mult, ALU.mult).then_inc(h_f, 1)
                dve.wait_ge(h_hi, before + k + 1)
                nc.vector.tensor_tensor(dst[:, 1, k, :], tmp[:, k % 2, 0:width], f(dst[:, 0, k, :]),
                                        ALU.subtract).then_inc(h_lo, 1)

            def after_chunk(c):
                kind, i = CHUNKS[c]
                if kind in NATURAL:
                    g, kp = i // 4, i % 4
                    if kp < 3:
                        return
                    if kind != "out":
                        dve.wait_ge(w_used, c + 1)
                    if kind == "mv":
                        if g == 0:
                            dve.wait_ge(h_lo, 2 * KT)
                        nc.vector.tensor_copy(mv[:, 1, g * 512:(g + 1) * 512], ps[:, SCORE + 2 * g + 1, :]).then_inc(nat_read, 1)
                    elif kind == "out":
                        dve.wait_ge(xn_in, 16)
                        dve.wait_ge(tab_in, 16 * 10)
                        dve.wait_ge(m_hi, KT)
                        for tt in range(TT):
                            cols = slice(g * 512, (g + 1) * 512)
                            if tt < TT - 1:
                                dve.wait_ge(out_tile, g * (TT - 1) + tt + 1)
                            else:
                                dve.wait_ge(w_used, c + 1)
                            nc.vector.tensor_tensor(x1[:, tt, cols], ps[:, 4 * g + tt, :], x_nat[:, tt, cols],
                                                    ALU.add).then_inc(x1_ready, 1)
                            dve.wait_ge(x1_ready, g * TT + tt + 1)
                            nc.vector.tensor_tensor(h2[:, tt, cols], x1[:, tt, cols], gain_b[:, cols],
                                                    ALU.mult).then_inc(xg_ready, 1)
                    else:
                        dst = fv if kind == "fv" else rv
                        for tt in (2, 3):
                            nc.vector.tensor_copy(dst[:, tt, g * 512:(g + 1) * 512], ps[:, 4 * g + tt, :]).then_inc(nat_read, 1)
                    return
                src = ps[:, tile_no[c] % 2, 0:M if kind == "mk" else S]
                if kind in ("fq", "fk", "mq", "mk"):
                    n, e = norm_of_chunk(kind, i)
                    dve.wait_ge(sq_ready, squares_by(n, e))
                    if n >= 2 and n in FOX_NORMS:
                        dve.wait_ge(normed, normed_by["norm", n - 2])
                    elif n not in FOX_NORMS:
                        dve.wait_ge(normed, normed_by["norm", n - 2])
                    dst = fox_raw[:, n % 2, :] if n in FOX_NORMS else mem_raw[:, n % 2, e, 0:M if kind == "mk" else S]
                    g = {"fq": G_FQ, "fk": G_FK, "mq": G_MQ + e, "mk": G_MK + e}[kind]
                    scale = {"fq": -FOX_DIM ** -0.5, "mq": -(2 * P) ** -0.5}.get(kind, 1.0)
                    nc.vector.tensor_scalar(dst, src, gains[:, g:g + 1], scale, ALU.mult, ALU.mult).then_inc(tile_dve, 1)
                    if n not in FOX_NORMS:
                        square_lo(e, M if kind == "mk" else S)
                elif kind == "ff":
                    z, e, lf = logits[0:FOX_HEADS, 0, :], prob[0:FOX_HEADS, 0, :], prob[0:FOX_HEADS, 1, :]
                    dve.wait_ge(gate_log, 1)
                    link(nc.vector.memset(forget[0:FOX_HEADS, 0, :], 1.0))
                    link(nc.vector.scalar_tensor_tensor(lf, z, 0.0, e, ALU.min, ALU.subtract))
                    cum = fox_k[0:FOX_HEADS, 0, :]
                    link(nc.vector.tensor_tensor_scan(cum, forget[0:FOX_HEADS, 0, :], lf, 0.0, ALU.mult, ALU.add))
                    link(nc.vector.tensor_copy(cum_r[:, 0, :], cum))
                    nc.vector.tensor_tensor(cum_r[:, 1, :], cum, f(cum_r[:, 0, :]), ALU.subtract).then_inc(cum_ready, 1)
                elif kind in ("o_fox", "o_ret", "o_mem"):
                    b = ("o_fox", "o_ret", "o_mem").index(kind)
                    dve.wait_ge(w_used, c + 1)
                    dve.wait_ge(tile_act, count_before(READ_BY_ACT, FIRST[kind]))
                    if b == 0:
                        nc.vector.tensor_tensor(merged[:, i, :], src, gate[:, i, :], ALU.mult).then_inc(tile_dve, 1)
                        return
                    nc.vector.tensor_tensor(gate[:, i, :], src, gate[:, i, :], ALU.mult).then_inc(tile_dve, 1)
                    dve.wait_ge(tile_dve, count_before(READ_BY_DVE, c + 1))
                    nc.vector.tensor_tensor(merged[:, i, :], merged[:, i, :], gate[:, i, :],
                                            ALU.add).then_inc(merge_done, 1)
                    if b == 2:
                        dve.wait_ge(m_hi, i + 1)
                        nc.vector.tensor_tensor(h_split[:, 1, i, :], merged[:, i, :], f(h_split[:, 0, i, :]),
                                                ALU.subtract).then_inc(m_lo, 1)

            def lo_part(t, src):
                dve.wait_ge(o_hi, t + 1)
                nc.vector.tensor_tensor(o_split[:, 1, t % KT, :], src, f(o_split[:, 0, t % KT, :]),
                                        ALU.subtract).then_inc(o_lo, 1)

            link(nc.vector.memset(cst[:, 0:1], EPS))
            nc.vector.memset(cst[:, 1:2], 1.0).then_inc(cum_zero, 1)
            for c in range(AHEAD):
                split_lo(c)
            dve.wait_ge(seed_ready, 1)
            v, r_, t_ = var[:, :], rstd[:, :], newton[:, :]
            link(nc.vector.tensor_tensor(t_, v, r_, ALU.mult))
            link(nc.vector.tensor_tensor(t_, t_, r_, ALU.mult))
            link(nc.vector.tensor_scalar(t_, t_, -0.5, 1.5, ALU.mult, ALU.add))
            nc.vector.tensor_tensor(r_, r_, t_, ALU.mult).then_inc(normed, 1)
            dve.wait_ge(normed, 1)
            dve.wait_ge(consts_in, 16 * 3)
            for k in range(KT):
                norm_input(k, xT, S, logits, h_split, G_MIX, 0)
            for slot in range(last_slot + 1):
                c = slot // 4
                if slot % 4 == 0:
                    if c:
                        after_chunk(c - 1)
                    if c + AHEAD < len(CHUNKS):
                        split_lo(c + AHEAD)
                for st in STEPS.get(slot, ()):
                    what, j = st
                    if what == "rotary":
                        h, is_q = j // 2, j % 2
                        dst = ret_q if is_q else ret_k
                        dve.wait_ge(tile_act, count_before(READ_BY_ACT, FIRST["rk"] + 6 * h + 2 * is_q + 2))
                        dve.wait_ge(rot_in, 32)
                        if h:
                            dve.wait_ge(sc_done, TT * (FOX_HEADS + h))
                        a, b = ret_raw[:, 0, :], ret_raw[:, 1, :]
                        nc.vector.tensor_tensor(dst[:, 1, :], b, cos, ALU.mult)
                        link(nc.vector.tensor_tensor(rot2[:], a, sin, ALU.mult))
                        nc.vector.tensor_tensor(dst[:, 1, :], dst[:, 1, :], rot2[:], ALU.add).then_inc(rotated_dve, 1)
                    elif what == "mem_sq":
                        square_lo(j % 2, M)
                    elif what == "mem_split":
                        dve.wait_ge(normed, normed_by["mem_norm", 0])
                        dve.wait_ge(o_lo, 2 * KT)
                        norm_input(j, memT, M, ret_raw, mem_split, G_MEM, KT)
                    elif what == "fox_score":
                        w = P * (j % TT + 1)
                        dve.wait_ge(sc_done, j + 1)
                        if j >= 2:
                            dve.wait_ge(prob_ready, j - 1)
                        dve.wait_ge(stat_read, stat_no["forget", j // TT] + 1)
                        nc.vector.tensor_tensor_reduce(logits[:, j % 2, 0:w], ps[:, SCORE + j % 2, 0:w],
                                                       forget[:, j // TT % 2, 0:w], 1.0, 3.0e38, ALU.add, ALU.min,
                                                       stat[:, j % 2:j % 2 + 1]).then_inc(sc_read, 1)
                    elif what in ("fox_scale", "mem_scale"):
                        n = soft[what[:3], j]
                        w = P * (j % TT + 1) if what[0] == "f" else M
                        buf = (prob if what[0] == "f" else mem_p)[:, n % 2, 0:w]
                        if what[0] == "f":
                            dve.wait_ge(prob_ready, j + 1)
                        else:
                            dve.wait_ge(sc_read, sc_no["mem_score", j] + 1)
                        link(nc.vector.reciprocal(stat[:, 4 + n % 2:5 + n % 2], stat[:, 2 + n % 2:3 + n % 2]))
                        nc.vector.tensor_scalar(buf, buf, stat[:, 4 + n % 2:5 + n % 2], None,
                                                ALU.mult).then_inc(prob_scaled, 1)
                    elif what == "fox_pv" and j % 2 == 1:
                        lo_part(j // 2, ps[:, PV, :])
                    elif what == "ret_score":
                        h, k = j // TT, j % TT
                        n = sc_no[st]
                        w = S - k * P
                        at = RET_AT[k]
                        dve.wait_ge(sc_done, n + 1)
                        dve.wait_ge(decay_in, 16 * (h + 1))
                        if h:
                            dve.wait_ge(pv_done, FOX_HEADS + HEAD_TILES * h)
                        nc.vector.tensor_tensor(ret_p[:, at:at + w], ps[:, SCORE + n % 2, 0:w], decay[:, 0:w],
                                                ALU.mult).then_inc(sc_read, 1)
                    elif what == "ret_pv":
                        h, e = j // 2, j % 2
                        dve.wait_ge(pv_done, FOX_HEADS + j + 1)
                        dve.wait_ge(ret_sq, j + 1)
                        dve.wait_ge(tile_act, count_before(READ_BY_ACT, FIRST["rk"] + 6 * h + 5 + e))
                        nc.vector.tensor_tensor(ret_o[:, e, :], ret_o[:, e, :], ps[:, PV if e == 0 else TURN, :],
                                                ALU.mult).then_inc(ret_gated, 1)
                        square_lo(e, S)
                    elif what == "ret_out":
                        dve.wait_ge(normed, normed_by["norm", RET_NORMS[j]])
                        for e in range(HEAD_TILES):
                            lo_part(KT + HEAD_TILES * j + e, ret_o[:, e, :])
                    elif what == "mem_score":
                        n = soft["mem", j]
                        dve.wait_ge(sc_done, sc_no[st] + 1)
                        if j >= 2:
                            dve.wait_ge(sc_read, sc_no[st] - 1)
                        nc.vector.tensor_reduce(stat[:, n % 2:n % 2 + 1], ps[:, SCORE + sc_no[st] % 2, 0:M], AX.X,
                                                ALU.min).then_inc(mem_min, 1)
                    elif what == "mem_pv":
                        lo_part(2 * KT + j, ps[:, PV, :])

            V = nc.vector
            V.tensor_scalar(sel_wide[:, 0:TT * N_EXPERTS], lanes[:, 0:TT * N_EXPERTS], 0.0, None, ALU.mult)
            V.tensor_scalar(sel_wide[:, 2 * TT * N_EXPERTS:], lanes[:, 0:N_EXPERTS], 0.0, None, ALU.mult)
            ms, r, t = sums[:, 2, :], sums[:, 1, :], sums[:, 3, :]
            dve.wait_ge(row_sq, 2 * TT)
            V.tensor_tensor(sums[:, 5, :], sums[:, 0, :], sums[:, 4, :], ALU.add).then_inc(row_sum, 1)
            dve.wait_ge(row_sum, 1)
            link(V.tensor_scalar(ms, sums[:, 5, :], 1.0 / D, EPS, ALU.mult, ALU.add))
            dve.wait_ge(row_seed, 1)
            link(V.tensor_tensor(t, ms, r, ALU.mult))
            link(V.tensor_tensor(t, t, r, ALU.mult))
            link(V.tensor_scalar(t, t, -0.5, 1.5, ALU.mult, ALU.add))
            V.tensor_tensor(r, r, t, ALU.mult).then_inc(row_rstd, 1)
            dve.wait_ge(row_rstd, 1)
            dve.wait_ge(logit_done, 2 * TT)
            link(V.tensor_copy(r64[8], ps[:, 3, 0:TT * N_EXPERTS]))
            link(V.tensor_tensor(r64[7], r64[8], ps[:, 3, TT * N_EXPERTS:2 * TT * N_EXPERTS], ALU.add))
            V.tensor_tensor(r64[7].rearrange("p (t e) -> p t e", t=TT), r64[7].rearrange("p (t e) -> p t e", t=TT),
                            r.unsqueeze(2).to_broadcast([P, TT, N_EXPERTS]), ALU.mult).then_inc(logit_ready, 1)

            score, biased, sel, w, pos = r64[0:5]
            t64a, t64b = r64[5], r64[6]

            def experts_of(ap):
                return ap.rearrange("p (q e) -> p q e", e=PER_GROUP)

            def ranks(v, n, out):
                a4 = v.unsqueeze(2).to_broadcast([P, n, 4, 4])
                b4 = v.unsqueeze(3).to_broadcast([P, n, 4, 4])
                g4 = r256a[:, 0:n * 16].rearrange("p (q b a) -> p q b a", b=4, a=4)
                e4 = r256b[:, 0:n * 16].rearrange("p (q b a) -> p q b a", b=4, a=4)
                V.tensor_tensor(g4, a4, b4, ALU.is_gt)
                link(V.tensor_tensor(e4, a4, b4, ALU.is_equal))
                link(V.tensor_tensor(e4, e4, order4.unsqueeze(1).to_broadcast([P, n, 4, 4]), ALU.mult))
                link(V.tensor_tensor(g4, g4, e4, ALU.add))
                link(V.tensor_reduce(out, g4, AX.X, ALU.add))

            dve.wait_ge(score_ready, 1)
            link(V.tensor_tensor(biased, score, bias_b, ALU.add))
            pair = biased.rearrange("p (q c d) -> p q c d", c=2, d=2)
            hi2 = t64a[:, 0:32].rearrange("p (q c) -> p q c", c=2)
            lo2 = t64a[:, 32:64].rearrange("p (q c) -> p q c", c=2)
            V.tensor_tensor(hi2, pair[:, :, :, 0], pair[:, :, :, 1], ALU.max)
            link(V.tensor_tensor(lo2, pair[:, :, :, 0], pair[:, :, :, 1], ALU.min))
            V.tensor_tensor(r16[0], hi2[:, :, 0], hi2[:, :, 1], ALU.max)
            V.tensor_tensor(r16[1], hi2[:, :, 0], hi2[:, :, 1], ALU.min)
            link(V.tensor_tensor(r16[2], lo2[:, :, 0], lo2[:, :, 1], ALU.max))
            link(V.tensor_tensor(r16[1], r16[1], r16[2], ALU.max))
            link(V.tensor_tensor(r16[3], r16[0], r16[1], ALU.add))
            ranks(r16[3].rearrange("p (t g) -> p t g", g=N_GROUPS), TT, r16[4].rearrange("p (t g) -> p t g", g=N_GROUPS))
            link(V.tensor_scalar(r16[4], r16[4], 1.0, None, ALU.is_lt))
            ranks(experts_of(biased), TT * N_GROUPS, experts_of(t64b))
            link(V.tensor_scalar(t64b, t64b, float(TOP_K), None, ALU.is_lt))
            link(V.tensor_tensor(experts_of(sel), experts_of(t64b),
                                 r16[4].unsqueeze(2).to_broadcast([P, TT * N_GROUPS, PER_GROUP]), ALU.mult))
            V.tensor_copy(sel_r, sel).then_inc(sel_ready, 1)
            link(V.tensor_tensor(w, score, sel, ALU.mult))
            by_token = (lambda ap: ap.rearrange("p (t e) -> p t e", e=N_EXPERTS))
            denom = r16[5][:, 0:TT]
            link(V.tensor_reduce(denom, by_token(w), AX.X, ALU.add))
            link(V.reciprocal(denom, denom))
            dve.wait_ge(pos_done, 1)
            count, blocks, ends, starts = r16[6], r16[7], r16[8], r16[9]
            link(V.tensor_copy(count, ps[:, 5, TT * N_EXPERTS:(TT + 1) * N_EXPERTS]))
            link(V.tensor_scalar(blocks, count, 0.5, None, ALU.is_gt))
            for n in range(1, TT):
                link(V.scalar_tensor_tensor(blocks, count, n * P + 0.5, blocks, ALU.is_gt, ALU.add))
            link(V.tensor_scalar(blocks[:, 0:1], blocks[:, 0:1], 1.0, None, ALU.max))
            link(V.tensor_tensor_scan(ends, ones[:, 0:N_EXPERTS], blocks, 0.0, ALU.mult, ALU.add))
            link(V.tensor_tensor(starts, ends, blocks, ALU.subtract))
            link(V.scalar_tensor_tensor(by_token(pos), starts.unsqueeze(1).to_broadcast([P, TT, N_EXPERTS]), float(P),
                                        by_token(ps[:, 5, 0:TT * N_EXPERTS]), ALU.mult, ALU.add))
            far = float(IDX_COLS * P)
            link(V.tensor_scalar(t64a, sel, -far, far, ALU.mult, ALU.add))
            link(V.tensor_tensor(t64a, t64a, pos, ALU.add))
            slots = r16[10][:, 0:2 * TT]
            first, second = slots[:, 0:TT], slots[:, TT:]
            link(V.tensor_reduce(first, by_token(t64a), AX.X, ALU.min))
            link(V.scalar_tensor_tensor(t64b, pos, 1.0, sel, ALU.add, ALU.mult))
            link(V.tensor_reduce(second, by_token(t64b), AX.X, ALU.max))
            link(V.tensor_scalar(second, second, -1.0, None, ALU.add))
            by_block = (lambda ap: ap[:, 0:2 * TT * IDX_COLS].rearrange("p (j b) -> p j b", b=IDX_COLS))
            lane_in, in_block, start_in = by_block(r256a), by_block(r384), by_block(r256b)
            link(V.tensor_tensor(lane_in, slots.unsqueeze(2).to_broadcast([P, 2 * TT, IDX_COLS]),
                                 block_at.unsqueeze(1).to_broadcast([P, 2 * TT, IDX_COLS]), ALU.subtract))
            link(V.tensor_scalar(start_in, lane_in, 0.0, None, ALU.is_ge))
            link(V.scalar_tensor_tensor(in_block, lane_in, float(P), start_in, ALU.is_lt, ALU.mult))
            link(V.tensor_tensor(lane_in, lane_in, in_block, ALU.mult))
            lane = r16[11][:, 0:2 * TT]
            link(V.tensor_reduce(lane, lane_in, AX.X, ALU.add))
            link(V.tensor_tensor(block_ids, in_block, token_f.unsqueeze(2).to_broadcast([P, 2 * TT, IDX_COLS]), ALU.mult))
            for j in range(2 * TT):
                V.tensor_scalar(lane_hot[:, j, :], lanes, lane[:, j:j + 1], None, ALU.is_equal).then_inc(hot_ready, 1)
            be = r384.rearrange("p (b e) -> p b e", e=N_EXPERTS)
            link(V.tensor_tensor(be, iota.unsqueeze(2).to_broadcast([P, IDX_COLS, N_EXPERTS]),
                                 ends.unsqueeze(1).to_broadcast([P, IDX_COLS, N_EXPERTS]), ALU.is_ge))
            link(V.tensor_reduce(r256a[:, 0:IDX_COLS], be, AX.X, ALU.add))
            link(V.tensor_scalar(r256a[:, 0:IDX_COLS], r256a[:, 0:IDX_COLS], float(N_EXPERTS - 1), None, ALU.min))
            link(V.tensor_copy(blocks_i[:, 0:IDX_COLS], r256a[:, 0:IDX_COLS]))
            link(V.tensor_scalar(blocks_i[:, IDX_COLS:IDX_COLS + 1], ends[:, N_EXPERTS - 1:N_EXPERTS], -1.0, None, ALU.add))
            dve.wait_ge(rows_done, 1)
            V.tensor_copy(row_i[:], ps[:, 4, 0:1]).then_inc(row_copied, 1)
            V.tensor_copy(rows_i[:], ps[:, 4, 0:IDX_COLS]).then_inc(rows_ready, 1)
            dve.wait_ge(w_used, len(CHUNKS))
            V.memset(stat[:, 3:4], 0.0).then_inc(e_hi, FT)
            V.memset(stat[:, 0:1], 0.0).then_inc(e_lo, FT)
            V.memset(stat[:, 1:2], 0.0).then_inc(e_used, FT)
            V.memset(stat[:, 2:3], 0.0).then_inc(y_stored, 16)
            for a, slot_ in ((0, first), (1, second)):
                link(V.tensor_tensor(by_token(t64a), by_token(pos), slot_.unsqueeze(2).to_broadcast([P, TT, N_EXPERTS]),
                                     ALU.is_equal))
                link(V.tensor_tensor(t64a, t64a, w, ALU.mult))
                link(V.tensor_reduce(token_w[:, a, :], by_token(t64a), AX.X, ALU.add))
                link(V.tensor_tensor(token_w[:, a, :], token_w[:, a, :], denom, ALU.mult))
                V.tensor_scalar(y_slot_i[:, a, :], slot_, float(P), None, ALU.add).then_inc(table_ready, 1)

            def rows_lo():
                for h in range(2):
                    ins = V.tensor_tensor(xe_split[:, 1, 4 * h:4 * h + 4, :], ps[:, 2 + h, :].rearrange("p (k s) -> p k s", k=4),
                                          f(xe_split[:, 0, 4 * h:4 * h + 4, :]), ALU.subtract)
                ins.then_inc(xe_lo, 1)

            turns = dve.value_load(blocks_i[0:1, IDX_COLS:IDX_COLS + 1], min_val=TOP_K * S // P - 1, max_val=MAX_BLOCKS - 1)
            n_blocks = turns + 1

            def expert_lo(at, k):
                dve.wait_ge(e_hi, at + (k + 1))
                V.tensor_tensor(ew_split[:, 1, k % E_SPLIT, :], e_raw[k], f(ew_split[:, 0, k % E_SPLIT, :]),
                                ALU.subtract).then_inc(e_lo, 1)

            def hidden(b):
                dve.wait_ge(silu_done, b + 1)
                V.tensor_tensor(h_e, h_act, ps[:, 1, :], ALU.mult).then_inc(he_ready, 1)

            def hidden_lo(b):
                dve.wait_ge(he_hi, b + 1)
                V.tensor_tensor(he_split[:, 1, :, :], ps[:, 4, :].rearrange("p (f s) -> p f s", f=FT),
                                f(he_split[:, 0, :, :]), ALU.subtract).then_inc(he_lo, 1)

            def leave_y(b, used):
                dve.wait_ge(e_used, used)
                dve.wait_ge(y_stored, b * 16 + 16)
                V.tensor_copy(y_rows[:, 512:], ps[:, 6, :]).then_inc(y_dve, 1)

            for k in range(FT, BLOCK_CHUNKS):
                if k == FT + E_SPLIT:
                    dve.wait_ge(xe_hi, 1)
                    rows_lo()
                expert_lo(0, k)
            hidden(0)
            dve.wait_ge(xe_hi, 2)
            rows_lo()
            with dve.Fori(0, turns) as turn:
                b = turn + 1
                for k in range(BLOCK_CHUNKS):
                    if k == BLOCK_CHUNKS - 1:
                        hidden(b)
                    expert_lo(b * BLOCK_CHUNKS, k)
                    if k == 3:
                        hidden_lo(b - 1)
                        leave_y(b - 1, b * BLOCK_CHUNKS)
                dve.wait_ge(xe_hi, b + 2)
                rows_lo()
            for k in range(FT):
                if k == FT - 1:
                    hidden_lo(n_blocks - 1)
                    leave_y(n_blocks - 1, n_blocks * BLOCK_CHUNKS)
                expert_lo(n_blocks * BLOCK_CHUNKS, k)
            leave_y(n_blocks, n_blocks * BLOCK_CHUNKS + FT)

            for a, (rows, landed_) in enumerate(((y_a, ya_in), (y_b, yb_in))):
                for tt in range(TT):
                    dve.wait_ge(landed_[tt], 16)
                    if a:
                        dve.wait_ge(token_out, tt + 1)
                    V.scalar_tensor_tensor(x1[:, tt, :], rows[:, tt, :], token_w[:, a, tt:tt + 1], x1[:, tt, :],
                                           ALU.mult, ALU.add).then_inc(token_out if a == 0 else mixed, 1)

        @block.gpsimd
        def _(pool):
            links = [0]

            def link(ins):
                links[0] += 1
                ins.then_inc(pool_chain, 1)
                pool.wait_ge(pool_chain, links[0])

            tt_ = nc.gpsimd.tensor_tensor

            def refine(st, width):
                pool.wait_ge(seed_ready, norm_no[st] + 1)
                v, r, t = var[:, 0:width], rstd[:, 0:width], newton[:, 0:width]
                link(tt_(t, v, r, ALU.mult))
                link(tt_(t, t, r, ALU.mult))
                link(nc.gpsimd.tensor_scalar(t, t, -0.5, 1.5, ALU.mult, ALU.add))
                if st[0] != "norm":
                    tt_(r, r, t, ALU.mult).then_inc(normed, 1)
                    return
                link(tt_(r, r, t, ALU.mult))
                n = st[1]
                src, dst, _ = norm_io(n)
                if n in RET_NORMS:
                    pool.wait_ge(ret_gated, HEAD_TILES * (n - RET_NORMS[0] + 1))
                else:
                    pool.wait_ge(tile_dve, count_before(READ_BY_DVE, chunk_of_norm(n) + 1))
                if n in FOX_NORMS and n >= 4:
                    pool.wait_ge(sc_done, 8 * (n // 2 - 1))
                if n == MK_NORMS[0]:
                    pool.wait_ge(pv_done, FOX_HEADS + RET_HEADS * HEAD_TILES)
                if n in MQ_NORMS and n >= MQ_NORMS[2]:
                    pool.wait_ge(sc_done, TT * (FOX_HEADS + RET_HEADS + n - MQ_NORMS[1]))
                for a, b in zip(src, dst):
                    tt_(b, a, r, ALU.mult).then_inc(normed, 1)

            for slot in range(last_slot):
                for st in STEPS.get(slot, ()):
                    what, j = st
                    if what == "norm":
                        refine(st, norm_io(j)[2])
                    elif what == "mem_norm":
                        refine(st, M)
                    elif what == "rotary":
                        h, is_q = j // 2, j % 2
                        dst = ret_q if is_q else ret_k
                        pool.wait_ge(tile_act, count_before(READ_BY_ACT, FIRST["rk"] + 6 * h + 2 * is_q + 2))
                        if j == 0:
                            pool.wait_ge(tile_dve, fox_merged)
                            nc.gpsimd.dma_start(cos, dram["cos"]).then_inc(rot_in, 16)
                            nc.gpsimd.dma_start(sin, dram["sin"]).then_inc(rot_in, 16)
                        if not is_q:
                            if h:
                                pool.wait_ge(sc_read, TT * (FOX_HEADS + h))
                            nc.gpsimd.dma_start(decay, dram["decay"][h]).then_inc(decay_in, 16)
                        pool.wait_ge(rot_in, 32)
                        if h:
                            pool.wait_ge(sc_done, TT * (FOX_HEADS + h))
                        a, b = ret_raw[:, 0, :], ret_raw[:, 1, :]
                        tt_(dst[:, 0, :], a, cos, ALU.mult)
                        link(tt_(rot, b, sin, ALU.mult))
                        tt_(dst[:, 0, :], dst[:, 0, :], rot, ALU.subtract).then_inc(rotated, 1)

            row = bass.IndirectOffsetOnAxis
            pool.wait_ge(h2_stored, 16 * TT)

            def gather_rows():
                nc.gpsimd.indirect_dma_start(x_rows, None, dram["h2"], row(row_i[:, 0:1], 0)).then_inc(x_landed, 16)

            pool.wait_ge(row_copied, 1)
            gather_rows()
            pool.wait_ge(rows_ready, 1)
            pool.wait_ge(e_lo, FT)
            turns = pool.value_load(blocks_i[0:1, IDX_COLS:IDX_COLS + 1], min_val=TOP_K * S // P - 1, max_val=MAX_BLOCKS - 1)
            n_blocks = turns + 1
            with pool.Fori(0, n_blocks) as b:
                pool.wait_ge(xe_turned, b + 1)
                nc.gpsimd.tensor_copy(row_i[:, :], rows_i[:, bass.ds(b + 1, 1)]).then_inc(row_copied, 1)
                pool.wait_ge(row_copied, b + 2)
                pool.sem_inc(gathers, 1)
                gather_rows()
            for a, (rows, landed_, stores) in enumerate(((y_a, ya_in, n_blocks * 16 + 16), (y_b, yb_in, n_blocks * 16 + 32))):
                pool.wait_ge(y_stored, stores)
                pool.sem_inc(gathers, 1)
                for tt in range(TT):
                    nc.gpsimd.indirect_dma_start(rows[:, tt, :], None, dram["y"],
                                                 row(y_slot_i[:, a, tt:tt + 1], 0)).then_inc(landed_[tt], 16)


def columns_of(w, kind, i):
    if kind in NATURAL:
        g, kp = i // 4, i % 4
        return w[2 * P * kp:2 * P * (kp + 1), 512 * g:512 * (g + 1)].reshape(2, P, 512).transpose(1, 0, 2).reshape(P, 1024)
    return w[:, P * i:P * (i + 1)].reshape(KT, P, P).transpose(1, 0, 2).reshape(P, 1024)


def tables():
    inv_freq = (np.float32(10000.0) ** (-np.arange(0, 2 * P, 2, dtype=np.float32) / np.float32(2 * P))).astype(np.float32)
    ang = (np.arange(S, dtype=np.float32)[None, :] * inv_freq[:, None]).astype(np.float32)
    j = np.arange(P)[:, None]
    i = np.arange(S)[None, :]
    decay = []
    for h in range(RET_HEADS):
        lg = np.log1p(-(2.0 ** (-5.0 - h)))
        decay.append(np.where(i >= j, np.exp(lg * np.maximum(i - j, 0)), 0.0) * (2 * P) ** -0.5)
    blocks = (np.arange(P)[:, None] // FOX_DIM == np.arange(P)[None, :] // FOX_DIM) / FOX_DIM
    avg = np.stack([blocks, np.full((P, P), 1.0 / (2 * P)), np.full((P, P), 1.0 / D)], 1)
    mask = np.where(np.arange(P)[None, :] > np.arange(P)[:, None], -NEG, 0.0)
    return {
        "cos": np.cos(ang), "sin": np.sin(ang), "decay": np.stack(decay), "avg": avg,
        "mask": mask, "ident": np.eye(P),
        "order4": np.broadcast_to(np.arange(4)[None, None, :] < np.arange(4)[None, :, None], (P, 4, 4)),
        "iota": np.broadcast_to(np.arange(IDX_COLS), (P, IDX_COLS)),
        "before": np.arange(P)[:, None] < np.arange(P)[None, :], "ones": np.ones((P, P)),
        "lanes": np.broadcast_to(np.arange(P), (P, P)), "block_at": np.broadcast_to(P * np.arange(IDX_COLS), (P, IDX_COLS)),
        "tokens": np.tile(np.arange(TT)[None, :] * P + np.arange(P)[:, None], (1, 2)),
    }


def kernel(**inputs):
    import concourse.bacc as bacc
    from concourse.bass_utils import run_bass_kernel_spmd

    a = {k: np.asarray(v) for k, v in inputs.items()}
    f32 = np.float32
    x, mem = a["x"][0], a["mem"][0]
    w_in = a["w_in"][0]
    names = ("rq", "rk", "rv", "rg", "fq", "fk", "fv", "ff", "mq", "g_ret", "g_fox", "g_mem")
    sizes = [D] * 7 + [FOX_HEADS] + [D] * 4
    at = np.concatenate([[0], np.cumsum(sizes)])
    w = {n: w_in[:, at[i]:at[i + 1]] for i, n in enumerate(names)}
    w["ff"] = np.concatenate([w["ff"], np.zeros((D, P - FOX_HEADS), f32)], 1)
    w["mk"], w["mv"] = a["w_mem_kv"][0][:, :D], a["w_mem_kv"][0][:, D:]
    w["o_ret"], w["o_fox"], w["o_mem"], w["out"] = (a[n][0] for n in ("w_o_ret", "w_o_fox", "w_o_mem", "w_out"))
    stream = np.empty((len(CHUNKS), P, 1024), f32)
    for c, (kind, i) in enumerate(CHUNKS):
        stream[c] = columns_of(w[kind], kind, i)

    def by_tile(v):
        return v.reshape(-1, P).T

    b_ff = np.zeros((P, 1), f32)
    b_ff[:FOX_HEADS, 0] = a["b_forget"][0]
    gains = np.concatenate([
        by_tile(a["norm_mix"][0]), by_tile(a["norm_mem"][0]),
        by_tile(np.concatenate([a["fox_q_norm"][0]] * 2)), by_tile(np.concatenate([a["fox_k_norm"][0]] * 2)),
        by_tile(a["mem_q_norm"][0]), by_tile(a["mem_k_norm"][0]), b_ff], 1)
    arrays = {
        "x": x, "xT": x.T.reshape(KT, P, S).transpose(1, 0, 2), "memT": mem.T.reshape(KT, P, M).transpose(1, 0, 2),
        "w": stream, "gains": gains,
    }
    arrays |= {k: v.astype(f32) for k, v in tables().items()}
    experts = np.empty((N_EXPERTS, BLOCK_CHUNKS, P, 1024), f32)
    experts[:, :KT, :, :FF] = a["w_gate"][0].reshape(N_EXPERTS, KT, P, FF)
    experts[:, :KT, :, FF:] = a["w_up"][0].reshape(N_EXPERTS, KT, P, FF)
    experts[:, KT:] = a["w_down"][0].reshape(N_EXPERTS, FT, P, D)
    arrays |= {
        "experts": experts, "router": a["router_w"].reshape(KT, P, N_EXPERTS).transpose(1, 0, 2),
        "bias_b": np.tile(a["router_bias"], (P, TT)), "gain_b": np.tile(a["norm_ffn"][0], (P, 1)),
    }
    nc = bacc.Bacc("TRN2", target_bir_lowering=False, num_devices=1)
    sent, dram = {}, {}
    for name, v in arrays.items():
        v = np.ascontiguousarray(v)
        sent[f"in_{name}"] = v
        dram[name] = nc.dram_tensor(f"in_{name}", v.shape, mybir.dt.from_np(v.dtype), kind="ExternalInput").ap()
    dram["out"] = nc.dram_tensor("out_x", (S, D), F32, kind="ExternalOutput").ap()
    dram["h2"] = nc.dram_tensor("h2", (S, D), F32, kind="Internal").ap()
    dram["y"] = nc.dram_tensor("y", ((MAX_BLOCKS + 1) * P, D), F32, kind="Internal").ap()
    mixing_and_experts(nc, dram)
    r = run_bass_kernel_spmd(nc, [sent], core_ids=[0])
    return r.results[0]["out_x"].reshape(1, S, D)
```
